# Optimizing a Trainium2 kernel written in Bass

```python
import jax, jax.numpy as jnp
from jax import lax
import numpy as np
import math

D_MODEL = 1024
BATCH = 1
SEQ = 256
DEPTH = 2

CHUNK = 64
MEM_LEN = 256
HEAD_GROUP = 64
A_WIDTH = 384
B_WIDTH = 320
C_WIDTH = 320
MIX_WIDTH = A_WIDTH + B_WIDTH + C_WIDTH
N_MIX_GROUPS = MIX_WIDTH // HEAD_GROUP
C_GROUPS = C_WIDTH // HEAD_GROUP
A_KERNEL = 31
B_KERNEL = 3
GMLP_BLOCK = 128
PROJ_WIDTH = 2 * A_WIDTH + 3 * B_WIDTH + 2 * C_WIDTH
X_HEADS = 4
X_HEAD_DIM = D_MODEL // X_HEADS
D_FF = 2816
N_EXPERTS = 8
TOP_K = 2
D_EXPERT = 3584
N_DENSE = (DEPTH + 1) // 2
N_MOE = DEPTH // 2
EPS = 1e-6


def rmsnorm(x, g):
    xf = x.astype(jnp.float32)
    y = xf * lax.rsqrt(jnp.mean(xf * xf, axis=-1, keepdims=True) + EPS)
    return (y * g.astype(jnp.float32)).astype(x.dtype)

def layernorm(x, g, b):
    xf = x.astype(jnp.float32)
    mu = jnp.mean(xf, axis=-1, keepdims=True)
    xc = xf - mu
    var = jnp.mean(xc * xc, axis=-1, keepdims=True)
    y = xc * lax.rsqrt(var + EPS) * g.astype(jnp.float32) + b.astype(jnp.float32)
    return y.astype(x.dtype)

def causal_depthwise_conv(x, w):
    k, c = w.shape
    return lax.conv_general_dilated(
        x, w[:, None, :], window_strides=(1,), padding=[(k - 1, 0)],
        dimension_numbers=("NWC", "WIO", "NWC"), feature_group_count=c)

def chunk_spatial_gate(u, v, ws, bias):
    bsz, s, c = v.shape
    n_blocks = s // GMLP_BLOCK
    chunk_id = jnp.arange(GMLP_BLOCK) // CHUNK
    mask = chunk_id[:, None] >= chunk_id[None, :]
    ws = jnp.where(mask[None], ws, jnp.zeros((), ws.dtype))
    vb = v.reshape(bsz, n_blocks, GMLP_BLOCK, C_GROUPS, HEAD_GROUP)
    mixed = jnp.einsum("gij,bnjgc->bnigc", ws, vb) + bias.T[None, None, :, :, None]
    return u * mixed.reshape(bsz, s, c)

def hybrid_mixer(xn, w_in, conv_a_w, conv_a_b, ln_a_g, ln_a_b, conv_b_w,
                 ln_c_g, ln_c_b, gmlp_ws, gmlp_b, mix_out_g, w_mix_out):
    z = xn @ w_in
    splits = [A_WIDTH, 2 * A_WIDTH, 2 * A_WIDTH + B_WIDTH,
              2 * A_WIDTH + 2 * B_WIDTH, 2 * A_WIDTH + 3 * B_WIDTH]
    a_val, a_gate, b_gate, c_gate, b_in, c_z = jnp.split(z, splits, axis=-1)
    ya = a_val * jax.nn.sigmoid(a_gate)
    ya = causal_depthwise_conv(ya, conv_a_w) + conv_a_b
    ya = jax.nn.silu(layernorm(ya, ln_a_g, ln_a_b))
    yb = b_gate * causal_depthwise_conv(c_gate * b_in, conv_b_w)
    c_z = jax.nn.gelu(c_z)
    c_u, c_v = jnp.split(c_z, 2, axis=-1)
    c_v = layernorm(c_v, ln_c_g, ln_c_b)
    yc = chunk_spatial_gate(c_u, c_v, gmlp_ws, gmlp_b)
    y = jnp.concatenate([ya, yb, yc], axis=-1)
    bsz, s, _ = y.shape
    y = rmsnorm(y.reshape(bsz, s, N_MIX_GROUPS, HEAD_GROUP),
                mix_out_g.reshape(N_MIX_GROUPS, HEAD_GROUP)).reshape(bsz, s, MIX_WIDTH)
    return y @ w_mix_out

def memory_cross_attention(xn, memn, w_xq, w_xkv, w_xo):
    bsz, s, _ = xn.shape
    m = memn.shape[1]
    q = (xn @ w_xq).reshape(bsz, s, X_HEADS, X_HEAD_DIM)
    k, v = jnp.split(memn @ w_xkv, 2, axis=-1)
    k = k.reshape(bsz, m, X_HEADS, X_HEAD_DIM)
    v = v.reshape(bsz, m, X_HEADS, X_HEAD_DIM)
    scores = jnp.einsum("bshd,bmhd->bhsm", q, k).astype(jnp.float32) * (X_HEAD_DIM ** -0.5)
    p = jax.nn.softmax(scores, axis=-1).astype(v.dtype)
    o = jnp.einsum("bhsm,bmhd->bshd", p, v).reshape(bsz, s, D_MODEL)
    return o @ w_xo

def swiglu(x, w_gate, w_up, w_down):
    return (jax.nn.silu(x @ w_gate) * (x @ w_up)) @ w_down

def moe_swiglu(xn, w_router, w_gate, w_up, w_down):
    bsz, s, d = xn.shape
    xt = xn.reshape(-1, d)
    logits = (xt @ w_router).astype(jnp.float32)
    top_vals, top_idx = lax.top_k(logits, TOP_K)
    top_w = jax.nn.softmax(top_vals, axis=-1)
    combine = jnp.sum(jax.nn.one_hot(top_idx, N_EXPERTS, dtype=jnp.float32) * top_w[..., None], axis=1)
    combine = combine.astype(xn.dtype)
    y = jnp.zeros_like(xt)
    for e in range(N_EXPERTS):
        y = y + combine[:, e:e + 1] * swiglu(xt, w_gate[e], w_up[e], w_down[e])
    return y.reshape(bsz, s, d)

def first_inputs(seed: int = 0) -> dict:
    key = jax.random.key(seed)
    ks = jax.random.split(key, 32)
    f32 = jnp.float32

    def nrm(k, shape, scale):
        return jax.random.normal(k, shape, f32) * scale

    def gain(k, shape):
        return 1.0 + 0.02 * jax.random.normal(k, shape, f32)

    return {
        "x": nrm(ks[0], (BATCH, SEQ, D_MODEL), 1.0),
        "mem": nrm(ks[1], (BATCH, MEM_LEN, D_MODEL), 1.0),
        "norm_mix_g": gain(ks[2], (DEPTH, D_MODEL)),
        "w_in": nrm(ks[3], (DEPTH, D_MODEL, PROJ_WIDTH), D_MODEL ** -0.5),
        "conv_a_w": nrm(ks[4], (DEPTH, A_KERNEL, A_WIDTH), A_KERNEL ** -0.5),
        "conv_a_b": nrm(ks[5], (DEPTH, A_WIDTH), 0.02),
        "ln_a_g": gain(ks[6], (DEPTH, A_WIDTH)),
        "ln_a_b": nrm(ks[7], (DEPTH, A_WIDTH), 0.02),
        "conv_b_w": nrm(ks[8], (DEPTH, B_KERNEL, B_WIDTH), B_KERNEL ** -0.5),
        "ln_c_g": gain(ks[9], (DEPTH, C_WIDTH)),
        "ln_c_b": nrm(ks[10], (DEPTH, C_WIDTH), 0.02),
        "gmlp_ws": nrm(ks[11], (DEPTH, C_GROUPS, GMLP_BLOCK, GMLP_BLOCK), GMLP_BLOCK ** -0.5),
        "gmlp_b": 1.0 + nrm(ks[12], (DEPTH, C_GROUPS, GMLP_BLOCK), 0.1),
        "mix_out_g": gain(ks[13], (DEPTH, MIX_WIDTH)),
        "w_mix_out": nrm(ks[14], (DEPTH, MIX_WIDTH, D_MODEL), MIX_WIDTH ** -0.5),
        "norm_x_g": gain(ks[15], (DEPTH, D_MODEL)),
        "norm_mem_g": gain(ks[16], (DEPTH, D_MODEL)),
        "w_xq": nrm(ks[17], (DEPTH, D_MODEL, D_MODEL), D_MODEL ** -0.5),
        "w_xkv": nrm(ks[18], (DEPTH, D_MODEL, 2 * D_MODEL), D_MODEL ** -0.5),
        "w_xo": nrm(ks[19], (DEPTH, D_MODEL, D_MODEL), D_MODEL ** -0.5),
        "norm_ffn_g": gain(ks[20], (DEPTH, D_MODEL)),
        "ffn_w_gate": nrm(ks[21], (N_DENSE, D_MODEL, D_FF), D_MODEL ** -0.5),
        "ffn_w_up": nrm(ks[22], (N_DENSE, D_MODEL, D_FF), D_MODEL ** -0.5),
        "ffn_w_down": nrm(ks[23], (N_DENSE, D_FF, D_MODEL), D_FF ** -0.5),
        "moe_router": nrm(ks[24], (N_MOE, D_MODEL, N_EXPERTS), D_MODEL ** -0.5),
        "moe_w_gate": nrm(ks[25], (N_MOE, N_EXPERTS, D_MODEL, D_EXPERT), D_MODEL ** -0.5),
        "moe_w_up": nrm(ks[26], (N_MOE, N_EXPERTS, D_MODEL, D_EXPERT), D_MODEL ** -0.5),
        "moe_w_down": nrm(ks[27], (N_MOE, N_EXPERTS, D_EXPERT, D_MODEL), D_EXPERT ** -0.5),
        "norm_final_g": gain(ks[28], (D_MODEL,)),
    }

def first_block(x, mem, norm_mix_g, w_in, conv_a_w, conv_a_b, ln_a_g, ln_a_b, conv_b_w,
              ln_c_g, ln_c_b, gmlp_ws, gmlp_b, mix_out_g, w_mix_out, norm_x_g, norm_mem_g,
              w_xq, w_xkv, w_xo, norm_ffn_g, ffn_w_gate, ffn_w_up, ffn_w_down,
              moe_router, moe_w_gate, moe_w_up, moe_w_down, norm_final_g):
    h = x
    for layer in range(DEPTH):
        h = h + hybrid_mixer(rmsnorm(h, norm_mix_g[layer]), w_in[layer], conv_a_w[layer],
                             conv_a_b[layer], ln_a_g[layer], ln_a_b[layer], conv_b_w[layer],
                             ln_c_g[layer], ln_c_b[layer], gmlp_ws[layer], gmlp_b[layer],
                             mix_out_g[layer], w_mix_out[layer])
        h = h + memory_cross_attention(rmsnorm(h, norm_x_g[layer]), rmsnorm(mem, norm_mem_g[layer]),
                                       w_xq[layer], w_xkv[layer], w_xo[layer])
        hn = rmsnorm(h, norm_ffn_g[layer])
        i = layer // 2
        if layer % 2 == 0:
            h = h + swiglu(hn, ffn_w_gate[i], ffn_w_up[i], ffn_w_down[i])
        else:
            h = h + moe_swiglu(hn, moe_router[i], moe_w_gate[i], moe_w_up[i], moe_w_down[i])
    return rmsnorm(h, norm_final_g)


DEPTH_2 = 1

MLSTM_HEADS = 4
MLSTM_HEAD_DIM = 256
MLSTM_WIDTH = MLSTM_HEADS * MLSTM_HEAD_DIM
MLSTM_CHUNK = 128
N_GATE_COLS = 4 * MLSTM_HEADS
LRU_WIDTH = D_MODEL
LRU_BLOCKS = 8
LRU_BLOCK_DIM = LRU_WIDTH // LRU_BLOCKS
LRU_C = 8.0
CONV_WIDTH = 4
CONV_PAD = (2, 1)
PEER_HEADS = 8
PEER_N_KEYS = 128
PEER_N_EXPERTS = PEER_N_KEYS * PEER_N_KEYS
PEER_QUERY_DIM = 256
PEER_HALF = PEER_QUERY_DIM // 2
PEER_TOPK = 16
PEER_TOKEN_BLOCK = 128

IN_SPLIT_SIZES = (MLSTM_WIDTH, MLSTM_WIDTH, N_GATE_COLS, LRU_WIDTH, LRU_WIDTH, 2 * D_MODEL)
D_IN = MLSTM_WIDTH * 2 + N_GATE_COLS + LRU_WIDTH * 2 + 2 * D_MODEL


def rms_norm(x, g):
    x32 = x.astype(jnp.float32)
    y = x32 * lax.rsqrt(jnp.mean(x32 * x32, axis=-1, keepdims=True) + EPS)
    return (y * g.astype(jnp.float32)).astype(x.dtype)

def dwconv_centred(x, w, b):
    y = lax.conv_general_dilated(
        x, w[:, None, :].astype(x.dtype), window_strides=(1,), padding=[CONV_PAD],
        dimension_numbers=("NWC", "WIO", "NWC"), feature_group_count=x.shape[-1])
    return y + b.astype(x.dtype)

def mlstm_scan(q, k, v, log_i, log_f):
    B, H, S, d = q.shape
    nc = S // MLSTM_CHUNK

    def to_chunks(t):
        return jnp.moveaxis(t.reshape((B, H, nc, MLSTM_CHUNK) + t.shape[3:]), 2, 0)

    tril = jnp.tril(jnp.ones((MLSTM_CHUNK, MLSTM_CHUNK), dtype=bool))

    def body(carry, xs):
        C, n, m = carry
        qc, kc, vc, ic, fc = xs
        b = jnp.cumsum(fc, axis=-1)
        d_log = jnp.where(tril, b[..., :, None] - b[..., None, :] + ic[..., None, :], -jnp.inf)
        inter = b + m[..., None]
        m_t = jnp.maximum(inter, jnp.max(d_log, axis=-1))
        w_intra = jnp.exp(d_log - m_t[..., None])
        w_inter = jnp.exp(inter - m_t)
        s = jnp.einsum("bhtd,bhsd->bhts", qc, kc) * w_intra
        num = w_inter[..., None] * jnp.einsum("bhtd,bhde->bhte", qc, C) + jnp.einsum("bhts,bhse->bhte", s, vc)
        den = w_inter * jnp.einsum("bhtd,bhd->bht", qc, n) + jnp.sum(s, axis=-1)
        h = num / jnp.maximum(jnp.abs(den), jnp.exp(-m_t))[..., None]
        g = b[..., -1]
        w_log = g[..., None] - b + ic
        m_new = jnp.maximum(g + m, jnp.max(w_log, axis=-1))
        decay = jnp.exp(g + m - m_new)
        w_state = jnp.exp(w_log - m_new[..., None])
        kw = kc * w_state[..., None]
        C_new = decay[..., None, None] * C + jnp.einsum("bhsd,bhse->bhde", kw, vc)
        n_new = decay[..., None] * n + jnp.sum(kw, axis=2)
        return (C_new, n_new, m_new), h

    init = (jnp.zeros((B, H, d, d), jnp.float32), jnp.zeros((B, H, d), jnp.float32),
            jnp.zeros((B, H), jnp.float32))
    _, h = lax.scan(body, init, (to_chunks(q), to_chunks(k), to_chunks(v), to_chunks(log_i), to_chunks(log_f)))
    return jnp.moveaxis(h, 0, 2).reshape(B, H, S, d)

def mlstm_branch(xm, o_pre, gate_pre, conv_w, conv_b, w_q, w_k, w_v, norm_g):
    B, S, _ = xm.shape
    H, d = MLSTM_HEADS, MLSTM_HEAD_DIM
    xc = jax.nn.silu(dwconv_centred(xm, conv_w, conv_b)).reshape(B, S, H, d)
    xv = xm.reshape(B, S, H, d)
    q = jnp.einsum("bshd,hde->bhse", xc, w_q).astype(jnp.float32)
    k = (jnp.einsum("bshd,hde->bhse", xc, w_k) / math.sqrt(d)).astype(jnp.float32)
    v = jnp.einsum("bshd,hde->bhse", xv, w_v).astype(jnp.float32)
    gates = gate_pre.astype(jnp.float32).reshape(B, S, 4, H).transpose(2, 0, 3, 1)
    i_f, f_f, i_b, f_b = gates[0], gates[1], gates[2], gates[3]
    flip = lambda t: jnp.flip(t, axis=2)
    h_fwd = mlstm_scan(q, k, v, i_f, jax.nn.log_sigmoid(f_f))
    h_bwd = flip(mlstm_scan(flip(q), flip(k), flip(v), flip(i_b), flip(jax.nn.log_sigmoid(f_b))))
    h = jnp.transpose(h_fwd + h_bwd, (0, 2, 1, 3))
    h = rms_norm(h, norm_g.reshape(H, d)).reshape(B, S, MLSTM_WIDTH)
    return (jax.nn.sigmoid(o_pre.astype(jnp.float32)) * h.astype(jnp.float32)).astype(xm.dtype)

def rglru_dir(x, w_r, b_r, w_i, b_i, lam):
    B, S, C = x.shape
    xb = x.reshape(B, S, LRU_BLOCKS, LRU_BLOCK_DIM)
    r = jax.nn.sigmoid(jnp.einsum("bsnc,ncd->bsnd", xb, w_r).reshape(B, S, C) + b_r)
    i = jax.nn.sigmoid(jnp.einsum("bsnc,ncd->bsnd", xb, w_i).reshape(B, S, C) + b_i)
    log_a = -LRU_C * r * jax.nn.softplus(-lam)
    a = jnp.exp(log_a)
    u = jnp.sqrt(-jnp.expm1(2.0 * log_a)) * (i * x)

    def combine(left, right):
        a1, b1 = left
        a2, b2 = right
        return a1 * a2, a2 * b1 + b2

    _, h = lax.associative_scan(combine, (a, u), axis=1)
    return h

def lru_branch(xl, gate_pre, conv_w, conv_b, w_r, b_r, w_i, b_i, lam):
    xc = dwconv_centred(xl, conv_w, conv_b).astype(jnp.float32)
    w_r, b_r, w_i, b_i, lam = (t.astype(jnp.float32) for t in (w_r, b_r, w_i, b_i, lam))
    h_fwd = rglru_dir(xc, w_r[0], b_r[0], w_i[0], b_i[0], lam[0])
    h_bwd = jnp.flip(rglru_dir(jnp.flip(xc, axis=1), w_r[1], b_r[1], w_i[1], b_i[1], lam[1]), axis=1)
    y = (h_fwd + h_bwd) * jax.nn.gelu(gate_pre.astype(jnp.float32), approximate=False)
    return y.astype(xl.dtype)

def peer(h, w_q, sub_keys, expert_u, expert_v):
    B, S, D = h.shape
    nb = (B * S) // PEER_TOKEN_BLOCK
    keys32 = sub_keys.astype(jnp.float32)

    def block_fn(hb):
        tb = hb.shape[0]
        q = jnp.einsum("td,de->te", hb, w_q).astype(jnp.float32).reshape(tb, PEER_HEADS, 2, PEER_HALF)
        scores = jnp.einsum("thpc,hpnc->thpn", q, keys32)
        s_top, i_top = lax.top_k(scores, PEER_TOPK)
        cand = (s_top[:, :, 0, :, None] + s_top[:, :, 1, None, :]).reshape(tb, PEER_HEADS, PEER_TOPK * PEER_TOPK)
        cand_idx = (i_top[:, :, 0, :, None] * PEER_N_KEYS + i_top[:, :, 1, None, :]).reshape(tb, PEER_HEADS, PEER_TOPK * PEER_TOPK)
        best, pos = lax.top_k(cand, PEER_TOPK)
        idx = jnp.take_along_axis(cand_idx, pos, axis=-1).reshape(tb, PEER_HEADS * PEER_TOPK)
        gate = jax.nn.softmax(best, axis=-1).reshape(tb, PEER_HEADS * PEER_TOPK)
        u = jnp.take(expert_u, idx, axis=0)
        act = jax.nn.gelu(jnp.einsum("tkd,td->tk", u, hb).astype(jnp.float32), approximate=False)
        vv = jnp.take(expert_v, idx, axis=0)
        return jnp.einsum("tk,tkd->td", (gate * act).astype(hb.dtype), vv)

    out = lax.map(block_fn, h.reshape(nb, PEER_TOKEN_BLOCK, D))
    return out.reshape(B, S, D)

def second_inputs(seed: int = 0) -> dict:
    key = jax.random.key(seed)
    ks = jax.random.split(key, 32)
    nrm = lambda k, shape, scale: jax.random.normal(k, shape, jnp.float32) * scale
    L = DEPTH_2
    f_base = jnp.linspace(3.0, 6.0, MLSTM_HEADS)
    z = jnp.zeros((MLSTM_HEADS,), jnp.float32)
    gate_base = jnp.stack([z, f_base, z, f_base])
    b_gates = (gate_base[None] + nrm(ks[3], (L, 4, MLSTM_HEADS), 0.1)).reshape(L, N_GATE_COLS)
    a0 = jax.random.uniform(ks[16], (L, 2, LRU_WIDTH), jnp.float32, 0.9, 0.999) ** (1.0 / LRU_C)
    lru_lambda = jnp.log(a0) - jnp.log1p(-a0)
    return {
        "x": nrm(ks[0], (BATCH, SEQ, D_MODEL), 1.0),
        "norm1_g": 1.0 + nrm(ks[1], (L, D_MODEL), 0.02),
        "w_in": nrm(ks[2], (L, D_MODEL, D_IN), D_MODEL ** -0.5),
        "b_gates": b_gates,
        "mlstm_conv_w": nrm(ks[4], (L, CONV_WIDTH, MLSTM_WIDTH), CONV_WIDTH ** -0.5),
        "mlstm_conv_b": nrm(ks[5], (L, MLSTM_WIDTH), 0.02),
        "mlstm_w_q": nrm(ks[6], (L, MLSTM_HEADS, MLSTM_HEAD_DIM, MLSTM_HEAD_DIM), MLSTM_HEAD_DIM ** -0.5),
        "mlstm_w_k": nrm(ks[7], (L, MLSTM_HEADS, MLSTM_HEAD_DIM, MLSTM_HEAD_DIM), MLSTM_HEAD_DIM ** -0.5),
        "mlstm_w_v": nrm(ks[8], (L, MLSTM_HEADS, MLSTM_HEAD_DIM, MLSTM_HEAD_DIM), MLSTM_HEAD_DIM ** -0.5),
        "mlstm_norm_g": 1.0 + nrm(ks[9], (L, MLSTM_WIDTH), 0.02),
        "lru_conv_w": nrm(ks[10], (L, CONV_WIDTH, LRU_WIDTH), CONV_WIDTH ** -0.5),
        "lru_conv_b": nrm(ks[11], (L, LRU_WIDTH), 0.02),
        "lru_w_r": nrm(ks[12], (L, 2, LRU_BLOCKS, LRU_BLOCK_DIM, LRU_BLOCK_DIM), LRU_BLOCK_DIM ** -0.5),
        "lru_b_r": nrm(ks[13], (L, 2, LRU_WIDTH), 0.02),
        "lru_w_i": nrm(ks[14], (L, 2, LRU_BLOCKS, LRU_BLOCK_DIM, LRU_BLOCK_DIM), LRU_BLOCK_DIM ** -0.5),
        "lru_b_i": nrm(ks[15], (L, 2, LRU_WIDTH), 0.02),
        "lru_lambda": lru_lambda,
        "w_branch_mlstm": nrm(ks[17], (L, MLSTM_WIDTH, D_MODEL), MLSTM_WIDTH ** -0.5),
        "w_branch_lru": nrm(ks[18], (L, LRU_WIDTH, D_MODEL), LRU_WIDTH ** -0.5),
        "w_out": nrm(ks[19], (L, D_MODEL, D_MODEL), D_MODEL ** -0.5),
        "norm2_g": 1.0 + nrm(ks[20], (L, D_MODEL), 0.02),
        "peer_w_q": nrm(ks[21], (L, D_MODEL, PEER_HEADS * PEER_QUERY_DIM), D_MODEL ** -0.5),
        "peer_sub_keys": nrm(ks[22], (L, PEER_HEADS, 2, PEER_N_KEYS, PEER_HALF), PEER_HALF ** -0.5),
        "peer_u": nrm(ks[23], (L, PEER_N_EXPERTS, D_MODEL), D_MODEL ** -0.5),
        "peer_v": nrm(ks[24], (L, PEER_N_EXPERTS, D_MODEL), PEER_HEADS ** -0.5),
        "final_norm_g": 1.0 + nrm(ks[25], (D_MODEL,), 0.02),
    }

def second_block(x, norm1_g, w_in, b_gates, mlstm_conv_w, mlstm_conv_b, mlstm_w_q, mlstm_w_k, mlstm_w_v,
              mlstm_norm_g, lru_conv_w, lru_conv_b, lru_w_r, lru_b_r, lru_w_i, lru_b_i, lru_lambda,
              w_branch_mlstm, w_branch_lru, w_out, norm2_g, peer_w_q, peer_sub_keys, peer_u, peer_v,
              final_norm_g):
    split_points = np.cumsum(IN_SPLIT_SIZES)[:-1].tolist()
    for l in range(DEPTH_2):
        h = rms_norm(x, norm1_g[l])
        proj = jnp.einsum("bsd,de->bse", h, w_in[l])
        xm, o_pre, gate_pre, xl, lru_gate, merge_pre = jnp.split(proj, split_points, axis=-1)
        gate_pre = gate_pre + b_gates[l].astype(gate_pre.dtype)
        y_m = mlstm_branch(xm, o_pre, gate_pre, mlstm_conv_w[l], mlstm_conv_b[l], mlstm_w_q[l],
                           mlstm_w_k[l], mlstm_w_v[l], mlstm_norm_g[l])
        y_l = lru_branch(xl, lru_gate, lru_conv_w[l], lru_conv_b[l], lru_w_r[l], lru_b_r[l],
                         lru_w_i[l], lru_b_i[l], lru_lambda[l])
        g_m, g_l = jnp.split(jax.nn.sigmoid(merge_pre), 2, axis=-1)
        merged = (g_m * jnp.einsum("bsc,cd->bsd", y_m, w_branch_mlstm[l])
                  + g_l * jnp.einsum("bsc,cd->bsd", y_l, w_branch_lru[l]))
        x = x + jnp.einsum("bsd,de->bse", merged, w_out[l])
        h2 = rms_norm(x, norm2_g[l])
        x = x + peer(h2, peer_w_q[l], peer_sub_keys[l], peer_u[l], peer_v[l])
    return rms_norm(x, final_norm_g)


def setup_inputs(seed=0):
    out = dict(first_inputs(seed))
    for name, value in second_inputs(seed + 1).items():
        if name != "x":
            out[name + "_2"] = value
    return out


def reference(
    x, mem, norm_mix_g, w_in, conv_a_w, conv_a_b, ln_a_g, ln_a_b, conv_b_w, ln_c_g, ln_c_b,
    gmlp_ws, gmlp_b, mix_out_g, w_mix_out, norm_x_g, norm_mem_g, w_xq, w_xkv, w_xo, norm_ffn_g,
    ffn_w_gate, ffn_w_up, ffn_w_down, moe_router, moe_w_gate, moe_w_up, moe_w_down,
    norm_final_g, norm1_g_2, w_in_2, b_gates_2, mlstm_conv_w_2, mlstm_conv_b_2, mlstm_w_q_2,
    mlstm_w_k_2, mlstm_w_v_2, mlstm_norm_g_2, lru_conv_w_2, lru_conv_b_2, lru_w_r_2, lru_b_r_2,
    lru_w_i_2, lru_b_i_2, lru_lambda_2, w_branch_mlstm_2, w_branch_lru_2, w_out_2, norm2_g_2,
    peer_w_q_2, peer_sub_keys_2, peer_u_2, peer_v_2, final_norm_g_2,
):
    x = first_block(
        x, mem, norm_mix_g, w_in, conv_a_w, conv_a_b, ln_a_g, ln_a_b, conv_b_w, ln_c_g, ln_c_b,
        gmlp_ws, gmlp_b, mix_out_g, w_mix_out, norm_x_g, norm_mem_g, w_xq, w_xkv, w_xo,
        norm_ffn_g, ffn_w_gate, ffn_w_up, ffn_w_down, moe_router, moe_w_gate, moe_w_up,
        moe_w_down, norm_final_g,
    )
    return second_block(
        x, norm1_g_2, w_in_2, b_gates_2, mlstm_conv_w_2, mlstm_conv_b_2, mlstm_w_q_2,
        mlstm_w_k_2, mlstm_w_v_2, mlstm_norm_g_2, lru_conv_w_2, lru_conv_b_2, lru_w_r_2,
        lru_b_r_2, lru_w_i_2, lru_b_i_2, lru_lambda_2, w_branch_mlstm_2, w_branch_lru_2,
        w_out_2, norm2_g_2, peer_w_q_2, peer_sub_keys_2, peer_u_2, peer_v_2, final_norm_g_2,
    )


_drawn_inputs = setup_inputs


def setup_inputs(seed=0):
    import zlib

    import numpy as np

    out = dict(_drawn_inputs(seed))
    spreads = {}
    factors = {'norm_x_g': 4.779,
     'mlstm_norm_g_2': 13.619,
     'lru_b_r_2': 122.231,
     'lru_b_i_2': 22.607,
     'final_norm_g_2': 22.434,
     'norm2_g_2': 11.514,
     'lru_conv_b_2': 2.976}
    for name, (base, spread) in spreads.items():
        noise = np.random.default_rng([zlib.crc32(name.encode()), seed]).standard_normal(out[name].shape)
        drawn = base * np.exp(spread * noise) if base else spread * noise
        out[name] = __import__('jax').numpy.asarray(drawn.astype(out[name].dtype))
    for name, factor in factors.items():
        out[name] = (out[name] * factor).astype(out[name].dtype)
    return out
```

```python
from contextlib import ExitStack

import concourse.bass as bass
from concourse import mybir
from concourse.alu_op_type import AluOpType as ALU

ACT = mybir.ActivationFunctionType
AX = mybir.AxisListType
F32 = mybir.dt.float32
I32 = mybir.dt.int32
U32 = mybir.dt.uint32

P = 128
EPS = 1e-6
DEPTH, D, SEQ = 2, 1024, 256
KT, TB = D // P, SEQ // P
A_W, BC_W = 384, 320
A_TAPS, B_TAPS, C_TAPS = 31, 3, 4
HEADS, HD = 4, 256
FF, N_EXP, EXP_W = 2816, 8, 3584
FT, ET = FF // P, EXP_W // P
LRU_C = 8.0
PK, PHEADS, TOPK = 128, 8, 16
SLOTS = PHEADS * TOPK
NEG = -3.0e38
RING = 7
SLOT_F = KT * 512
GATHER, BATCH = 16, 4
BATCHES = GATHER // BATCH
ROUNDS = SLOTS // GATHER
CHUNKS = EXP_W // 512
EXP_GROUPS, EXP_V, EXP_A = 32, 16, 16
EXP_TILES = 3 * CHUNKS


class Groups:

    def __init__(self, pe, banks, group_done, took_sems, loads):
        self.pe, self.banks, self.group_done, self.took_sems = pe, banks, group_done, took_sems
        self.total, self.given = 0, {"v": 0, "a": 0}
        self.after, self.took = {}, {}
        self.loads, self.loaded, self.slots = loads, [0] * RING, []
        self.freed, self.need = [], []
        self.turn = None

    def begin(self, who, key):
        n = self.given[who]
        if n >= 4:
            extra = 0 if self.turn is None else self.turn * EXP_V
            self.pe.wait_ge(self.took_sems[who], n - 3 + extra)
        self.given[who] = n + 1
        self.total += 1
        self.after[key], self.took[key] = self.total, n + 1
        return self.banks[who][n % 4]

    def end(self, mm):
        mm.then_inc(self.group_done, 1)

    def tile(self, dmas=1, per_turn=0):
        n = len(self.need)
        slot = n % RING
        self.loaded[slot] += 16 * dmas
        self.need.append(self.loaded[slot])
        self.freed.append(None)
        extra = 0 if self.turn is None else self.turn * per_turn
        self.pe.wait_ge(self.loads[slot], self.loaded[slot] + extra)
        return slot

    def free(self):
        self.freed[-1] = (self.group_done, self.total, EXP_GROUPS)

    def loop(self, turn):
        self.turn, self.start = turn, (self.total, dict(self.given), len(self.need))

    def close(self, turns):
        total, given, tiles = self.start
        assert self.total - total == EXP_GROUPS and len(self.need) - tiles == EXP_TILES
        assert self.given["v"] - given["v"] == EXP_V and self.given["a"] - given["a"] == EXP_A
        self.turn = None
        self.total += EXP_GROUPS * (turns - 1)
        self.given["v"] += EXP_V * (turns - 1)
        self.given["a"] += EXP_A * (turns - 1)
        self.loaded = [x + 16 * (EXP_TILES // RING) * (turns - 1) for x in self.loaded]
        self.final = {"v": self.given["v"], "a": self.given["a"]}


class Steps:

    def __init__(self, eng, sem):
        self.eng, self.sem, self.n, self.turn, self.per = eng, sem, 0, None, 0

    def value(self, n):
        return n if self.turn is None else n + self.turn * self.per

    def then(self, ins):
        ins.then_inc(self.sem, 1)
        self.n += 1

    def settle(self, back=0):
        if self.n > back:
            self.eng.wait_ge(self.sem, self.value(self.n - back))

    def now(self, ins):
        self.then(ins)
        self.settle()


class Tally:
    def __init__(self):
        self.n = {}

    def next(self, name):
        self.n[name] = self.n.get(name, 0) + 1
        return self.n[name]


def two_blocks(nc, t, out):
    with ExitStack() as ctx:
        def sb(name, shape, dt=F32):
            return ctx.enter_context(nc.sbuf_tensor(name, shape, dt))

        def sem(name):
            return ctx.enter_context(nc.semaphore(name))

        ring = sb("weight_ring", [P, RING, SLOT_F])
        hF = sb("residual", [P, KT, SEQ])
        xF = sb("normed", [P, KT, SEQ])
        squares = sb("squares", [P, KT, SEQ])
        ident = sb("ident", [P, P])
        ones = sb("ones", [P, P])
        lower = sb("lower", [P, P])
        half_ones = sb("half_ones", [P, P])
        tri = sb("tri", [P, P])
        iota = sb("iota", [P, P])
        pair_sel = sb("pair_sel", [5, 3, P])
        gate_bias = sb("gmlp_bias", [5, DEPTH, P])
        spatialT = sb("spatialT", [P, DEPTH, 5, P])
        cols = sb("cols", [P, 474])
        mean_row = sb("neg_mean", [P, SEQ])
        std_row = sb("std", [P, SEQ])
        rstd_row = sb("rstd", [P, SEQ])
        eps = sb("eps", [P, 1])
        router = sb("router", [P, KT, N_EXP])
        small = sb("small", [P, 256])
        extra_flag = sb("extra_flag", [P, 1], I32)
        WORK = 13848
        work = sb("work", [P, WORK])

        def view(off, *shape):
            n = 1
            for s in shape:
                n *= s
            assert off + n <= WORK, (off, shape)
            flat = work[:, off:off + n]
            if len(shape) == 1:
                return flat
            names = "abcd"[:len(shape)]
            kw = {c: s for c, s in zip(names, shape)}
            return flat.rearrange(f"p ({' '.join(names)}) -> p {' '.join(names)}", **kw)

        psum_all = ctx.enter_context(nc.psum_tensor("banks", [P, 8, 512], F32))
        psum = [psum_all[:, i, :] for i in range(8)]
        banks = {"v": psum[0:4], "a": psum[4:8]}

        def pair(bank, n=2, w=SEQ):
            return bank[:, 0:n * w].rearrange("p (a b) -> p a b", a=n)

        def c_vec(l, which, k):
            return cols[:, 49 * l + which + k:49 * l + which + k + 1]
        MIX_G, X_G, MEM_G, FFN_G, OUT_G, CONVA_B, LNA_G, LNA_B = 0, 8, 16, 24, 32, 40, 43, 46
        C1, C2 = 98, 98 + 2 * 93
        N1_G, MC_B, MN_G, LC_B, BR, BI, LAM, N2_G, MC_W = 0, 8, 16, 24, 32, 48, 64, 80, 88
        C3 = C2 + 120
        LC_W, FIN_G = 0, 32
        C4 = C3 + 40

        def col(i, rows=P):
            return cols[0:rows, i:i + 1]

        def bc_col(l, which, k):
            return col(C4 + 10 * k + 5 * l + which, P if k < 2 else 64)

        MEM = WORK - KT * SEQ
        mem_hat = view(MEM, KT, SEQ)
        x_in, mem_in = view(0, TB, D), view(2048, TB, D)
        rows = view(4096, 5, P)
        bc_rows = view(4736, 320)
        spatial_in = view(5056, DEPTH, 5, P)
        sig_a = view(0, 3, SEQ)
        ya_pad = view(768, 3, SEQ + A_TAPS - 1)
        conv_a = view(1626, 3, SEQ)
        c_gate = view(2394, 3, SEQ)
        yb_pad = view(3162, 3, SEQ + B_TAPS - 1)
        b_gate = view(3936, 3, SEQ)
        conv_b = view(4704, 3, SEQ)
        c_u = view(5472, 3, SEQ)
        c_v = view(6240, 3, SEQ)
        vT = view(7008, TB, BC_W)
        yF = view(7648, KT, SEQ)
        std8 = view(9696, KT, SEQ)
        mem_g, qF, kF = view(0, KT, SEQ), view(2048, KT, SEQ), view(4096, KT, SEQ)
        vM = view(6144, TB, D)
        probs = view(8192, HEADS, TB, SEQ)
        probsT = squares[:, :, :].rearrange("p (h m) s -> p h m s", h=HEADS)
        oF = view(0, KT, SEQ)
        hid = view(0, FT, SEQ)
        sil = view(5632, 2, 2, SEQ)
        xT = view(0, TB, D)
        pick = view(2048, TB, N_EXP, P)
        put = squares[:, :, :]
        xeT = view(4096, KT, P)
        he = view(5120, EXP_W)
        heT = view(8704, ET, P)
        ye = view(12288, D)
        weighted = view(5120, TB, N_EXP, P)

        def pairs_of(off):
            return small[:, off:off + TB * N_EXP].rearrange("p (b e) -> p b e", b=TB)
        logits, top, top_at, first, second, chosen, share, place = (pairs_of(16 * i) for i in range(8))
        gap, ratio, total_w, w_first, w_second = (small[:, 128 + 2 * i:130 + 2 * i] for i in range(5))
        counts, most = small[:, 144:152], small[:, 152:153]
        top_raw = small[:, 160:176].bitcast(U32).rearrange("p (b e) -> p b e", b=TB)

        xm_pad = view(0, KT, SEQ + C_TAPS - 1)
        xm_conv = view(2072, KT, SEQ)
        qM, kM = view(4120, KT, SEQ), view(6168, KT, SEQ)
        vL = view(8216, TB, D)
        scoresT = view(10264, 2, 2, 2, P)
        decay = view(11288, 2, 2, P)
        intra = view(11800, 2, 2, P)
        floor_ = view(12312, 2, SEQ)
        head_sel = view(12824, 8, P)
        gate_cols = squares[:, 0, :].rearrange("p (b g r) -> p b g r", b=TB, g=2)
        g_in, g_fo, g_t, g_z, g_w, g_q, g_b, g_a = (squares[0:64, i, :] for i in range(8))
        g_max, g_sum, g_zero, g_one = g_t, g_z, g_w, mean_row[0:64, :]
        a_cols = small[:, 96:224].rearrange("p (b r) -> p b r", b=TB)
        gate_row = small[:, 240:256]
        hM = view(2072, KT, SEQ)
        o_sig = view(0, KT, SEQ)
        std4 = view(10520, HEADS, SEQ)
        g_m, merged = view(4120, KT, SEQ), view(6168, KT, SEQ)
        xl_pad = view(8216, KT, SEQ + C_TAPS - 1)
        xl_conv = view(0, KT, SEQ)
        h_l = view(2072, KT, SEQ)
        gate_l = view(4120, KT, SEQ)
        lru_a, lru_u = view(8216, KT, SEQ), view(10264, KT, SEQ)
        lru_t = squares
        half_tmp = view(12312, 4, SEQ)
        g_l = view(0, KT, SEQ)
        pair_tmp = view(12312, 2, SEQ)
        lam_t, lam_z, lam_w, lam_q, lam_neg, lam_pos = (small[:, 16 * i:16 * i + 16] for i in range(6))

        qP, keysT = view(0, 2 * PHEADS, SEQ), view(4096, 2 * PHEADS, PK)
        key_scores, key_rest = view(6144, 2 * PHEADS, PK), view(8192, 2 * PHEADS, PK)
        pairs_, pairs_rest = view(6144, PHEADS, TOPK * TOPK), view(8192, PHEADS, TOPK * TOPK)
        key_top, key_at = view(10240, 2 * PHEADS, TOPK), view(10496, 2 * PHEADS, TOPK).bitcast(U32)
        key_at_f = view(10752, PHEADS, 2, TOPK)
        best, best_at = view(11008, PHEADS, TOPK), view(11136, PHEADS, TOPK).bitcast(U32)
        half_raw = [view(11264 + SLOTS * i, SLOTS).bitcast(U32) for i in range(2)]
        half_at = [view(11520 + SLOTS * i, SLOTS) for i in range(2)]
        half_key = [view(11776 + SLOTS * i, SLOTS) for i in range(2)]
        gates = view(12032, TB, PHEADS, TOPK)
        rows_at = view(12288, TB * SLOTS).bitcast(U32)
        acts = view(12544, TB * SLOTS)
        final_gain = view(12800, D)
        match = squares[:, :, :].rearrange("p k s -> p (k s)").rearrange("p (a j) -> p a j", j=TOPK)
        zero_row = squares[0:1, 0:2, :].rearrange("p k s -> p (k s)")
        gathered_rows = ring[:, 0:GATHER * D // SLOT_F, :].rearrange("p s (r d) -> p (s r) d", d=D)
        diag = view(0, BATCHES, BATCH, P)
        final_sq = view(4096, D)
        final_rows = view(6144, TB, D)
        stage = sb("gather_stage", [P, GATHER], U32)
        dots = small[:, 0:GATHER]
        gate_sum, gate_inv = small[:, 16:24], small[:, 24:32]
        final_ss, final_std, final_rstd = (small[:, 32 + 2 * i:34 + 2 * i] for i in range(3))

        loads = [sem(f"weights_loaded{i}") for i in range(RING)]
        group_done = sem("pe_group_done")
        dve_took, act_took = sem("dve_took"), sem("act_took")
        took_sems = {"v": dve_took, "a": act_took}
        dve_step, act_step, pool_step = sem("dve_step"), sem("act_step"), sem("pool_step")
        inputs_loaded = sem("inputs_loaded")
        params_loaded = sem("params_loaded")
        consts_ready = sem("consts_ready")
        sq_ready = sem("squares_ready")
        x_ready = sem("normed_ready")
        conv_ready = sem("conv_ready")
        centred = sem("centred")
        ln_ready = sem("ln_ready")
        ya_ready = sem("ya_ready")
        y_all = sem("y_all_ready")
        y_ready = sem("y_ready")
        cv_ready = sem("cv_ready")
        mask_ready = sem("spatial_masked")
        mem_normed = sem("mem_normed")
        mem_ready = sem("mem_ready")
        max_ready = sem("max_ready")
        probs_ready = sem("probs_ready")
        exp_ready = sem("exp_ready")
        out_done = sem("out_stored")
        routing_ready = sem("routing_ready")
        chosen_ready = sem("chosen_ready")
        gap_ready = sem("logit_gap_ready")
        ratio_ready = sem("expert_ratio_ready")
        weighted_ready = sem("weighted_ready")
        pick_ready = sem("pick_ready")
        final_ready = sem("first_block_normed")
        gates_ready = sem("gate_columns_ready")
        abs_ready, exp_done = sem("abs_ready"), sem("exp_done")
        a_ready = sem("gate_rows_ready")
        sel_ready = sem("head_sel_ready")
        xm_conv_ready, xm_act = sem("xm_conv_ready"), sem("xm_activated")
        arg_ready = sem("decay_argument_ready")
        intra_ready = sem("intra_ready")
        h_sum_ready = sem("mlstm_sum_ready")
        ym_ready = sem("y_mlstm_ready")
        xl_conv_ready = sem("xl_conv_ready")
        lam_ready = sem("lam_ready")
        gated_ready = sem("lru_input_gated")
        lru_a_ready = sem("lru_decay_ready")
        lru_v_ready, lru_s_ready = sem("lru_scale_squared_ready"), sem("lru_scale_ready")
        lru_free = sem("lru_buffers_free")
        yl_ready = sem("y_lru_ready")
        merged_ready = sem("merged_ready")
        index_ready = sem("peer_index_ready")
        margin_ready, margin_exp = sem("gate_margin_ready"), sem("gate_margin_exp")
        gathered = [sem(f"rows_gathered{i}") for i in range(BATCHES)]
        staged, pool_turn = sem("indices_staged"), sem("pool_turn")
        dot_done, dots_kept = sem("dot_batch_done"), sem("dots_kept")
        act_ready, weight_ready = sem("peer_activation_ready"), sem("peer_weight_ready")
        diag_ready, mix_done = sem("diag_ready"), sem("mix_batch_done")
        zero_ready = sem("zero_row_ready")
        gain_loaded = sem("final_gain_loaded")
        final_std_ready, final_out = sem("final_std_ready"), sem("final_rows_ready")
        down_used, more_down_used = sem("down_tile_used"), sem("more_down_tile_used")
        more_places = sem("more_places")
        more_done = sem("more_groups_done")
        more_took = {"v": sem("more_dve_took"), "a": sem("more_act_took")}
        more_loads = [sem(f"more_weights_loaded{i}") for i in range(RING)]

        EPS_AP = eps[:, 0:1]
        G = None
        passes = []
        N_NORMS = 3 * DEPTH + 1
        N_PARAMS = DEPTH * 17 + 13
        block = ctx.enter_context(nc.Block())

        @block.tensor
        def _(pe):
            nonlocal G
            G = Groups(pe, banks, group_done, took_sems, loads)
            seen = Tally()

            def transposes(who, key, parts):
                bank = G.begin(who, key)
                for off, a in parts:
                    k, m = a.shape[0], a.shape[1]
                    mm = pe.transpose(bank[0:m, off:off + k], a, ident[0:k, 0:k])
                G.end(mm)

            def sum_features(who, key, src, n=KT, weights=None, w=SEQ):
                bank = G.begin(who, key)
                for k in range(n):
                    a = src(k)
                    mm = pe.matmul(bank[:, 0:w], (weights or ones)[0:a.shape[0], :], a,
                                   start=(k == 0), stop=(k == n - 1))
                G.end(mm)

            def norm_sums(key):
                pe.wait_ge(sq_ready, seen.next("sq"))
                sum_features("a", key, lambda k: squares[:, k, :])

            def linear(key, who, n_tiles, x, kts, widths=(0, P, 2 * P, 3 * P), per_group=2, dmas=1, ms=None):
                c = 0
                for tile in range(n_tiles):
                    slot = G.tile(dmas)
                    for i, off in enumerate(widths):
                        m = P if ms is None else ms[i]
                        if c % per_group == 0:
                            bank = G.begin(who, (key, c // per_group))
                        o = bank[0:m, (c % per_group) * SEQ:(c % per_group + 1) * SEQ]
                        for k in range(kts):
                            mm = pe.matmul(o, weight(slot, kts, widths)[:, k, off:off + m], x(k),
                                           start=(k == 0), stop=(k == kts - 1))
                        c += 1
                        if c % per_group == 0 or (tile == n_tiles - 1 and i == len(widths) - 1):
                            G.end(mm)
                    G.free()

            def weight(slot, kts, widths, cols_n=None):
                n = cols_n or 512
                return ring[:, slot, 0:kts * n].rearrange("p (k n) -> p k n", k=kts)

            pe.wait_ge(consts_ready, 1)
            pe.wait_ge(inputs_loaded, 32)
            for who, src, name in (("v", x_in, "x"), ("a", mem_in, "mem")):
                for g in range(4):
                    transposes(who, (name, g), [((k % 2) * SEQ + b * P, src[:, b, k * P:(k + 1) * P])
                                                for k in (2 * g, 2 * g + 1) for b in range(TB)])
            pe.wait_ge(params_loaded, 16 * N_PARAMS)
            parts = [(0, rows[0:98, 0, :]), (C1, rows[0:93, 1, :]), (C1 + 93, rows[0:93, 2, :]),
                     (C2, rows[0:120, 3, :]), (C3, rows[0:40, 4, :])]
            parts += [(C4 + 10 * k, bc_rows[0:10, k * P:min((k + 1) * P, 320)]) for k in range(3)]
            transposes("v", "cols", parts)
            for l in range(DEPTH):
                transposes("a", ("spatial", l, 0), [(g * P, spatial_in[:, l, g, :]) for g in range(4)])
            transposes("a", "spatial_last", [(l * P, spatial_in[:, l, 4, :]) for l in range(DEPTH)])
            norm_sums("mem_ms")

            def mixer(l):
                norm_sums(("mix_ms", l))
                pe.wait_ge(x_ready, seen.next("x"))
                x = lambda k: xF[:, k, :]

                def section(name, who, width, offs, ms):
                    slot = G.tile()
                    w = ring[:, slot, 0:KT * width].rearrange("p (k n) -> p k n", k=KT)
                    for g, tiles in enumerate(((0, 1), (2,))):
                        bank = G.begin(who, (name, l, g))
                        for i, c in enumerate(tiles):
                            for k in range(KT):
                                mm = pe.matmul(bank[0:ms[c], i * SEQ:(i + 1) * SEQ], w[:, k, offs[c]:offs[c] + ms[c]],
                                               x(k), start=(k == 0), stop=(k == KT - 1))
                        G.end(mm)
                    G.free()

                section("a_gate", "a", A_W, (0, P, 2 * P), (P, P, P))
                section("a_val", "v", A_W, (0, P, 2 * P), (P, P, P))
                section("c_gate", "a", BC_W, (0, P, 2 * P), (P, P, 64))
                section("b_in", "v", BC_W, (0, P, 2 * P), (P, P, 64))
                section("b_gate", "a", BC_W, (0, P, 2 * P), (P, P, 64))
                section("c_v", "a", BC_W, (0, P, 2 * P), (P, P, 64))
                section("c_u", "a", BC_W, (0, P, BC_W - P), (P, P, P))

                def three(src):
                    return lambda k: src[0:(P if k < 2 else 64), k, :]

                pe.wait_ge(act_took, G.took["c_v", l, 1])
                sum_features("a", ("c_mean", l), three(c_v), 3)
                pe.wait_ge(sq_ready, seen.next("sq"))
                sum_features("a", ("c_var", l), three(squares), 3)
                pe.wait_ge(cv_ready, l + 1)
                for b in range(TB):
                    transposes("v", ("c_vT", l, b), [(k * P, three(c_v)(k)[:, b * P:(b + 1) * P]) for k in range(3)])
                pe.wait_ge(dve_took, G.took["c_vT", l, 1])
                pe.wait_ge(mask_ready, 1)
                for p in range(3):
                    n = 2 if p < 2 else 1
                    first = p * P if p < 2 else BC_W - P
                    for b in range(TB):
                        bank = G.begin("v", ("mixed", l, p, b))
                        for i in range(n):
                            o = bank[:, i * P:(i + 1) * P]
                            pe.matmul(o, vT[:, b, first:first + P], spatialT[:, l, 2 * p + i, :], start=True, stop=False)
                            mm = pe.matmul(o, pair_sel[:, p, :], gate_bias[:, l, :], start=False, stop=True)
                        G.end(mm)
                pe.wait_ge(conv_ready, l + 1)
                sum_features("a", ("a_mean", l), lambda k: conv_a[:, k, :], 3)
                pe.wait_ge(sq_ready, seen.next("sq"))
                sum_features("a", ("a_var", l), lambda k: squares[:, k, :], 3)
                pe.wait_ge(sq_ready, seen.next("sq"))
                for g in range(4):
                    bank = G.begin("a", ("group_ms", l, g))
                    for i in range(2):
                        mm = pe.matmul(bank[:, i * SEQ:(i + 1) * SEQ], half_ones[:, :], squares[:, 2 * g + i, :],
                                       start=True, stop=True)
                    G.end(mm)
                pe.wait_ge(y_ready, l + 1)
                linear(("mix_out", l), "v", 2, lambda k: yF[:, k, :], KT, dmas=4)

            def attention(l):
                pe.wait_ge(mem_ready, l + 1)
                linear(("k", l), "a", 2, lambda k: mem_g[:, k, :], KT)
                for half in range(2):
                    slot = G.tile()
                    for b in range(TB):
                        bank = G.begin("a", ("v", l, half, b))
                        for k in range(KT):
                            mm = pe.matmul(bank[:, :], mem_g[:, k, b * P:(b + 1) * P], weight(slot, KT, None)[:, k, :],
                                           start=(k == 0), stop=(k == KT - 1))
                        G.end(mm)
                    G.free()
                norm_sums(("x_ms", l))
                pe.wait_ge(x_ready, seen.next("x"))
                linear(("q", l), "a", 2, lambda k: xF[:, k, :], KT)
                pe.wait_ge(act_took, G.took[("q", l), 3])
                for h in range(HEADS):
                    bank = G.begin("a", ("scores", l, h))
                    for b in range(TB):
                        for j in range(2):
                            mm = pe.matmul(bank[:, b * SEQ:(b + 1) * SEQ], qF[:, 2 * h + j, b * P:(b + 1) * P],
                                           kF[:, 2 * h + j, :], start=(j == 0), stop=(j == 1))
                    G.end(mm)
                for h in range(HEADS):
                    pe.wait_ge(probs_ready, HEADS * l + h + 1)
                    transposes("v", ("probsT", l, h), [(m * SEQ + b * P, probs[:, h, b, m * P:(m + 1) * P])
                                                       for m in range(TB) for b in range(TB)])
                for h in range(HEADS):
                    pe.wait_ge(dve_took, G.took["probsT", l, h])
                    bank = G.begin("a", ("o", l, h))
                    for e in range(2):
                        for m in range(TB):
                            mm = pe.matmul(bank[:, e * SEQ:(e + 1) * SEQ], vM[:, m, h * HD + e * P:h * HD + (e + 1) * P],
                                           probsT[:, h, m, :], start=(m == 0), stop=(m == TB - 1))
                    G.end(mm)
                pe.wait_ge(act_took, G.took["o", l, HEADS - 1])
                linear(("xo", l), "v", 2, lambda k: oF[:, k, :], KT)

            def feed_forward():
                norm_sums("ffn_ms")
                pe.wait_ge(x_ready, seen.next("x"))
                for c in range(FT // 2):
                    slot = G.tile(2)
                    w = ring[:, slot, :].rearrange("p (a k n) -> p a k n", a=2, k=KT)
                    for a, who in ((0, "a"), (1, "v")):
                        bank = G.begin(who, ("ffn", a, c))
                        for i in range(2):
                            for k in range(KT):
                                mm = pe.matmul(bank[:, i * SEQ:(i + 1) * SEQ], w[:, a, k, i * P:(i + 1) * P], xF[:, k, :],
                                               start=(k == 0), stop=(k == KT - 1))
                        G.end(mm)
                    G.free()
                pe.wait_ge(dve_took, G.took["ffn", 1, FT // 2 - 1])
                for c in range(KT):
                    slot = G.tile()
                    w = ring[:, slot, 0:FT * P].rearrange("p (k n) -> p k n", k=FT)
                    if c % 2 == 0:
                        bank = G.begin("v", ("ffn_down", c // 2))
                    for k in range(FT):
                        mm = pe.matmul(bank[:, (c % 2) * SEQ:(c % 2 + 1) * SEQ], w[:, k, :], hid[:, k, :],
                                       start=(k == 0), stop=(k == FT - 1))
                    if c % 2 == 1:
                        G.end(mm)
                        G.free()
                        G.freed[-2] = G.freed[-1]

            def routing():
                norm_sums("moe_ms")
                pe.wait_ge(x_ready, seen.next("x"))
                bank = G.begin("v", "logits")
                for b in range(TB):
                    for k in range(KT):
                        mm = pe.matmul(bank[:, b * N_EXP:(b + 1) * N_EXP], xF[:, k, b * P:(b + 1) * P], router[:, k, :],
                                       start=(k == 0), stop=(k == KT - 1))
                G.end(mm)
                for b in range(TB):
                    for half in range(2):
                        transposes("a", ("xT", b, half), [(i * P, xF[:, 4 * half + i, b * P:(b + 1) * P]) for i in range(4)])
                pe.wait_ge(chosen_ready, 1)
                bank = G.begin("v", "places")
                pe.matmul(bank[:, 0:N_EXP], tri[:, :], chosen[:, 0, :], start=True, stop=True)
                pe.matmul(bank[:, N_EXP:2 * N_EXP], ones[:, :], chosen[:, 0, :], start=True, stop=False)
                pe.matmul(bank[:, N_EXP:2 * N_EXP], tri[:, :], chosen[:, 1, :], start=False, stop=True)
                pe.matmul(bank[:, 2 * N_EXP:3 * N_EXP], ones[:, :], chosen[:, 0, :], start=True, stop=False)
                G.end(pe.matmul(bank[:, 2 * N_EXP:3 * N_EXP], ones[:, :], chosen[:, 1, :], start=False, stop=True))

            def experts(n):
                g = passes[n]
                pe.wait_ge(weighted_ready, n + 1)
                for e in range(N_EXP):
                    bank = g.begin("v" if e < 4 else "a", ("put", e))
                    for b in range(TB):
                        mm = pe.transpose(bank[:, b * P:(b + 1) * P], weighted[:, b, e, :], ident[:, :])
                    g.end(mm)
                pe.wait_ge(g.took_sems["a"], g.took["put", N_EXP - 1])
                pe.wait_ge(g.took_sems["v"], g.took["put", 3])
                pe.wait_ge(act_took, G.took["xT", TB - 1, 1])
                pe.wait_ge(pick_ready, n + 1)
                with pe.Fori(0, N_EXP) as e:
                    g.loop(e)

                    def taken(who, key):
                        pe.wait_ge(g.took_sems[who], g.took[key] + e * (EXP_V if who == "v" else EXP_A))

                    for i, tiles in enumerate(((0, 1), (2, 3), (4, 5), (6,), (7,))):
                        bank = g.begin("v", ("gather", i))
                        for j, k in enumerate(tiles):
                            for b in range(TB):
                                mm = pe.matmul(bank[:, j * P:(j + 1) * P], xT[:, b, k * P:(k + 1) * P],
                                               pick[:, b, bass.ds(e, 1), :].rearrange("p o s -> p (o s)"),
                                               start=(b == 0), stop=(b == TB - 1))
                        g.end(mm)
                    taken("v", ("gather", 4))

                    def hidden_transposes(c):
                        taken("v", ("up", c))
                        bank = g.begin("a", ("hidden", c))
                        for i in range(4):
                            mm = pe.transpose(bank[:, i * P:(i + 1) * P], he[:, c * 512 + i * P:c * 512 + (i + 1) * P], ident[:, :])
                        g.end(mm)

                    for c in range(CHUNKS):
                        for who, name in (("a", "gate"), ("v", "up")):
                            slot = g.tile(1, 16 * (EXP_TILES // RING))
                            bank = g.begin(who, (name, c))
                            for k in range(KT):
                                mm = pe.matmul(bank[:, :], xeT[:, k, :], weight(slot, KT, None)[:, k, :],
                                               start=(k == 0), stop=(k == KT - 1))
                            g.end(mm)
                            g.free()
                        if c >= 1:
                            hidden_transposes(c - 1)
                    hidden_transposes(CHUNKS - 1)
                    halves = [g.begin("a", ("down", h)) for h in range(2)]
                    for c in range(CHUNKS):
                        slot = g.tile(1, 16 * (EXP_TILES // RING))
                        w = ring[:, slot, :].rearrange("p (k n) -> p k n", k=4)
                        taken("a", ("hidden", c))
                        for i in range(4):
                            f = 4 * c + i
                            for h in range(2):
                                mm = pe.matmul(halves[h][:, :], heT[:, f, :], w[:, i, h * 512:(h + 1) * 512],
                                               start=(f == 0), stop=(f == ET - 1))
                                if f == ET - 1:
                                    g.end(mm)
                        if c < CHUNKS - 1:
                            mm.then_inc(g.down_used, 1)
                            g.freed[-1] = (g.down_used, c + 1, CHUNKS - 1)
                        else:
                            g.free()
                    taken("a", ("down", 1))
                    for k in range(KT):
                        if k % 2 == 0:
                            bank = g.begin("v", ("scatter", k // 2))
                        mm = pe.matmul(bank[:, (k % 2) * SEQ:(k % 2 + 1) * SEQ], ye[:, k * P:(k + 1) * P],
                                       put[:, bass.ds(e, 1), :].rearrange("p o s -> p (o s)"), start=True, stop=True)
                        if k % 2 == 1:
                            g.end(mm)
                g.close(N_EXP)

            for l in range(DEPTH):
                mixer(l)
                attention(l)
                if l == 0:
                    feed_forward()
            routing()
            passes[:] = [G, Groups(pe, banks, more_done, more_took, more_loads)]
            G.down_used, passes[1].down_used = down_used, more_down_used
            experts(0)
            G.given_moe = G.given["v"]
            pe.wait_ge(routing_ready, 1)
            with pe.If(pe.value_load(extra_flag[0:1, 0:1], min_val=0, max_val=1) > 0):
                for who in "va":
                    pe.wait_ge(took_sems[who], G.given[who])
                experts(1)
                for who in "va":
                    pe.wait_ge(more_took[who], passes[1].given[who])

            def mlstm():
                norm_sums("final_ms")
                norm_sums("norm1_ms")
                pe.wait_ge(x_ready, seen.next("x"))
                x = lambda k: xF[:, k, :]
                slot = G.tile()
                bank = G.begin("v", "gates")
                w = ring[:, slot, 0:KT * 16].rearrange("p (k n) -> p k n", k=KT)
                for b in range(TB):
                    for k in range(KT):
                        mm = pe.matmul(bank[:, 16 * b:16 * b + 16], xF[:, k, b * P:(b + 1) * P], w[:, k, :],
                                       start=(k == 0), stop=(k == KT - 1))
                G.end(mm)
                G.free()
                linear("xm", "a", 2, x, KT)
                pe.wait_ge(gates_ready, 1)
                for g in range(2):
                    transposes("v", ("gate_rows", g), [(b * P, gate_cols[:, b, g, :]) for b in range(TB)])
                pe.wait_ge(xm_act, 1)
                for name, dst in (("qM", qM), ("kM", kM)):
                    slot = G.tile()
                    w = ring[:, slot, 0:8 * HD].rearrange("p (k n) -> p k n", k=8)
                    for h in range(HEADS):
                        bank = G.begin("a", (name, h))
                        for e in range(2):
                            for j in range(2):
                                mm = pe.matmul(bank[:, e * SEQ:(e + 1) * SEQ], w[:, 2 * h + j, e * P:(e + 1) * P],
                                               xm_conv[:, 2 * h + j, :], start=(j == 0), stop=(j == 1))
                        G.end(mm)
                    G.free()
                slot = G.tile()
                w = ring[:, slot, 0:8 * HD].rearrange("p (k n) -> p k n", k=8)
                for b in range(TB):
                    for hp in range(2):
                        bank = G.begin("v", ("vL", b, hp))
                        for i in range(2):
                            h = 2 * hp + i
                            for j in range(2):
                                mm = pe.matmul(bank[:, i * HD:(i + 1) * HD], xm_pad[:, 2 * h + j, 2 + b * P:2 + (b + 1) * P],
                                               w[:, 2 * h + j, :], start=(j == 0), stop=(j == 1))
                        G.end(mm)
                G.free()
                linear("o_pre", "a", 2, x, KT)
                pe.wait_ge(a_ready, 1)
                transposes("v", "a_cols", [(64 * b, g_a[:, b * P:(b + 1) * P]) for b in range(TB)])

                def scores(h):
                    pe.wait_ge(act_took, G.took["kM", HEADS - 1])
                    bank = G.begin("a", ("scoresT", h))
                    for sblk in range(2):
                        for j in range(2):
                            mm = pe.matmul(bank[:, sblk * SEQ:(sblk + 1) * SEQ], kM[:, 2 * h + j, sblk * P:(sblk + 1) * P],
                                           qM[:, 2 * h + j, :], start=(j == 0), stop=(j == 1))
                    G.end(mm)

                def maxima(i):
                    h, d = divmod(i, 2)
                    bank = G.begin("a", ("maxima", i))
                    s = head_sel[0:64, 4 * d + h, :]
                    pe.matmul(bank[:, 0:SEQ], s, g_max, start=True, stop=True)
                    G.end(pe.matmul(bank[:, SEQ:2 * SEQ], s, g_sum, start=True, stop=True))

                pe.wait_ge(sel_ready, 1)
                pe.wait_ge(dve_took, G.took["vL", TB - 1, 1])
                scores(0)
                maxima(0)
                for i in range(2 * HEADS):
                    h, d = divmod(i, 2)
                    if i + 1 < 2 * HEADS:
                        if d == 1:
                            scores(h + 1)
                        maxima(i + 1)
                    pe.wait_ge(intra_ready, i + 1)
                    reach = ((0, 0, 2), (1, 1, 2)) if d == 0 else ((1, 0, 2), (0, 0, 1))
                    bank = G.begin("v", ("den", i))
                    for n_, (sblk, lo, hi) in enumerate(reach):
                        mm = pe.matmul(bank[:, lo * P:hi * P], ones[:, :], intra[:, sblk, lo:hi, :], start=(n_ == 0), stop=(n_ == 1))
                    G.end(mm)
                    bank = G.begin("v", ("num", i))
                    for e in range(2):
                        for n_, (sblk, lo, hi) in enumerate(reach):
                            mm = pe.matmul(bank[:, e * SEQ + lo * P:e * SEQ + hi * P], vL[:, sblk, h * HD + e * P:h * HD + (e + 1) * P],
                                           intra[:, sblk, lo:hi, :], start=(n_ == 0), stop=(n_ == 1))
                    G.end(mm)
                linear("merge_m", "a", 2, x, KT)
                pe.wait_ge(sq_ready, seen.next("sq"))
                for g in range(2):
                    bank = G.begin("a", ("head_ms", g))
                    for i in range(2):
                        for j in range(2):
                            mm = pe.matmul(bank[:, i * SEQ:(i + 1) * SEQ], ones[:, :], squares[:, 4 * g + 2 * i + j, :],
                                           start=(j == 0), stop=(j == 1))
                    G.end(mm)

            def lru():
                x = lambda k: xF[:, k, :]
                linear("xl", "a", 2, x, KT)
                pe.wait_ge(ym_ready, 1)
                linear("branch_m", "v", 2, lambda k: hM[:, k, :], KT)
                linear("gate_l", "a", 2, x, KT)
                wr, wi = G.tile(), G.tile()
                pe.wait_ge(xl_conv_ready, 1)
                for d in range(2):
                    for name, slot in (("r", wr), ("i", wi)):
                        w = ring[:, slot, 0:16 * P].rearrange("p (k n) -> p k n", k=16)
                        for g in range(4):
                            bank = G.begin("a", (name, d, g))
                            for i in range(2):
                                mm = pe.matmul(bank[:, i * SEQ:(i + 1) * SEQ], w[:, 8 * d + 2 * g + i, :], xl_conv[:, 2 * g + i, :],
                                               start=True, stop=True)
                            G.end(mm)
                        if d == 1:
                            G.free()
                G.freed[-2] = G.freed[-1]

            def merge():
                x = lambda k: xF[:, k, :]
                linear("merge_l", "a", 2, x, KT)
                pe.wait_ge(yl_ready, 1)
                linear("branch_l", "v", 2, lambda k: h_l[:, k, :], KT)
                pe.wait_ge(merged_ready, 4)
                linear("w_out", "v", 2, lambda k: merged[:, k, :], KT)

            def peer():
                norm_sums("norm2_ms")
                pe.wait_ge(x_ready, seen.next("x"))
                linear("pq", "a", 4, lambda k: xF[:, k, :], KT)
                slot = G.tile()
                keys = ring[:, slot, 0:16 * P].rearrange("p (k c) -> p k c", k=16)
                for g in range(4):
                    transposes("v", ("keysT", g), [(i * P, keys[:, 4 * g + i, :]) for i in range(4)])
                G.free()
                pe.wait_ge(act_took, G.took["pq", 7])
                pe.wait_ge(dve_took, G.took["keysT", 3])
                for b in range(TB):
                    for g in range(4):
                        bank = G.begin("a", ("key_scores", b, g))
                        for i in range(4):
                            mm = pe.matmul(bank[:, i * P:(i + 1) * P], qP[:, 4 * g + i, b * P:(b + 1) * P], keysT[:, 4 * g + i, :],
                                           start=True, stop=True)
                        G.end(mm)
                for b in range(TB):
                    for half in range(2):
                        transposes("v", ("tokens", b, half), [(i * P, xF[:, 4 * half + i, b * P:(b + 1) * P]) for i in range(4)])
                pe.wait_ge(zero_ready, 1)
                for b in range(TB):
                    halves = [G.begin("a", ("out", b, half)) for half in range(2)]
                    for k in range(KT):
                        pe.matmul(halves[k // 4][:, (k % 4) * P:(k % 4 + 1) * P], hF[:, k, b * P:(b + 1) * P], ident[:, :],
                                  start=(k % 4 == 0), stop=False)
                    with pe.Fori(b * ROUNDS, (b + 1) * ROUNDS) as r:
                        for q in range(BATCHES):
                            pe.wait_ge(diag_ready, r * BATCHES + q + 1)
                            pe.wait_ge(gathered[q], r * 16 * BATCH + 16 * BATCH * (TB * ROUNDS + 1))
                            for j in range(BATCH):
                                for half in range(2):
                                    mm = pe.matmul(halves[half], diag[:, q, j, :],
                                                   gathered_rows[:, q * BATCH + j, half * 512:(half + 1) * 512], start=False, stop=False)
                            mm.then_inc(mix_done, 1)
                    for half in range(2):
                        G.end(pe.matmul(halves[half], ones[0:1, :], zero_row, start=False, stop=True))

            mlstm()
            lru()
            merge()
            peer()

        @block.sync
        def _(sp):
            n = 0

            def load(*parts):
                nonlocal n
                slot = n % RING
                if n >= RING:
                    sp.wait_ge(*G.freed[n - RING][0:2])
                for place, src in parts:
                    sp.dma_start(place(ring[:, slot, :]), src).then_inc(loads[slot], 16)
                n += 1

            def by_rows(w, kts=KT):
                return w.rearrange("(k p) n -> p k n", p=P)

            def block_of(kts, n, off=0):
                return lambda s: s[:, off:off + kts * n].rearrange("p (k n) -> p k n", k=kts)

            def matrix(w, cols_n=512):
                for c in range(0, w.shape[1], cols_n):
                    load((block_of(KT, cols_n), by_rows(w[:, c:c + cols_n])))

            for l in range(DEPTH):
                w = t["w_in"][l]
                b0 = 2 * A_W
                for first, width in ((A_W, A_W), (0, A_W), (b0 + BC_W, BC_W), (b0 + 2 * BC_W, BC_W), (b0, BC_W),
                                     (b0 + 4 * BC_W, BC_W), (b0 + 3 * BC_W, BC_W)):
                    load((block_of(KT, width), by_rows(w[:, first:first + width])))
                w = t["w_mix_out"][l]
                for c in range(2):
                    s = slice(c * 512, (c + 1) * 512)

                    def at(a, b, lo=0, hi=P):
                        return lambda s_: s_[lo:hi, a * 512:b * 512].rearrange("p (k n) -> p k n", k=b - a)
                    load((at(0, 5), by_rows(w[0:640, s])), (at(5, 6, 0, 64), w[640:704, s].rearrange("(k p) n -> p k n", k=1)),
                         (at(5, 6, 64, P), w[960:1024, s].rearrange("(k p) n -> p k n", k=1)), (at(6, 8), by_rows(w[704:960, s])))
                matrix(t["w_xkv"][l])
                matrix(t["w_xq"][l])
                matrix(t["w_xo"][l])
                if l == 0:
                    for c in range(FT // 2):
                        s = slice(c * 256, (c + 1) * 256)
                        load((block_of(KT, 256), by_rows(t["ffn_w_gate"][0][:, s])),
                             (block_of(KT, 256, SLOT_F // 2), by_rows(t["ffn_w_up"][0][:, s])))
                    for c in range(KT):
                        load((block_of(FT, P), by_rows(t["ffn_w_down"][0][:, c * P:(c + 1) * P])))
            def expert_tiles(g, e, first, last):
                gate, up = (t[n][0].rearrange("e (k p) n -> p (e k) n", p=P) for n in ("moe_w_gate", "moe_w_up"))
                down = t["moe_w_down"][0].rearrange("e (k p) n -> p (e k) n", p=P)
                base = g.tile0
                for j in range(first, last):
                    slot = (base + j) % RING
                    if j >= RING:
                        used, count, per = g.freed[base + j - RING]
                        sp.wait_ge(used, count + e * per)
                    elif not isinstance(e, int):
                        used, count, per = g.freed[base + j + EXP_TILES - RING]
                        sp.wait_ge(used, count + (e - 1) * per)
                    else:
                        sp.wait_ge(*(G.freed_before if g is G else G.freed_last)[j][0:2])
                    if j < 2 * CHUNKS:
                        c = j // 2
                        src = (gate, up)[j % 2][:, bass.ds(e * KT, KT), c * 512:(c + 1) * 512]
                        dst = block_of(KT, 512)
                    else:
                        src = down[:, bass.ds(e * ET + 4 * (j - 2 * CHUNKS), 4), :]
                        dst = block_of(4, D)
                    sp.dma_start(dst(ring[:, slot, :]), src).then_inc(g.loads[slot], 16)

            def experts(g):
                expert_tiles(g, 0, 0, RING)
                with sp.Fori(0, N_EXP - 1) as e:
                    expert_tiles(g, e, RING, EXP_TILES)
                    expert_tiles(g, e + 1, 0, RING)
                expert_tiles(g, N_EXP - 1, RING, EXP_TILES)

            tile0 = n
            G.tile0 = tile0
            G.freed_before = G.freed[tile0 - RING:tile0]
            last0 = tile0 + EXP_TILES - RING
            G.freed_last = [(u, c + (N_EXP - 1) * per, 0) for u, c, per in G.freed[last0:last0 + RING]]
            experts(G)
            for j in range(RING):
                G.freed[last0 + j] = G.freed_last[j]
            n += EXP_TILES
            more = passes[1]
            more.tile0 = 0
            sp.wait_ge(routing_ready, 1)
            with sp.If(sp.value_load(extra_flag[0:1, 0:1], min_val=0, max_val=1) > 0):
                for j in range(RING):
                    sp.wait_ge(*G.freed_last[j][0:2])
                experts(more)
                sp.wait_ge(more_done, more.total)
            n0 = 2 * D
            w = t["w_in_2"][0]
            load((block_of(KT, 16), by_rows(w[:, n0:n0 + 16])))
            matrix(w[:, 0:D])
            for name in ("q", "k", "v"):
                load((block_of(8, HD), t["mlstm_w_" + name + "_2"][0].rearrange("h (j p) e -> p (h j) e", p=P)))
            matrix(w[:, D:2 * D])
            matrix(w[:, n0 + 16 + 2 * D:n0 + 16 + 3 * D])
            matrix(w[:, n0 + 16:n0 + 16 + D])
            matrix(t["w_branch_mlstm_2"][0])
            matrix(w[:, n0 + 16 + D:n0 + 16 + 2 * D])
            for name in ("r", "i"):
                load((block_of(16, P), t["lru_w_" + name + "_2"][0].rearrange("s n c d -> c (s n) d")))
            matrix(w[:, n0 + 16 + 3 * D:n0 + 16 + 4 * D])
            matrix(t["w_branch_lru_2"][0])
            matrix(t["w_out_2"][0])
            matrix(t["peer_w_q_2"][0])
            load((block_of(16, P), t["peer_sub_keys_2"][0].rearrange("h s n c -> n (h s) c")))
            sp.wait_ge(x_ready, N_NORMS + 1)
            sp.dma_start(final_gain, t["final_norm_g_2"].partition_broadcast(P)).then_inc(gain_loaded, 16)
            for b in range(TB):
                sp.wait_ge(final_out, b + 1)
                sp.dma_start(out[0, b * P:(b + 1) * P, :], final_rows[:, b, :]).then_inc(out_done, 16)
            sp.wait_ge(out_done, 16 * TB)

        @block.gpsimd
        def _(pool):
            step = Steps(pool, pool_step)
            step.then(pool.memset(ident[:, :], 0.0))
            step.then(pool.memset(tri[:, :], 1.0))
            step.then(pool.memset(lower[:, :], 1.0))
            step.then(pool.memset(half_ones[:, :], 0.0))
            step.then(pool.memset(pair_sel[:, :, :], 1.0))
            pool.memset(ones[:, :], 1.0)
            pool.memset(eps[:, :], EPS)
            pool.iota(iota[:, :], [[1, P]], base=0, channel_multiplier=0, allow_small_or_imprecise_dtypes=True)
            step.settle()
            pool.affine_select(out=ident[:, :], in_=ident[:, :], compare_op=ALU.not_equal, fill=1.0, base=0,
                               pattern=[[-1, P]], channel_multiplier=1)
            step.now(pool.affine_select(out=tri[:, :], in_=tri[:, :], compare_op=ALU.is_ge, fill=0.0, base=0,
                                        pattern=[[1, P]], channel_multiplier=-1))
            step.now(pool.affine_select(out=lower[:, :], in_=lower[:, :], compare_op=ALU.is_ge, fill=0.0, base=0,
                                        pattern=[[-1, P]], channel_multiplier=1))
            step.now(pool.memset(half_ones[0:64, 0:64], 1.0))
            step.now(pool.memset(half_ones[64:P, 64:P], 1.0))
            for lo, hi, base in ((0, 2, 0), (2, 3, BC_W - P)):
                s = pair_sel[:, lo:hi, :]
                step.now(pool.affine_select(out=s, in_=s, compare_op=ALU.is_ge, fill=0.0, base=base,
                                            pattern=[[P, hi - lo], [1, P]], channel_multiplier=-64))
                step.now(pool.affine_select(out=s, in_=s, compare_op=ALU.is_ge, fill=0.0, base=63 - base,
                                            pattern=[[-P, hi - lo], [-1, P]], channel_multiplier=64))
            pool.memset(small[:, 0:1], 0.0).then_inc(consts_ready, 1)
            pool.wait_ge(x_ready, N_NORMS)
            s = head_sel[0:64, :, :]
            step.now(pool.memset(s, 0.0))
            pool.affine_select(out=s, in_=s, compare_op=ALU.not_equal, fill=1.0, base=0,
                               pattern=[[-32, 2], [-1, 4], [0, P]], channel_multiplier=1).then_inc(sel_ready, 1)

            def rounds(table, n):
                rows_ = t[table][0]

                def round_(r, after):
                    for q in range(BATCHES):
                        after(q)
                        pool.tensor_copy(stage[:, q * BATCH:(q + 1) * BATCH], rows_at[:, bass.ds(r * GATHER + q * BATCH, BATCH)]
                                         ).then_inc(staged, 1)
                        pool.wait_ge(staged, r * BATCHES + TB * ROUNDS * BATCHES * n + q + 1)
                        pool.sem_inc(pool_turn, 1)
                        for j in range(q * BATCH, (q + 1) * BATCH):
                            pool.indirect_dma_start(out=gathered_rows[:, j, :], out_offset=None, in_=rows_,
                                                    in_offset=bass.IndirectOffsetOnAxis(ap=stage[:, j:j + 1], axis=0)
                                                    ).then_inc(gathered[q], 16)

                def later(r):
                    def after(q):
                        pool.wait_ge((dot_done, mix_done)[n], (r - 1) * BATCHES + q + 1)
                        pool.sem_inc(pool_turn, 1)
                    return after

                def first(q):
                    if n:
                        pool.wait_ge(dot_done, (TB * ROUNDS - 1) * BATCHES + q + 1)

                for b in range(TB):
                    pool.wait_ge(index_ready, b + 1)
                    if b == 0:
                        round_(0, first)
                    with pool.Fori(max(b * ROUNDS, 1), (b + 1) * ROUNDS) as r:
                        round_(r, later(r))

            pool.wait_ge(group_done, G.after["keysT", 3])
            rounds("peer_u_2", 0)
            rounds("peer_v_2", 1)

        @block.scalar
        def _(act):
            seen = Tally()
            step = Steps(act, act_step)

            def ready(key):
                act.wait_ge(group_done, G.after[key])

            def take(ins):
                ins.then_inc(act_took, 1)

            act.dma_start(x_in, t["x"].rearrange("o (b p) d -> p (o b) d", p=P)).then_inc(inputs_loaded, 16)
            act.dma_start(mem_in, t["mem"].rearrange("o (b p) d -> p (o b) d", p=P)).then_inc(inputs_loaded, 16)
            sent = 0

            def param(dst, src):
                nonlocal sent
                act.dma_start(dst, src).then_inc(params_loaded, 16)
                sent += 1

            def vec(r, set_, src):
                n = src.shape[0] // P
                param(rows[r:r + n, set_, :], src.rearrange("(k c) -> k c", c=P))

            for l in range(DEPTH):
                r = 49 * l
                vec(r + MIX_G, 0, t["norm_mix_g"][l])
                vec(r + X_G, 0, t["norm_x_g"][l])
                vec(r + MEM_G, 0, t["norm_mem_g"][l])
                vec(r + FFN_G, 0, t["norm_ffn_g"][l])
                g = t["mix_out_g"][l]
                vec(r + OUT_G, 0, g[0:640])
                param(rows[r + OUT_G + 5:r + OUT_G + 6, 0, 0:64], g[640:704].rearrange("(k c) -> k c", k=1))
                param(rows[r + OUT_G + 5:r + OUT_G + 6, 0, 64:P], g[960:1024].rearrange("(k c) -> k c", k=1))
                vec(r + OUT_G + 6, 0, g[704:960])
                vec(r + CONVA_B, 0, t["conv_a_b"][l])
                vec(r + LNA_G, 0, t["ln_a_g"][l])
                vec(r + LNA_B, 0, t["ln_a_b"][l])
                param(rows[0:93, 1 + l, :], t["conv_a_w"][l].rearrange("j (k c) -> (j k) c", c=P))
                param(bc_rows[5 * l:5 * l + 3, :], t["conv_b_w"][l])
                param(bc_rows[5 * l + 3:5 * l + 4, :], t["ln_c_g"][l].rearrange("(k c) -> k c", k=1))
                param(bc_rows[5 * l + 4:5 * l + 5, :], t["ln_c_b"][l].rearrange("(k c) -> k c", k=1))
                param(gate_bias[:, l, :], t["gmlp_b"][l])
                param(spatial_in[:, l, :, :], t["gmlp_ws"][l].rearrange("g i j -> i g j"))
            for r, name in ((N1_G, "norm1_g_2"), (MC_B, "mlstm_conv_b_2"), (MN_G, "mlstm_norm_g_2"), (LC_B, "lru_conv_b_2"),
                            (N2_G, "norm2_g_2")):
                vec(r, 3, t[name][0])
            for r, name in ((BR, "lru_b_r_2"), (BI, "lru_b_i_2"), (LAM, "lru_lambda_2")):
                param(rows[r:r + 16, 3, :], t[name][0].rearrange("s (k c) -> (s k) c", c=P))
            param(rows[MC_W:MC_W + 32, 3, :], t["mlstm_conv_w_2"][0].rearrange("j (k c) -> (j k) c", c=P))
            param(rows[LC_W:LC_W + 32, 4, :], t["lru_conv_w_2"][0].rearrange("j (k c) -> (j k) c", c=P))
            vec(FIN_G, 4, t["norm_final_g"])
            param(router[:, :, :], t["moe_router"][0].rearrange("(k p) e -> p k e", p=P))
            param(gate_row, t["b_gates_2"][0].partition_broadcast(P))
            assert sent == N_PARAMS, sent

            def square(src, n=KT):
                act.activation(squares[:, 0:n, :], src, ACT.Square).then_inc(sq_ready, 1)

            def std(key, n, rows_=P):
                ready(key)
                take(act.activation(std_row[:, :], banks_of(key)[:, 0:SEQ], ACT.Sqrt, bias=EPS_AP, scale=1.0 / n))

            def banks_of(key):
                return banks["a"][(G.took[key] - 1) % 4]

            def norm(key, h_taken):
                act.wait_ge(dve_took, h_taken)
                square(hF[:, :, :])
                std(key, D)

            for g in range(4):
                ready(("mem", g))
                take(act.activation(mem_hat[:, 2 * g:2 * g + 2, :], pair(banks_of(("mem", g))), ACT.Copy))
            for l in range(DEPTH):
                ready(("spatial", l, 0))
                take(act.activation(spatialT[:, l, 0:4, :], pair(banks_of(("spatial", l, 0)), 4, P), ACT.Copy))
            ready("spatial_last")
            take(act.activation(spatialT[:, :, 4, :], pair(banks_of("spatial_last"), DEPTH, P), ACT.Copy))
            act.wait_ge(act_took, G.took["mem", 3])
            square(mem_hat)
            std("mem_ms", D)
            act.wait_ge(mem_normed, 1)

            def mixer(l):
                norm(("mix_ms", l), G.took["cols"] if l == 0 else G.took["ffn_down", 3])

                def section(name, dst, func, ms, lo=0):
                    for g in range(2):
                        ready((name, l, g))
                        bank = banks_of((name, l, g))
                        if g == 0:
                            take(act.activation(dst[:, 0:2, :], pair(bank), func))
                        else:
                            take(act.activation(dst[lo:ms, 2, :], bank[lo:ms, 0:SEQ], func))

                section("a_gate", sig_a, ACT.Sigmoid, P)
                section("c_gate", c_gate, ACT.Copy, 64)
                section("b_gate", b_gate, ACT.Copy, 64)
                section("c_v", c_v, ACT.Gelu_apprx_tanh, 64)
                section("c_u", c_u, ACT.Gelu_apprx_tanh, P, 64)

                def layer_norm(name, n, src, last64):
                    ready((name + "_mean", l))
                    take(act.activation(mean_row[:, :], banks_of((name + "_mean", l))[:, 0:SEQ], ACT.Copy, scale=-1.0 / n))
                    act.wait_ge(centred, seen.next("centred"))
                    if last64:
                        step.then(act.activation(squares[:, 0:2, :], src[:, 0:2, :], ACT.Square))
                        act.activation(squares[0:64, 2, :], src[0:64, 2, :], ACT.Square).then_inc(sq_ready, 1)
                    else:
                        square(src, 3)
                    std((name + "_var", l), n)

                layer_norm("c", BC_W, c_v, True)
                layer_norm("a", A_W, conv_a, False)
                act.wait_ge(ln_ready, l + 1)
                for k in range(3):
                    ins = act.activation(yF[:, k, :], conv_a[:, k, :], ACT.Silu, scale=c_vec(l, LNA_G, k), bias=c_vec(l, LNA_B, k))
                ins.then_inc(ya_ready, 1)
                act.wait_ge(ya_ready, l + 1)
                act.wait_ge(y_all, l + 1)
                square(yF)
                for g in range(4):
                    ready(("group_ms", l, g))
                    take(act.activation(std8[:, 2 * g:2 * g + 2, :], pair(banks_of(("group_ms", l, g))), ACT.Sqrt,
                                        bias=EPS_AP, scale=1.0 / 64))

            def copies(key, dst, n=4, func=ACT.Copy, scale=1.0):
                for g in range(n):
                    ready((key, g))
                    take(act.activation(dst[:, 2 * g:2 * g + 2, :], pair(banks_of((key, g))), func, scale=scale))

            def attention(l):
                copies(("k", l), kF)
                for half in range(2):
                    for b in range(TB):
                        ready(("v", l, half, b))
                        take(act.activation(vM[:, b, half * 512:(half + 1) * 512], banks_of(("v", l, half, b))[:, :], ACT.Copy))
                norm(("x_ms", l), G.took[("mix_out", l), 3])
                copies(("q", l), qF)
                for h in range(HEADS):
                    act.wait_ge(max_ready, HEADS * l + h + 1)
                    bank = banks_of(("scores", l, h))
                    for b in range(TB):
                        c = h * TB + b
                        ins = act.activation(probs[:, h, b, :], bank[:, b * SEQ:(b + 1) * SEQ], ACT.Exp, bias=small[:, c:c + 1],
                                             scale=HD ** -0.5, accum_out=small[:, 8 + c:9 + c])
                    take(ins)
                for h in range(HEADS):
                    ready(("o", l, h))
                    take(act.activation(oF[:, 2 * h:2 * h + 2, :], pair(banks_of(("o", l, h))), ACT.Copy))

            def feed_forward():
                norm("ffn_ms", G.took[("xo", 0), 3])
                for c in range(FT // 2):
                    ready(("ffn", 0, c))
                    if c >= 2:
                        act.wait_ge(dve_took, G.took["ffn", 1, c - 2])
                    take(act.activation(sil[:, c % 2, :, :], pair(banks_of(("ffn", 0, c))), ACT.Silu))

            def routing():
                norm("moe_ms", G.took[("xo", 1), 3])
                for b in range(TB):
                    for half in range(2):
                        ready(("xT", b, half))
                        take(act.activation(xT[:, b, half * 512:(half + 1) * 512], banks_of(("xT", b, half))[:, :], ACT.Copy))
                act.wait_ge(gap_ready, 1)
                act.activation(ratio, gap, ACT.Exp).then_inc(ratio_ready, 1)

            def experts(n):
                g = passes[n]

                def bank_in(key):
                    return banks["a"][(g.took[key] - 1) % 4]

                def took_it(ins):
                    ins.then_inc(g.took_sems["a"], 1)

                for e in range(4, N_EXP):
                    act.wait_ge(g.group_done, g.after["put", e])
                    took_it(act.activation(put[:, e, :], bank_in(("put", e))[:, 0:SEQ], ACT.Copy))
                with act.Fori(0, N_EXP) as e:
                    def done(key):
                        act.wait_ge(g.group_done, g.after[key] + e * EXP_GROUPS)

                    def hidden(c):
                        done(("hidden", c))
                        took_it(act.activation(heT[:, 4 * c:4 * c + 4, :], pair(bank_in(("hidden", c)), 4, P), ACT.Copy))

                    for c in range(CHUNKS):
                        done(("gate", c))
                        took_it(act.activation(he[:, c * 512:(c + 1) * 512], bank_in(("gate", c))[:, :], ACT.Silu))
                        if c >= 1:
                            hidden(c - 1)
                    hidden(CHUNKS - 1)
                    for h in range(2):
                        done(("down", h))
                        took_it(act.activation(ye[:, h * 512:(h + 1) * 512], bank_in(("down", h))[:, :], ACT.Copy))

            for l in range(DEPTH):
                mixer(l)
                attention(l)
                if l == 0:
                    feed_forward()
            routing()
            experts(0)
            act.wait_ge(routing_ready, 1)
            with act.If(act.value_load(extra_flag[0:1, 0:1], min_val=0, max_val=1) > 0):
                experts(1)
                act.wait_ge(more_took["v"], passes[1].given["v"])

            def mlstm():
                norm("final_ms", G.given_moe)
                act.wait_ge(final_ready, 1)
                square(hF[:, :, :])
                std("norm1_ms", D)
                act.wait_ge(abs_ready, 1)
                act.activation(lam_t, lam_t, ACT.Exp, scale=-1.0).then_inc(exp_done, 1)
                for g in range(4):
                    ready(("xm", g))
                    take(act.activation(xm_pad[:, 2 * g:2 * g + 2, 2:2 + SEQ], pair(banks_of(("xm", g))), ACT.Copy))
                act.wait_ge(abs_ready, 2)
                act.activation(g_t, g_t, ACT.Exp, scale=-1.0).then_inc(exp_done, 1)
                act.wait_ge(xm_conv_ready, 1)
                act.activation(xm_conv, xm_conv, ACT.Silu).then_inc(xm_act, 1)
                for name, dst, scale in (("qM", qM, 1.0), ("kM", kM, HD ** -0.5)):
                    copies(name, dst, scale=scale)
                copies("o_pre", o_sig, func=ACT.Sigmoid)

                def scores(h):
                    ready(("scoresT", h))
                    take(act.activation(scoresT[:, h % 2, :, :, :].rearrange("p s t j -> p (s t j)"),
                                        banks_of(("scoresT", h))[:, :], ACT.Copy))

                def maxima(i):
                    act.wait_ge(arg_ready, i + 1)
                    for sblk, lo, hi in (((0, 0, 2), (1, 1, 2)) if i % 2 == 0 else ((1, 0, 2), (0, 0, 1))):
                        a = decay[:, sblk, lo:hi, :]
                        act.activation(a, a, ACT.Exp, scale=-1.0)
                    take(act.activation(floor_[:, i % 2, :], banks_of(("maxima", i))[:, SEQ:2 * SEQ], ACT.Exp, scale=-1.0))

                scores(0)
                maxima(0)
                for i in range(2 * HEADS - 1):
                    if i % 2 == 1:
                        scores(i // 2 + 1)
                    maxima(i + 1)
                copies("merge_m", g_m, func=ACT.Sigmoid)
                act.wait_ge(h_sum_ready, 1)
                square(hM)
                for g in range(2):
                    ready(("head_ms", g))
                    take(act.activation(std4[:, 2 * g:2 * g + 2, :], pair(banks_of(("head_ms", g))), ACT.Sqrt, bias=EPS_AP, scale=1.0 / HD))

            def lru():
                for g in range(4):
                    ready(("xl", g))
                    take(act.activation(xl_pad[:, 2 * g:2 * g + 2, 2:2 + SEQ], pair(banks_of(("xl", g))), ACT.Copy))
                act.wait_ge(dve_took, G.took["branch_m", 3])
                copies("gate_l", gate_l, func=ACT.Gelu)
                for d in range(2):
                    act.wait_ge(lru_free, d + 1)
                    for name, dst, bias in (("r", lru_a, BR), ("i", lru_u, BI)):
                        for g in range(4):
                            ready((name, d, g))
                            for i in range(2):
                                k = 2 * g + i
                                ins = act.activation(dst[:, k, :], banks_of((name, d, g))[:, i * SEQ:(i + 1) * SEQ], ACT.Sigmoid,
                                                     bias=col(C2 + bias + 8 * d + k))
                            take(ins)
                    act.wait_ge(lam_ready, 1)
                    act.wait_ge(act_took, G.took["r", d, 3])
                    for k in range(KT):
                        step.then(act.activation(lru_t[:, k, :], lru_a[:, k, :], ACT.Tanh, scale=lam_pos[:, 8 * d + k:8 * d + k + 1]))
                    step.settle()
                    for k in range(KT):
                        ins = act.activation(lru_a[:, k, :], lru_a[:, k, :], ACT.Exp, scale=lam_neg[:, 8 * d + k:8 * d + k + 1])
                    ins.then_inc(lru_a_ready, 1)
                    act.wait_ge(lru_v_ready, d + 1)
                    act.activation(lru_t[:, :, :], lru_t[:, :, :], ACT.Sqrt).then_inc(lru_s_ready, 1)

            def merge():
                act.wait_ge(gated_ready, 2)
                copies("merge_l", g_l, func=ACT.Sigmoid)

            def peer():
                norm("norm2_ms", G.took["w_out", 3])
                copies("pq", qP, 8)
                for b in range(TB):
                    if b:
                        act.wait_ge(index_ready, b)
                    for g in range(4):
                        ready(("key_scores", b, g))
                        take(act.activation(key_scores[:, 4 * g:4 * g + 4, :], pair(banks_of(("key_scores", b, g)), 4, P), ACT.Copy))
                    act.wait_ge(margin_ready, b + 1)
                    act.activation(gates[:, b, :, :], gates[:, b, :, :], ACT.Exp).then_inc(margin_exp, 1)
                for b in range(TB):
                    act.wait_ge(dots_kept, (b + 1) * ROUNDS)
                    s = acts[:, b * SLOTS:(b + 1) * SLOTS]
                    act.activation(s, s, ACT.Gelu).then_inc(act_ready, 1)
                for b in range(TB):
                    ready(("out", b, 1))
                    n = 4 + (G.took["out", b, 0] - 1) % 4
                    step.now(act.activation(final_sq, psum_all[:, n:n + 2, :].rearrange("p h d -> p (h d)"), ACT.Square,
                                            accum_out=final_ss[:, b:b + 1]))
                    act.activation(final_std[:, b:b + 1], final_ss[:, b:b + 1], ACT.Sqrt, bias=EPS_AP, scale=1.0 / D).then_inc(final_std_ready, 1)

            mlstm()
            lru()
            merge()
            peer()

        @block.vector
        def _(dve):
            seen = Tally()
            step = Steps(dve, dve_step)

            def ready(key):
                dve.wait_ge(group_done, G.after[key])

            def bank_of(key):
                return banks["v"][(G.took[key] - 1) % 4]

            def take(ins):
                ins.then_inc(dve_took, 1)

            def scaled(dst, src, gain, sem_):
                step.now(dve.reciprocal(rstd_row[:, :], std_row[:, :]))
                for k in range(KT):
                    ins = dve.scalar_tensor_tensor(dst[:, k, :], src[:, k, :], gain(k), rstd_row[:, :], ALU.mult, ALU.mult)
                    if k < KT - 1:
                        step.then(ins)
                ins.then_inc(sem_, 1)

            def norm(key, gain):
                dve.wait_ge(act_took, G.took[key])
                scaled(xF, hF, gain, x_ready)

            def add_to_residual(key, n=4):
                for g in range(n):
                    ready((key, g))
                    s = hF[:, 2 * g:2 * g + 2, :]
                    take(dve.tensor_tensor(s, pair(bank_of((key, g))), s, ALU.add))

            def conv(dst, src, taps, weight, bias, tiles):
                for j in range(taps):
                    for k, m in tiles:
                        a = src(k, j)
                        if j == 0 and bias is not None:
                            ins = dve.tensor_scalar(dst[0:m, k, :], a, weight(k, j), bias(k), ALU.mult, ALU.add)
                        elif j == 0:
                            ins = dve.tensor_scalar(dst[0:m, k, :], a, weight(k, j), None, ALU.mult)
                        else:
                            step.settle(len(tiles) - 1)
                            ins = dve.scalar_tensor_tensor(dst[0:m, k, :], a, weight(k, j), dst[0:m, k, :], ALU.mult, ALU.add)
                        step.then(ins)
                step.settle()

            for g in range(4):
                ready(("x", g))
                take(dve.tensor_copy(hF[:, 2 * g:2 * g + 2, :], pair(bank_of(("x", g)))))
            ready("cols")
            step.then(dve.tensor_copy(cols[:, 0:C4 + 20], bank_of("cols")[:, 0:C4 + 20]))
            take(dve.tensor_copy(cols[0:64, C4 + 20:C4 + 30], bank_of("cols")[0:64, C4 + 20:C4 + 30]))
            dve.wait_ge(dve_took, G.took["cols"])
            dve.wait_ge(act_took, G.took["spatial_last"])
            dve.memset(spatialT[64:P, :, :, 0:64], 0.0).then_inc(mask_ready, 1)
            dve.wait_ge(act_took, G.took["mem_ms"])
            step.now(dve.reciprocal(rstd_row[:, :], std_row[:, :]))
            dve.tensor_tensor(mem_hat, mem_hat, rstd_row[:, :].unsqueeze(1).to_broadcast([P, KT, SEQ]), ALU.mult).then_inc(mem_normed, 1)

            def mixer(l):
                norm(("mix_ms", l), lambda k: c_vec(l, MIX_G, k))
                step.then(dve.memset(ya_pad[:, :, 0:A_TAPS - 1], 0.0))
                step.then(dve.memset(yb_pad[:, :, 0:B_TAPS - 1], 0.0))
                dve.wait_ge(act_took, G.took["a_gate", l, 1])
                ready(("a_val", l, 0))
                take(dve.tensor_tensor(ya_pad[:, 0:2, A_TAPS - 1:], pair(bank_of(("a_val", l, 0))), sig_a[:, 0:2, :], ALU.mult))
                ready(("a_val", l, 1))
                take(dve.tensor_tensor(ya_pad[:, 2, A_TAPS - 1:], bank_of(("a_val", l, 1))[:, 0:SEQ], sig_a[:, 2, :], ALU.mult))
                dve.wait_ge(dve_took, G.took["a_val", l, 1])
                step.settle()
                conv(conv_a, lambda k, j: ya_pad[:, k, j:j + SEQ], A_TAPS, lambda k, j: col(C1 + 93 * l + 3 * j + k),
                     lambda k: c_vec(l, CONVA_B, k), ((0, P), (1, P), (2, P)))
                dve.engine_nop().then_inc(conv_ready, 1)
                dve.wait_ge(act_took, G.took["c_gate", l, 1])
                ready(("b_in", l, 0))
                take(dve.tensor_tensor(yb_pad[:, 0:2, B_TAPS - 1:], pair(bank_of(("b_in", l, 0))), c_gate[:, 0:2, :], ALU.mult))
                ready(("b_in", l, 1))
                take(dve.tensor_tensor(yb_pad[0:64, 2, B_TAPS - 1:], bank_of(("b_in", l, 1))[0:64, 0:SEQ], c_gate[0:64, 2, :], ALU.mult))
                dve.wait_ge(dve_took, G.took["b_in", l, 1])
                tiles = ((0, P), (1, P), (2, 64))
                conv(conv_b, lambda k, j: yb_pad[0:(P if k < 2 else 64), k, j:j + SEQ], B_TAPS, lambda k, j: bc_col(l, j, k), None, tiles)
                dve.wait_ge(act_took, G.took["b_gate", l, 1])
                step.then(dve.tensor_tensor(yF[:, 3:5, :], b_gate[:, 0:2, :], conv_b[:, 0:2, :], ALU.mult))
                step.then(dve.tensor_tensor(yF[0:64, 5, :], b_gate[0:64, 2, :], conv_b[0:64, 2, :], ALU.mult))

                def wide(ap, n):
                    return ap.unsqueeze(1).to_broadcast([P, n, SEQ])

                dve.wait_ge(act_took, G.took["c_mean", l])
                step.then(dve.tensor_tensor(c_v[:, 0:2, :], c_v[:, 0:2, :], wide(mean_row[:, :], 2), ALU.add))
                dve.tensor_tensor(c_v[0:64, 2, :], c_v[0:64, 2, :], mean_row[0:64, :], ALU.add).then_inc(centred, 1)
                dve.wait_ge(act_took, G.took["c_var", l])
                dve.wait_ge(centred, seen.next("centred"))
                step.now(dve.reciprocal(rstd_row[:, :], std_row[:, :]))
                for k, m in tiles:
                    step.then(dve.scalar_tensor_tensor(c_v[0:m, k, :], c_v[0:m, k, :], bc_col(l, 3, k), rstd_row[0:m, :], ALU.mult, ALU.mult))
                step.settle()
                for k, m in tiles:
                    ins = dve.tensor_scalar(c_v[0:m, k, :], c_v[0:m, k, :], bc_col(l, 4, k), None, ALU.add)
                    if k < 2:
                        step.then(ins)
                ins.then_inc(cv_ready, 1)
                for b in range(TB):
                    ready(("c_vT", l, b))
                    take(dve.tensor_copy(vT[:, b, :], bank_of(("c_vT", l, b))[:, 0:BC_W]))
                dve.wait_ge(act_took, G.took["c_u", l, 1])
                for p in range(3):
                    for b in range(TB):
                        ready(("mixed", l, p, b))
                        bank = bank_of(("mixed", l, p, b))
                        s = slice(b * P, (b + 1) * P)
                        if p < 2:
                            step.then(dve.tensor_tensor(yF[0:64, 6 + p, s], bank[0:64, 0:P], c_u[0:64, p, s], ALU.mult))
                            take(dve.tensor_tensor(yF[64:P, 6 + p, s], bank[64:P, P:2 * P], c_u[64:P, p, s], ALU.mult))
                        else:
                            take(dve.tensor_tensor(yF[64:P, 5, s], bank[64:P, 0:P], c_u[64:P, 2, s], ALU.mult))
                dve.engine_nop().then_inc(y_all, 1)
                dve.wait_ge(act_took, G.took["a_mean", l])
                dve.tensor_tensor(conv_a, conv_a, wide(mean_row[:, :], 3), ALU.add).then_inc(centred, 1)
                dve.wait_ge(act_took, G.took["a_var", l])
                dve.wait_ge(centred, seen.next("centred"))
                step.now(dve.reciprocal(rstd_row[:, :], std_row[:, :]))
                dve.tensor_tensor(conv_a, conv_a, wide(rstd_row[:, :], 3), ALU.mult).then_inc(ln_ready, 1)
                dve.wait_ge(act_took, G.took["group_ms", l, 3])
                dve.wait_ge(ya_ready, l + 1)
                dve.wait_ge(dve_took, G.took["mixed", l, 2, 1])
                step.now(dve.reciprocal(std8, std8))
                for k in range(KT):
                    ins = dve.scalar_tensor_tensor(yF[:, k, :], yF[:, k, :], c_vec(l, OUT_G, k), std8[:, k, :], ALU.mult, ALU.mult)
                    if k < KT - 1:
                        step.then(ins)
                ins.then_inc(y_ready, 1)
                add_to_residual(("mix_out", l))

            def attention(l):
                dve.wait_ge(mem_normed, 1)
                for k in range(KT):
                    ins = dve.tensor_scalar(mem_g[:, k, :], mem_hat[:, k, :], c_vec(l, MEM_G, k), None, ALU.mult)
                    if k < KT - 1:
                        step.then(ins)
                ins.then_inc(mem_ready, 1)
                norm(("x_ms", l), lambda k: c_vec(l, X_G, k))
                for h in range(HEADS):
                    ready(("scores", l, h))
                    bank = banks["a"][(G.took["scores", l, h] - 1) % 4]
                    s = small[:, h * TB:(h + 1) * TB]
                    step.now(dve.tensor_reduce(s, pair(bank), AX.X, ALU.max))
                    dve.tensor_scalar(s, s, -(HD ** -0.5), None, ALU.mult).then_inc(max_ready, 1)
                for h in range(HEADS):
                    dve.wait_ge(act_took, G.took["scores", l, h])
                    r = small[:, 16 + h * TB:16 + (h + 1) * TB]
                    step.now(dve.reciprocal(r, small[:, 8 + h * TB:8 + (h + 1) * TB]))
                    for b in range(TB):
                        ins = dve.tensor_scalar(probs[:, h, b, :], probs[:, h, b, :], r[:, b:b + 1], None, ALU.mult)
                        if b < TB - 1:
                            step.then(ins)
                    ins.then_inc(probs_ready, 1)
                for h in range(HEADS):
                    ready(("probsT", l, h))
                    take(dve.tensor_copy(probsT[:, h, :, :], pair(bank_of(("probsT", l, h)))))
                add_to_residual(("xo", l))

            def feed_forward():
                norm("ffn_ms", lambda k: c_vec(0, FFN_G, k))
                for c in range(FT // 2):
                    ready(("ffn", 1, c))
                    dve.wait_ge(act_took, G.took["ffn", 0, c])
                    take(dve.tensor_tensor(hid[:, 2 * c:2 * c + 2, :], pair(bank_of(("ffn", 1, c))), sil[:, c % 2, :, :], ALU.mult))
                add_to_residual("ffn_down")

            def routing():
                norm("moe_ms", lambda k: c_vec(1, FFN_G, k))
                ready("logits")
                b8 = bank_of("logits")[:, 0:TB * N_EXP].rearrange("p (b e) -> p b e", b=TB)
                take(dve.tensor_copy(logits, b8))
                dve.wait_ge(dve_took, G.took["logits"])
                for b in range(TB):
                    step.then(dve.max(top[:, b, :], logits[:, b, :]))
                step.settle()
                for b in range(TB):
                    step.then(dve.max_index(top_raw[:, b, :], top[:, b, :], logits[:, b, :]))
                step.settle()
                step.then(dve.tensor_copy(top_at, top_raw))
                dve.tensor_tensor(gap, top[:, :, 1], top[:, :, 0], ALU.subtract).then_inc(gap_ready, 1)
                step.settle()
                for b in range(TB):
                    for i, m in ((0, first), (1, second)):
                        step.then(dve.tensor_scalar(m[:, b, :], iota[:, 0:N_EXP], top_at[:, b, i:i + 1], None, ALU.is_equal))
                step.settle()
                dve.tensor_tensor(chosen, first, second, ALU.add).then_inc(chosen_ready, 1)
                dve.wait_ge(ratio_ready, 1)
                step.now(dve.tensor_scalar(total_w, ratio, 1.0, None, ALU.add))
                step.now(dve.reciprocal(w_first, total_w))
                step.now(dve.tensor_tensor(w_second, w_first, ratio, ALU.mult))
                for b in range(TB):
                    step.now(dve.tensor_scalar(share[:, b, :], first[:, b, :], w_first[:, b:b + 1], None, ALU.mult))
                    step.now(dve.scalar_tensor_tensor(share[:, b, :], second[:, b, :], w_second[:, b:b + 1], share[:, b, :], ALU.mult, ALU.add))
                ready("places")
                dve.wait_ge(chosen_ready, 1)
                bank = bank_of("places")
                p8 = bank[:, 0:TB * N_EXP].rearrange("p (b e) -> p b e", b=TB)
                step.now(dve.tensor_tensor(place, p8, chosen, ALU.mult))
                step.then(dve.tensor_scalar(place, place, -1.0, None, ALU.add))
                step.now(dve.tensor_reduce(most, bank[:, 2 * N_EXP:3 * N_EXP], AX.X, ALU.max))
                take(dve.tensor_scalar(extra_flag[:, 0:1], most, float(P), None, ALU.is_gt))
                dve.wait_ge(dve_took, G.took["places"])
                dve.engine_nop().then_inc(routing_ready, 1)

            def experts(n):
                g = passes[n]

                def bank_in(key):
                    return banks["v"][(g.took[key] - 1) % 4]

                def took_it(ins):
                    ins.then_inc(g.took_sems["v"], 1)

                if n:
                    dve.tensor_scalar(place, place, -float(P), None, ALU.add).then_inc(more_places, 1)
                    dve.wait_ge(more_places, 1)
                for scale, dst, sem_ in ((True, weighted, weighted_ready), (False, pick, pick_ready)):
                    for b in range(TB):
                        for e in range(N_EXP):
                            if scale:
                                ins = dve.tensor_scalar(dst[:, b, e, :], iota[:, :], place[:, b, e:e + 1], share[:, b, e:e + 1],
                                                        ALU.is_equal, ALU.mult)
                            else:
                                ins = dve.tensor_scalar(dst[:, b, e, :], iota[:, :], place[:, b, e:e + 1], None, ALU.is_equal)
                    ins.then_inc(sem_, 1)
                for e in range(4):
                    dve.wait_ge(g.group_done, g.after["put", e])
                    took_it(dve.tensor_copy(put[:, e, :], bank_in(("put", e))[:, 0:SEQ]))
                with dve.Fori(0, N_EXP) as e:
                    def done(key):
                        dve.wait_ge(g.group_done, g.after[key] + e * EXP_GROUPS)

                    for i, (k, m) in enumerate(((0, 2), (2, 2), (4, 2), (6, 1), (7, 1))):
                        done(("gather", i))
                        took_it(dve.tensor_copy(xeT[:, k:k + m, :], pair(bank_in(("gather", i)), m, P)))
                    for c in range(CHUNKS):
                        done(("up", c))
                        dve.wait_ge(g.took_sems["a"], g.took["gate", c] + e * EXP_A)
                        s = he[:, c * 512:(c + 1) * 512]
                        took_it(dve.tensor_tensor(s, bank_in(("up", c))[:, :], s, ALU.mult))
                    for k in range(4):
                        done(("scatter", k))
                        s = hF[:, 2 * k:2 * k + 2, :]
                        took_it(dve.tensor_tensor(s, pair(bank_in(("scatter", k))), s, ALU.add))

            for l in range(DEPTH):
                mixer(l)
                attention(l)
                if l == 0:
                    feed_forward()
            routing()
            experts(0)
            with dve.If(dve.value_load(extra_flag[0:1, 0:1], min_val=0, max_val=1) > 0):
                experts(1)

            def log1p(q, t_, z, w):
                step.now(dve.tensor_scalar(z, t_, 2.0, None, ALU.add))
                step.now(dve.reciprocal(z, z))
                step.now(dve.tensor_tensor(z, z, t_, ALU.mult))
                step.now(dve.tensor_tensor(w, z, z, ALU.mult))
                step.now(dve.tensor_scalar(q, w, 1.0 / 15, None, ALU.mult))
                for c in (13, 11, 9, 7, 5, 3):
                    step.now(dve.scalar_tensor_tensor(q, q, 1.0 / c, w, ALU.add, ALU.mult))
                step.now(dve.scalar_tensor_tensor(q, q, 1.0, z, ALU.add, ALU.mult))
                step.now(dve.tensor_scalar(q, q, 2.0, None, ALU.mult))

            def mlstm():
                dve.wait_ge(act_took, G.took["final_ms"])
                scaled(hF, hF, lambda k: col(C3 + FIN_G + k), final_ready)
                lam = cols[:, C2 + LAM:C2 + LAM + 16]
                dve.scalar_tensor_tensor(lam_t, lam, -1.0, lam, ALU.mult, ALU.max).then_inc(abs_ready, 1)
                dve.wait_ge(exp_done, 1)
                log1p(lam_q, lam_t, lam_z, lam_w)
                step.now(dve.tensor_scalar(lam_z, lam, -1.0, 0.0, ALU.mult, ALU.max))
                step.now(dve.tensor_tensor(lam_z, lam_z, lam_q, ALU.add))
                step.then(dve.tensor_scalar(lam_neg, lam_z, -LRU_C, None, ALU.mult))
                dve.tensor_scalar(lam_pos, lam_z, LRU_C, None, ALU.mult).then_inc(lam_ready, 1)
                norm("norm1_ms", lambda k: col(C2 + N1_G + k))
                dve.wait_ge(x_ready, N_NORMS)
                step.then(dve.memset(xm_pad[:, :, 0:2], 0.0))
                step.then(dve.memset(xm_pad[:, :, 2 + SEQ:], 0.0))
                ready("gates")
                step.now(dve.memset(gate_cols, 0.0))
                src = bank_of("gates")[:, 0:32].rearrange("p (b d g h) -> p b d g h", b=TB, d=2, g=2)
                bias = gate_row.rearrange("p (d g h) -> p d g h", d=2, g=2)
                for b in range(TB):
                    for d in range(2):
                        ins = dve.tensor_tensor(gate_cols[:, b, :, 32 * d:32 * d + HEADS], src[:, b, d, :, :], bias[:, d, :, :], ALU.add)
                        if (b, d) != (1, 1):
                            step.then(ins)
                take(ins)
                dve.wait_ge(dve_took, G.took["gates"])
                step.settle()
                dve.engine_nop().then_inc(gates_ready, 1)
                ready(("gate_rows", 1))
                for g, row in enumerate((g_in, g_fo)):
                    take(dve.tensor_copy(row, bank_of(("gate_rows", g))[0:64, 0:SEQ]))
                dve.wait_ge(dve_took, G.took["gate_rows", 1])
                dve.scalar_tensor_tensor(g_t, g_fo, -1.0, g_fo, ALU.mult, ALU.max).then_inc(abs_ready, 1)
                dve.wait_ge(exp_done, 2)
                log1p(g_q, g_t, g_z, g_w)
                step.then(dve.memset(g_one, 1.0))
                step.then(dve.memset(g_zero, 0.0))
                step.now(dve.scalar_tensor_tensor(g_fo, g_fo, 0.0, g_q, ALU.min, ALU.subtract))
                fwd, bwd = slice(0, 32), slice(32, 64)
                step.then(dve.tensor_tensor_scan(g_b[fwd, :], g_one[fwd, :], g_fo[fwd, :], 0.0, ALU.mult, ALU.add))
                step.then(dve.tensor_tensor_scan(g_b[bwd, ::-1], g_one[bwd, ::-1], g_fo[bwd, ::-1], 0.0, ALU.mult, ALU.add))
                step.settle()
                step.now(dve.tensor_tensor(g_a, g_in, g_b, ALU.subtract))
                step.then(dve.tensor_tensor_scan(g_max[fwd, :], g_a[fwd, :], g_zero[fwd, :], 0.0, ALU.max, ALU.max))
                step.then(dve.tensor_tensor_scan(g_max[bwd, ::-1], g_a[bwd, ::-1], g_zero[bwd, ::-1], 0.0, ALU.max, ALU.max))
                step.settle()
                dve.tensor_tensor(g_sum, g_b, g_max, ALU.add).then_inc(a_ready, 1)
                dve.wait_ge(act_took, G.took["xm", 3])
                conv(xm_conv, lambda k, j: xm_pad[:, k, j:j + SEQ], C_TAPS, lambda k, j: col(C2 + MC_W + 8 * j + k),
                     lambda k: col(C2 + MC_B + k), tuple((k, P) for k in range(KT)))
                dve.engine_nop().then_inc(xm_conv_ready, 1)
                for b in range(TB):
                    for hp in range(2):
                        ready(("vL", b, hp))
                        take(dve.tensor_copy(vL[:, b, 512 * hp:512 * (hp + 1)], bank_of(("vL", b, hp))[:, :]))
                ready("a_cols")
                take(dve.tensor_copy(a_cols, pair(bank_of("a_cols"), TB, 64)))
                dve.wait_ge(dve_took, G.took["a_cols"])

                def argument(i):
                    h, d = divmod(i, 2)
                    ready(("maxima", i))
                    bank = banks["a"][(G.took["maxima", i] - 1) % 4][:, 0:SEQ].rearrange("p (t j) -> p t j", t=2)
                    for n_, (sblk, lo, hi) in enumerate(((0, 0, 2), (1, 1, 2)) if d == 0 else ((1, 0, 2), (0, 0, 1))):
                        ins = dve.tensor_scalar(decay[:, sblk, lo:hi, :], bank[:, lo:hi, :], a_cols[:, sblk, 32 * d + h:32 * d + h + 1],
                                                0.0, ALU.subtract, ALU.max)
                        if n_ == 0:
                            step.then(ins)
                    ins.then_inc(arg_ready, 1)

                argument(0)
                for i in range(2 * HEADS):
                    h, d = divmod(i, 2)
                    dve.wait_ge(act_took, G.took["maxima", i])
                    s4 = scoresT[:, h % 2, :, :, :].rearrange("p s t j -> p (s t) j")
                    w4, p4 = (a.rearrange("p s t j -> p (s t) j") for a in (decay, intra))
                    diag = slice(0, 4, 3)
                    other = 1 if d == 0 else 2
                    m = (tri if d == 0 else lower)[:, :].unsqueeze(1).to_broadcast([P, 2, P])
                    step.then(dve.tensor_tensor(p4[:, other, :], s4[:, other, :], w4[:, other, :], ALU.mult))
                    step.now(dve.tensor_tensor(p4[:, diag, :], s4[:, diag, :], m, ALU.mult))
                    dve.tensor_tensor(p4[:, diag, :], p4[:, diag, :], w4[:, diag, :], ALU.mult).then_inc(intra_ready, 1)
                    if i + 1 < 2 * HEADS:
                        dve.wait_ge(intra_ready, i + 1)
                        argument(i + 1)
                    ready(("den", i))
                    den = bank_of(("den", i))[:, 0:SEQ]
                    step.now(dve.tensor_tensor(rstd_row[:, :], den, floor_[:, i % 2, :], ALU.max))
                    take(dve.scalar_tensor_tensor(rstd_row[:, :], den, -1.0, rstd_row[:, :], ALU.mult, ALU.max))
                    dve.wait_ge(dve_took, G.took["den", i])
                    step.now(dve.reciprocal(rstd_row[:, :], rstd_row[:, :]))
                    r2 = rstd_row[:, :].unsqueeze(1).to_broadcast([P, 2, SEQ])
                    ready(("num", i))
                    part = hM[:, 2 * h:2 * h + 2, :]
                    if d == 0:
                        take(dve.tensor_tensor(part, pair(bank_of(("num", i))), r2, ALU.mult))
                    else:
                        num = bank_of(("num", i))
                        step.now(dve.tensor_tensor(pair(num), pair(num), r2, ALU.mult))
                        dve.wait_ge(dve_took, G.took["num", i - 1])
                        take(dve.tensor_tensor(part, part, pair(num), ALU.add))
                dve.wait_ge(dve_took, G.took["num", 2 * HEADS - 1])
                dve.engine_nop().then_inc(h_sum_ready, 1)
                dve.wait_ge(act_took, G.took["head_ms", 1])
                step.now(dve.reciprocal(std4, std4))
                for k in range(KT):
                    step.then(dve.scalar_tensor_tensor(hM[:, k, :], hM[:, k, :], col(C2 + MN_G + k), std4[:, k // 2, :], ALU.mult, ALU.mult))
                step.settle()
                dve.tensor_tensor(hM, hM, o_sig, ALU.mult).then_inc(ym_ready, 1)

            def lru():
                dve.wait_ge(ym_ready, 1)
                step.then(dve.memset(xl_pad[:, :, 0:2], 0.0))
                step.then(dve.memset(xl_pad[:, :, 2 + SEQ:], 0.0))
                dve.wait_ge(act_took, G.took["xl", 3])
                step.settle()
                conv(xl_conv, lambda k, j: xl_pad[:, k, j:j + SEQ], C_TAPS, lambda k, j: col(C3 + LC_W + 8 * j + k),
                     lambda k: col(C2 + LC_B + k), tuple((k, P) for k in range(KT)))
                dve.engine_nop().then_inc(xl_conv_ready, 1)
                dve.engine_nop().then_inc(lru_free, 1)
                for g in range(4):
                    ready(("branch_m", g))
                    take(dve.tensor_tensor(merged[:, 2 * g:2 * g + 2, :], pair(bank_of(("branch_m", g))), g_m[:, 2 * g:2 * g + 2, :], ALU.mult))
                for d in range(2):
                    dve.wait_ge(act_took, G.took["i", d, 3])
                    dve.tensor_tensor(lru_u, lru_u, xl_conv, ALU.mult).then_inc(gated_ready, 1)
                    dve.wait_ge(lru_a_ready, d + 1)
                    for i in range(2):
                        s = slice(4 * i, 4 * i + 4)
                        step.now(dve.tensor_tensor(half_tmp, lru_a[:, s, :], lru_a[:, s, :], ALU.mult))
                        ins = dve.scalar_tensor_tensor(lru_t[:, s, :], half_tmp, 1.0, lru_t[:, s, :], ALU.add, ALU.mult)
                        if i == 0:
                            step.now(ins)
                    ins.then_inc(lru_v_ready, 1)
                    edge = 0 if d == 0 else SEQ - 1
                    step.then(dve.memset(lru_a[:, :, edge:edge + 1], 0.0))
                    dve.wait_ge(lru_s_ready, d + 1)
                    dve.wait_ge(gated_ready, d + 1)
                    step.now(dve.tensor_tensor(lru_u, lru_u, lru_t[:, :, :], ALU.mult))
                    a, u, h, h2 = (x_.rearrange("p k s -> p (k s)") for x_ in (lru_a, lru_u, h_l, lru_t[:, :, :]))
                    if d == 0:
                        dve.wait_ge(group_done, G.after["branch_m", 3])
                        step.now(dve.tensor_tensor_scan(h, a, u, 0.0, ALU.mult, ALU.add))
                        dve.engine_nop().then_inc(lru_free, 1)
                    else:
                        step.now(dve.tensor_tensor_scan(h2[:, ::-1], a[:, ::-1], u[:, ::-1], 0.0, ALU.mult, ALU.add))
                step.now(dve.tensor_tensor(h_l, h_l, lru_t[:, :, :], ALU.add))
                dve.wait_ge(act_took, G.took["gate_l", 3])
                dve.tensor_tensor(h_l, h_l, gate_l, ALU.mult).then_inc(yl_ready, 1)

            def merge():
                dve.wait_ge(yl_ready, 1)
                dve.wait_ge(act_took, G.took["merge_l", 3])
                dve.wait_ge(dve_took, G.took["branch_m", 3])
                for g in range(4):
                    ready(("branch_l", g))
                    if g:
                        dve.wait_ge(merged_ready, g)
                    s = slice(2 * g, 2 * g + 2)
                    take(dve.tensor_tensor(pair_tmp, pair(bank_of(("branch_l", g))), g_l[:, s, :], ALU.mult))
                    dve.wait_ge(dve_took, G.took["branch_l", g])
                    dve.tensor_tensor(merged[:, s, :], merged[:, s, :], pair_tmp, ALU.add).then_inc(merged_ready, 1)
                add_to_residual("w_out")

            def top16(top, at, values, rest, n):
                lo, hi = slice(0, 8), slice(8, 16)
                for i in range(n):
                    step.then(dve.max(top[:, i, lo], values[:, i, :]))
                step.settle()
                for i in range(n):
                    step.then(dve.max_index(at[:, i, lo], top[:, i, lo], values[:, i, :]))
                    step.then(dve.match_replace(rest[:, i, :], top[:, i, lo], values[:, i, :], NEG))
                step.settle()
                for i in range(n):
                    step.then(dve.max(top[:, i, hi], rest[:, i, :]))
                step.settle()
                for i in range(n):
                    step.then(dve.max_index(at[:, i, hi], top[:, i, hi], rest[:, i, :]))
                step.settle()

            def choose(b):
                dve.wait_ge(act_took, G.took["key_scores", b, 3])
                top16(key_top, key_at, key_scores, key_rest, 2 * PHEADS)
                step.then(dve.tensor_copy(key_at_f.rearrange("p h s k -> p (h s) k"), key_at))
                t4 = key_top.rearrange("p (h s) k -> p h s k", s=2)
                shape = [P, PHEADS, TOPK, TOPK]
                step.then(dve.tensor_tensor(pairs_.rearrange("p h (i j) -> p h i j", i=TOPK), t4[:, :, 0, :].unsqueeze(3).to_broadcast(shape),
                                            t4[:, :, 1, :].unsqueeze(2).to_broadcast(shape), ALU.add))
                step.settle()
                top16(best, best_at, pairs_, pairs_rest, PHEADS)
                at = best_at.rearrange("p h k -> p (h k)")
                step.then(dve.tensor_scalar(half_raw[0], at, 4, None, ALU.logical_shift_right))
                step.then(dve.tensor_scalar(half_raw[1], at, TOPK - 1, None, ALU.bitwise_and))
                step.settle()
                for i in range(2):
                    step.now(dve.tensor_copy(half_at[i], half_raw[i]))
                    wide = [P, SLOTS, TOPK]
                    step.now(dve.tensor_tensor(match, half_at[i].unsqueeze(2).to_broadcast(wide),
                                               iota[:, 0:TOPK].unsqueeze(1).to_broadcast(wide), ALU.is_equal))
                    m4 = match.rearrange("p (h k) j -> p h k j", h=PHEADS)
                    step.now(dve.tensor_tensor(m4, m4, key_at_f[:, :, i, :].unsqueeze(2).to_broadcast(shape), ALU.mult))
                    step.now(dve.tensor_reduce(half_key[i], match, AX.X, ALU.add))
                dve.scalar_tensor_tensor(rows_at[:, b * SLOTS:(b + 1) * SLOTS], half_key[0], float(PK), half_key[1],
                                         ALU.mult, ALU.add).then_inc(index_ready, 1)
                g = gates[:, b, :, :]
                dve.tensor_tensor(g, best, best[:, :, 0:1].to_broadcast([P, PHEADS, TOPK]), ALU.subtract).then_inc(margin_ready, 1)
                dve.wait_ge(margin_exp, b + 1)
                step.now(dve.tensor_reduce(gate_sum, g, AX.X, ALU.add))
                step.now(dve.reciprocal(gate_inv, gate_sum))
                step.now(dve.tensor_tensor(g, g, gate_inv.unsqueeze(2).to_broadcast([P, PHEADS, TOPK]), ALU.mult))

            def peer():
                norm("norm2_ms", lambda k: col(C2 + N2_G + k))
                for g in range(4):
                    ready(("keysT", g))
                    take(dve.tensor_copy(keysT[:, 4 * g:4 * g + 4, :], pair(bank_of(("keysT", g)), 4, P)))
                for b in range(TB):
                    choose(b)
                dve.memset(zero_row, 0.0).then_inc(zero_ready, 1)
                for b in range(TB):
                    ready(("tokens", b, 1))
                    n = (G.took["tokens", b, 0] - 1) % 4
                    assert n % 2 == 0
                    x = psum_all[:, n:n + 2, :].rearrange("p h d -> p (h d)")
                    with dve.Fori(b * ROUNDS, (b + 1) * ROUNDS) as r:
                        for q in range(BATCHES):
                            dve.wait_ge(gathered[q], r * 16 * BATCH + 16 * BATCH)
                            for j in range(q * BATCH, (q + 1) * BATCH):
                                row = gathered_rows[:, j, :]
                                ins = dve.tensor_tensor_reduce(row, row, x, 1.0, 0.0, ALU.mult, ALU.add, dots[:, j:j + 1])
                            ins.then_inc(dot_done, 1)
                        dve.wait_ge(dot_done, r * BATCHES + BATCHES)
                        dve.tensor_copy(acts[:, bass.ds(r * GATHER, GATHER)], dots).then_inc(dots_kept, 1)
                        dve.wait_ge(dots_kept, r + 1)
                for b in range(TB):
                    dve.wait_ge(act_ready, b + 1)
                    s = acts[:, b * SLOTS:(b + 1) * SLOTS]
                    dve.tensor_tensor(s, s, gates[:, b, :, :].rearrange("p h k -> p (h k)"), ALU.mult).then_inc(weight_ready, 1)
                dve.wait_ge(weight_ready, TB)

                def diagonals(r, first):
                    for q in range(BATCHES):
                        if not first:
                            dve.wait_ge(mix_done, (r - 1) * BATCHES + q + 1)
                        shape = [P, BATCH, P]
                        dve.tensor_tensor(diag[:, q, :, :], ident[:, :].unsqueeze(1).to_broadcast(shape),
                                          acts[:, bass.ds(r * GATHER + q * BATCH, BATCH)].unsqueeze(2).to_broadcast(shape), ALU.mult
                                          ).then_inc(diag_ready, 1)

                diagonals(0, True)
                with dve.Fori(1, TB * ROUNDS) as r:
                    diagonals(r, False)
                dve.wait_ge(gain_loaded, 16)
                for b in range(TB):
                    dve.wait_ge(final_std_ready, b + 1)
                    step.now(dve.reciprocal(final_rstd[:, b:b + 1], final_std[:, b:b + 1]))
                    n = 4 + (G.took["out", b, 0] - 1) % 4
                    dve.scalar_tensor_tensor(final_rows[:, b, :], psum_all[:, n:n + 2, :].rearrange("p h d -> p (h d)"),
                                             final_rstd[:, b:b + 1], final_gain, ALU.mult, ALU.mult).then_inc(final_out, 1)

            mlstm()
            lru()
            merge()
            peer()


_OUT = ((1, SEQ, D), "float32")


def kernel(**inputs):
    import numpy as _np
    import concourse.bacc as _bacc
    from concourse import mybir as _mybir
    from concourse.bass_utils import run_bass_kernel_spmd as _run

    nc = _bacc.Bacc("TRN2", target_bir_lowering=False, num_devices=1)
    arrays, t = {}, {}
    for name, a in inputs.items():
        a = _np.ascontiguousarray(a)
        arrays[f"in_{name}"] = a
        t[name] = nc.dram_tensor(f"in_{name}", a.shape, _mybir.dt.from_np(a.dtype), kind="ExternalInput").ap()
    out = nc.dram_tensor("out_0", _OUT[0], F32, kind="ExternalOutput").ap()
    two_blocks(nc, t, out)
    r = _run(nc, [arrays], core_ids=[0])
    return r.results[0]["out_0"]
```

```python
from contextlib import ExitStack

import concourse.bass as bass
from concourse import mybir
from concourse.alu_op_type import AluOpType as ALU

ACT = mybir.ActivationFunctionType
AX = mybir.AxisListType
F32 = mybir.dt.float32
I32 = mybir.dt.int32
F32R = mybir.dt.float32r
U32 = mybir.dt.uint32

P = 128
EPS = 1e-6
DEPTH, D, SEQ = 2, 1024, 256
KT, TB = D // P, SEQ // P
A_W, BC_W = 384, 320
A_TAPS, B_TAPS, C_TAPS = 31, 3, 4
HEADS, HD = 4, 256
FF, N_EXP, EXP_W = 2816, 8, 3584
FT, ET = FF // P, EXP_W // P
LRU_C = 8.0
PK, PHEADS, TOPK = 128, 8, 16
SLOTS = PHEADS * TOPK
NEG = -3.0e38
RING = 7
SLOT_F = KT * 512
GATHER, BATCH = 16, 4
BATCHES = GATHER // BATCH
GATHERED = 16 * BATCH
ROUNDS = SLOTS // GATHER
CHUNKS = EXP_W // 512
GATE_UP, DOWN = 4 * CHUNKS, ET // 2
EXP_TILES = GATE_UP + DOWN
AHEAD = 2
EXP_GROUPS, EXP_V, EXP_A = 32, 16, 16
EXP_MARKS = 2 * CHUNKS + DOWN - 1


class Groups:

    def __init__(self, pe, banks, group_done, took_sems, loads):
        self.pe, self.banks, self.group_done, self.took_sems = pe, banks, group_done, took_sems
        self.total, self.given = 0, {"v": 0, "a": 0}
        self.after, self.took, self.open = {}, {}, []
        self.loads, self.loaded, self.slots = loads, [0] * RING, []
        self.freed, self.need = [], []
        self.turn = None

    def begin(self, who, key):
        n = self.given[who]
        if n >= 4:
            extra = 0 if self.turn is None else self.turn * EXP_V
            self.pe.wait_ge(self.took_sems[who], n - 3 + extra)
        self.given[who] = n + 1
        self.took[key] = n + 1
        self.open.append(key)
        return self.banks[who][n % 4]

    def end(self, mm, key=None):
        key = key or self.open[0]
        self.open.remove(key)
        self.total += 1
        self.after[key] = self.total
        mm.then_inc(self.group_done, 1)

    def tile(self, dmas=1):
        n = len(self.need)
        slot = n % RING
        self.loaded[slot] += 16 * dmas
        self.need.append(self.loaded[slot])
        self.freed.append(None)
        self.pe.wait_ge(self.loads[slot], self.loaded[slot])
        return slot

    def free(self):
        self.freed[-1] = (self.group_done, self.total)

    def loop(self, turn):
        self.turn, self.start = turn, (self.total, dict(self.given))

    def close(self, turns):
        total, given = self.start
        assert self.total - total == EXP_GROUPS and len(self.used) == EXP_TILES and self.marks == 2 * EXP_MARKS
        assert self.given["v"] - given["v"] == EXP_V and self.given["a"] - given["a"] == EXP_A
        self.turn = None
        self.total += EXP_GROUPS * (turns - 1)
        self.given["v"] += EXP_V * (turns - 1)
        self.given["a"] += EXP_A * (turns - 1)
        self.loaded0 = self.loaded
        self.loaded = [x + 16 * turns * EXP_TILES // RING for x in self.loaded]


class Experts:

    def __init__(self, groups, sem, name):
        groups.split, groups.high, groups.marked = (sem(f"{name}_{x}") for x in ("tiles_split", "tiles_rounded", "tile_used"))
        groups.x_high, groups.hidden_split = sem(f"{name}_x_rounded"), sem(f"{name}_hidden_split")
        groups.used, groups.marks = [], EXP_MARKS


class Steps:

    def __init__(self, eng, sem):
        self.eng, self.sem, self.n, self.turn, self.per = eng, sem, 0, None, 0

    def value(self, n):
        return n if self.turn is None else n + self.turn * self.per

    def then(self, ins):
        ins.then_inc(self.sem, 1)
        self.n += 1

    def settle(self, back=0):
        if self.n > back:
            self.eng.wait_ge(self.sem, self.value(self.n - back))

    def now(self, ins):
        self.then(ins)
        self.settle()


class Tally:
    def __init__(self):
        self.n = {}

    def next(self, name):
        self.n[name] = self.n.get(name, 0) + 1
        return self.n[name]


def two_blocks(nc, t, out):
    with ExitStack() as ctx:
        def sb(name, shape, dt=F32):
            return ctx.enter_context(nc.sbuf_tensor(name, shape, dt))

        def sem(name):
            return ctx.enter_context(nc.semaphore(name))

        def sb_under(name, shape):
            with nc.sbuf_tensor(name, shape, F32) as under:
                return under

        ring = sb_under("weight_ring", [P, RING, SLOT_F])
        raw_tiles = sb_under("expert_tiles", [P, RING, SLOT_F // 2])
        low_tiles, high_tiles = (sb(f"expert_tiles_{x}", [P, RING, SLOT_F // 2], F32R) for x in ("low", "high"))
        hF = sb("residual", [P, KT, SEQ])
        xF = sb_under("normed", [P, KT, SEQ])
        xe_parts = sb("gathered_parts", [P, 2, KT, P], F32R)
        squares = sb("squares", [P, KT, SEQ])
        ident = sb("ident", [P, P])
        ones = sb("ones", [P, P])
        lower = sb("lower", [P, P])
        half_ones = sb("half_ones", [P, P])
        tri = sb("tri", [P, P])
        iota = sb("iota", [P, P])
        pair_sel = sb("pair_sel", [5, 3, P])
        gate_bias = sb("gmlp_bias", [5, DEPTH, P])
        spatialT = sb("spatialT", [P, DEPTH, 5, P])
        cols = sb("cols", [P, 474])
        mean_row = sb("neg_mean", [P, SEQ])
        std_row = sb("std", [P, SEQ])
        rstd_row = sb("rstd", [P, SEQ])
        eps = sb("eps", [P, 1])
        router = sb("router", [P, KT, N_EXP])
        small = sb("small", [P, 256])
        extra_flag = sb("extra_flag", [P, 1], I32)
        WORK = 13848
        work = sb_under("work", [P, WORK])
        work_parts = sb("work_parts", [P, WORK], F32R)

        def view(off, *shape):
            n = 1
            for s in shape:
                n *= s
            assert off + n <= WORK, (off, shape)
            flat = work[:, off:off + n]
            if len(shape) == 1:
                return flat
            names = "abcd"[:len(shape)]
            kw = {c: s for c, s in zip(names, shape)}
            return flat.rearrange(f"p ({' '.join(names)}) -> p {' '.join(names)}", **kw)

        psum_all = ctx.enter_context(nc.psum_tensor("banks", [P, 8, 512], F32))
        psum = [psum_all[:, i, :] for i in range(8)]
        banks = {"v": psum[0:4], "a": psum[4:8]}

        def pair(bank, n=2, w=SEQ):
            return bank[:, 0:n * w].rearrange("p (a b) -> p a b", a=n)

        def c_vec(l, which, k):
            return cols[:, 49 * l + which + k:49 * l + which + k + 1]
        MIX_G, X_G, MEM_G, FFN_G, OUT_G, CONVA_B, LNA_G, LNA_B = 0, 8, 16, 24, 32, 40, 43, 46
        C1, C2 = 98, 98 + 2 * 93
        N1_G, MC_B, MN_G, LC_B, BR, BI, LAM, N2_G, MC_W = 0, 8, 16, 24, 32, 48, 64, 80, 88
        C3 = C2 + 120
        LC_W, FIN_G = 0, 32
        C4 = C3 + 40

        def col(i, rows=P):
            return cols[0:rows, i:i + 1]

        def bc_col(l, which, k):
            return col(C4 + 10 * k + 5 * l + which, P if k < 2 else 64)

        MEM = WORK - KT * SEQ
        mem_hat = view(MEM, KT, SEQ)
        x_in, mem_in = view(0, TB, D), view(2048, TB, D)
        rows = view(4096, 5, P)
        bc_rows = view(4736, 320)
        spatial_in = view(5056, DEPTH, 5, P)
        sig_a = view(0, 3, SEQ)
        ya_pad = view(768, 3, SEQ + A_TAPS - 1)
        conv_a = view(1626, 3, SEQ)
        c_gate = view(2394, 3, SEQ)
        yb_pad = view(3162, 3, SEQ + B_TAPS - 1)
        b_gate = view(3936, 3, SEQ)
        conv_b = view(4704, 3, SEQ)
        c_u = view(5472, 3, SEQ)
        c_v = view(6240, 3, SEQ)
        vT = view(7008, TB, BC_W)
        yF = view(7648, KT, SEQ)
        std8 = view(9696, KT, SEQ)
        mem_g, qF, kF = view(0, KT, SEQ), view(2048, KT, SEQ), view(4096, KT, SEQ)
        vM = view(6144, TB, D)
        probs = view(8192, HEADS, TB, SEQ)
        probsT = squares[:, :, :].rearrange("p (h m) s -> p h m s", h=HEADS)
        oF = view(0, KT, SEQ)
        hid = view(0, FT, SEQ)
        sil = view(5632, 2, 2, SEQ)
        xT = view(0, TB, D)
        pick = view(2048, TB, N_EXP + 1, P)
        put = squares[:, :, :]
        he = view(4352, 2, 512)
        xe_high, xe_low = xe_parts[:, 0, :, :], xe_parts[:, 1, :, :]
        he_high, he_low = (work_parts[:, 5376 + i * EXP_W:5376 + (i + 1) * EXP_W].rearrange("p (a b) -> p a b", b=P) for i in range(2))
        he_all = view(5376 + EXP_W, ET, P)
        ye = view(12544, D)
        weighted = view(5376, TB, N_EXP, P)
        def raw_tile(j):
            return raw_tiles[:, j % RING, :]

        def low_tile(j):
            return low_tiles[:, j % RING, :]

        def high_tile(j):
            return high_tiles[:, j % RING, :]

        def pairs_of(off):
            return small[:, off:off + TB * N_EXP].rearrange("p (b e) -> p b e", b=TB)
        logits, top, top_at, first, second, chosen, share, place = (pairs_of(16 * i) for i in range(8))
        gap, ratio, total_w, w_first, w_second = (small[:, 128 + 2 * i:130 + 2 * i] for i in range(5))
        counts, most = small[:, 144:152], small[:, 152:153]
        top_raw = small[:, 160:176].bitcast(U32).rearrange("p (b e) -> p b e", b=TB)

        xm_pad = view(0, KT, SEQ + C_TAPS - 1)
        xm_conv = view(2072, KT, SEQ)
        qM, kM = view(4120, KT, SEQ), view(6168, KT, SEQ)
        vL = view(8216, TB, D)
        scoresT = view(10264, 2, 2, 2, P)
        decay = view(11288, 2, 2, P)
        intra = view(11800, 2, 2, P)
        floor_ = view(12312, 2, SEQ)
        head_sel = view(12824, 8, P)
        gate_cols = squares[:, 0, :].rearrange("p (b g r) -> p b g r", b=TB, g=2)
        g_in, g_fo, g_t, g_z, g_w, g_q, g_b, g_a = (squares[0:64, i, :] for i in range(8))
        g_max, g_sum, g_zero, g_one = g_t, g_z, g_w, mean_row[0:64, :]
        a_cols = small[:, 96:224].rearrange("p (b r) -> p b r", b=TB)
        gate_row = small[:, 240:256]
        hM = view(2072, KT, SEQ)
        o_sig = view(0, KT, SEQ)
        std4 = view(10520, HEADS, SEQ)
        g_m, merged = view(4120, KT, SEQ), view(6168, KT, SEQ)
        xl_pad = view(8216, KT, SEQ + C_TAPS - 1)
        xl_conv = view(0, KT, SEQ)
        h_l = view(2072, KT, SEQ)
        gate_l = view(4120, KT, SEQ)
        lru_a, lru_u = view(8216, KT, SEQ), view(10264, KT, SEQ)
        lru_t = squares
        half_tmp = view(12312, 4, SEQ)
        g_l = view(0, KT, SEQ)
        pair_tmp = view(12312, 2, SEQ)
        lam_t, lam_z, lam_w, lam_q, lam_neg, lam_pos = (small[:, 16 * i:16 * i + 16] for i in range(6))

        qP, keysT = view(0, 2 * PHEADS, SEQ), view(4096, 2 * PHEADS, PK)
        key_scores, key_rest = view(6144, 2 * PHEADS, PK), view(8192, 2 * PHEADS, PK)
        pairs_, pairs_rest = view(6144, PHEADS, TOPK * TOPK), view(8192, PHEADS, TOPK * TOPK)
        key_top, key_at = view(10240, 2 * PHEADS, TOPK), view(10496, 2 * PHEADS, TOPK).bitcast(U32)
        key_at_f = view(10752, PHEADS, 2, TOPK)
        best, best_at = view(11008, PHEADS, TOPK), view(11136, PHEADS, TOPK).bitcast(U32)
        half_raw = [view(11264 + SLOTS * i, SLOTS).bitcast(U32) for i in range(2)]
        half_at = [view(11520 + SLOTS * i, SLOTS) for i in range(2)]
        half_key = [view(11776 + SLOTS * i, SLOTS) for i in range(2)]
        gates = view(12032, TB, PHEADS, TOPK)
        rows_at = view(12288, TB * SLOTS).bitcast(U32)
        acts = view(12544, TB * SLOTS)
        final_gain = view(12800, D)
        match = squares[:, :, :].rearrange("p k s -> p (k s)").rearrange("p (a j) -> p a j", j=TOPK)
        gathered_rows = ring[:, 0:GATHER * D // SLOT_F, :].rearrange("p s (r d) -> p (s r) d", d=D)
        diag = view(0, BATCHES, BATCH - 1, P)
        zero_row = view(1536, 512)[0:1, :]
        final_sq, v_sum = view(4096, D), view(5120, D)
        final_rows = view(6144, TB, D)
        stage = sb("gather_stage", [P, GATHER], U32)
        dots = small[:, 0:GATHER]
        gate_sum, gate_inv = small[:, 16:24], small[:, 24:32]
        final_ss, final_std, final_rstd = (small[:, 32 + 2 * i:34 + 2 * i] for i in range(3))

        loads = [sem(f"weights_loaded{i}") for i in range(RING)]
        group_done = sem("pe_group_done")
        dve_took, act_took = sem("dve_took"), sem("act_took")
        took_sems = {"v": dve_took, "a": act_took}
        dve_step, act_step, pool_step = sem("dve_step"), sem("act_step"), sem("pool_step")
        inputs_loaded = sem("inputs_loaded")
        params_loaded = sem("params_loaded")
        consts_ready = sem("consts_ready")
        sq_ready = sem("squares_ready")
        x_ready = sem("normed_ready")
        conv_ready = sem("conv_ready")
        centred = sem("centred")
        ln_ready = sem("ln_ready")
        ya_ready = sem("ya_ready")
        y_all = sem("y_all_ready")
        y_ready = sem("y_ready")
        cv_ready = sem("cv_ready")
        mask_ready = sem("spatial_masked")
        mem_normed = sem("mem_normed")
        mem_ready = sem("mem_ready")
        max_ready = sem("max_ready")
        probs_ready = sem("probs_ready")
        exp_ready = sem("exp_ready")
        out_done = sem("out_stored")
        routing_ready = sem("routing_ready")
        chosen_ready = sem("chosen_ready")
        gap_ready = sem("logit_gap_ready")
        ratio_ready = sem("expert_ratio_ready")
        weighted_ready = sem("weighted_ready")
        pick_ready = sem("pick_ready")
        final_ready = sem("first_block_normed")
        gates_ready = sem("gate_columns_ready")
        abs_ready, exp_done = sem("abs_ready"), sem("exp_done")
        a_ready = sem("gate_rows_ready")
        sel_ready = sem("head_sel_ready")
        xm_conv_ready, xm_act = sem("xm_conv_ready"), sem("xm_activated")
        arg_ready = sem("decay_argument_ready")
        intra_ready = sem("intra_ready")
        h_sum_ready = sem("mlstm_sum_ready")
        ym_ready = sem("y_mlstm_ready")
        xl_conv_ready = sem("xl_conv_ready")
        lam_ready = sem("lam_ready")
        gated_ready = sem("lru_input_gated")
        lru_a_ready = sem("lru_decay_ready")
        lru_v_ready, lru_s_ready = sem("lru_scale_squared_ready"), sem("lru_scale_ready")
        lru_free = sem("lru_buffers_free")
        yl_ready = sem("y_lru_ready")
        merged_ready = sem("merged_ready")
        index_ready = sem("peer_index_ready")
        margin_ready, margin_exp = sem("gate_margin_ready"), sem("gate_margin_exp")
        gathered = [sem(f"rows_gathered{i}") for i in range(BATCHES)]
        staged, pool_turn = sem("indices_staged"), sem("pool_turn")
        dot_done, dots_kept = sem("dot_batch_done"), sem("dots_kept")
        act_ready, weight_ready = sem("peer_activation_ready"), sem("peer_weight_ready")
        diag_ready, mix_done, add_done = sem("diag_ready"), sem("mix_batch_done"), sem("add_batch_done")
        v_zeroed, v_summed = sem("v_sum_zeroed"), sem("v_summed")
        zero_ready = sem("zero_row_ready")
        gain_loaded = sem("final_gain_loaded")
        final_std_ready, final_out = sem("final_std_ready"), sem("final_rows_ready")
        more_places = sem("more_places")
        more_done = sem("more_groups_done")
        more_took = {"v": sem("more_dve_took"), "a": sem("more_act_took")}
        more_loads = [sem(f"more_weights_loaded{i}") for i in range(RING)]

        EPS_AP = eps[:, 0:1]
        G = None
        passes = []
        N_NORMS = 3 * DEPTH + 1
        N_PARAMS = DEPTH * 17 + 13
        def wait_used(eng, g, e, j):
            if j >= RING:
                used, count, per = g.used[j - RING]
                eng.wait_ge(used, count + e * per)
            elif not isinstance(e, int) or e > 0:
                used, count, per = g.used[j + EXP_TILES - RING]
                eng.wait_ge(used, count + (e - 1) * per)

        block = ctx.enter_context(nc.Block())

        @block.tensor
        def _(pe):
            nonlocal G
            G = Groups(pe, banks, group_done, took_sems, loads)
            seen = Tally()

            def transposes(who, key, parts):
                bank = G.begin(who, key)
                for off, a in parts:
                    k, m = a.shape[0], a.shape[1]
                    mm = pe.transpose(bank[0:m, off:off + k], a, ident[0:k, 0:k])
                G.end(mm)

            def sum_features(who, key, src, n=KT, weights=None, w=SEQ):
                bank = G.begin(who, key)
                for k in range(n):
                    a = src(k)
                    mm = pe.matmul(bank[:, 0:w], (weights or ones)[0:a.shape[0], :], a,
                                   start=(k == 0), stop=(k == n - 1))
                G.end(mm)

            def norm_sums(key):
                pe.wait_ge(sq_ready, seen.next("sq"))
                sum_features("a", key, lambda k: squares[:, k, :])

            def linear(key, who, n_tiles, x, kts, widths=(0, P, 2 * P, 3 * P), per_group=2, dmas=1, ms=None):
                c = 0
                for tile in range(n_tiles):
                    slot = G.tile(dmas)
                    for i, off in enumerate(widths):
                        m = P if ms is None else ms[i]
                        if c % per_group == 0:
                            bank = G.begin(who, (key, c // per_group))
                        o = bank[0:m, (c % per_group) * SEQ:(c % per_group + 1) * SEQ]
                        for k in range(kts):
                            mm = pe.matmul(o, weight(slot, kts, widths)[:, k, off:off + m], x(k),
                                           start=(k == 0), stop=(k == kts - 1))
                        c += 1
                        if c % per_group == 0 or (tile == n_tiles - 1 and i == len(widths) - 1):
                            G.end(mm)
                    G.free()

            def weight(slot, kts, widths, cols_n=None):
                n = cols_n or 512
                return ring[:, slot, 0:kts * n].rearrange("p (k n) -> p k n", k=kts)

            pe.wait_ge(consts_ready, 1)
            pe.wait_ge(inputs_loaded, 32)
            for who, src, name in (("v", x_in, "x"), ("a", mem_in, "mem")):
                for g in range(4):
                    transposes(who, (name, g), [((k % 2) * SEQ + b * P, src[:, b, k * P:(k + 1) * P])
                                                for k in (2 * g, 2 * g + 1) for b in range(TB)])
            pe.wait_ge(params_loaded, 16 * N_PARAMS)
            parts = [(0, rows[0:98, 0, :]), (C1, rows[0:93, 1, :]), (C1 + 93, rows[0:93, 2, :]),
                     (C2, rows[0:120, 3, :]), (C3, rows[0:40, 4, :])]
            parts += [(C4 + 10 * k, bc_rows[0:10, k * P:min((k + 1) * P, 320)]) for k in range(3)]
            transposes("v", "cols", parts)
            for l in range(DEPTH):
                transposes("a", ("spatial", l, 0), [(g * P, spatial_in[:, l, g, :]) for g in range(4)])
            transposes("a", "spatial_last", [(l * P, spatial_in[:, l, 4, :]) for l in range(DEPTH)])
            norm_sums("mem_ms")

            def mixer(l):
                norm_sums(("mix_ms", l))
                pe.wait_ge(x_ready, seen.next("x"))
                x = lambda k: xF[:, k, :]

                def section(name, who, width, offs, ms):
                    slot = G.tile()
                    w = ring[:, slot, 0:KT * width].rearrange("p (k n) -> p k n", k=KT)
                    for g, tiles in enumerate(((0, 1), (2,))):
                        bank = G.begin(who, (name, l, g))
                        for i, c in enumerate(tiles):
                            for k in range(KT):
                                mm = pe.matmul(bank[0:ms[c], i * SEQ:(i + 1) * SEQ], w[:, k, offs[c]:offs[c] + ms[c]],
                                               x(k), start=(k == 0), stop=(k == KT - 1))
                        G.end(mm)
                    G.free()

                section("a_gate", "a", A_W, (0, P, 2 * P), (P, P, P))
                section("a_val", "v", A_W, (0, P, 2 * P), (P, P, P))
                section("c_gate", "a", BC_W, (0, P, 2 * P), (P, P, 64))
                section("b_in", "v", BC_W, (0, P, 2 * P), (P, P, 64))
                section("b_gate", "a", BC_W, (0, P, 2 * P), (P, P, 64))
                section("c_v", "a", BC_W, (0, P, 2 * P), (P, P, 64))
                section("c_u", "a", BC_W, (0, P, BC_W - P), (P, P, P))

                def three(src):
                    return lambda k: src[0:(P if k < 2 else 64), k, :]

                pe.wait_ge(act_took, G.took["c_v", l, 1])
                sum_features("a", ("c_mean", l), three(c_v), 3)
                pe.wait_ge(sq_ready, seen.next("sq"))
                sum_features("a", ("c_var", l), three(squares), 3)
                pe.wait_ge(cv_ready, l + 1)
                for b in range(TB):
                    transposes("v", ("c_vT", l, b), [(k * P, three(c_v)(k)[:, b * P:(b + 1) * P]) for k in range(3)])
                pe.wait_ge(dve_took, G.took["c_vT", l, 1])
                pe.wait_ge(mask_ready, 1)
                for p in range(3):
                    n = 2 if p < 2 else 1
                    first = p * P if p < 2 else BC_W - P
                    for b in range(TB):
                        bank = G.begin("v", ("mixed", l, p, b))
                        for i in range(n):
                            o = bank[:, i * P:(i + 1) * P]
                            pe.matmul(o, vT[:, b, first:first + P], spatialT[:, l, 2 * p + i, :], start=True, stop=False)
                            mm = pe.matmul(o, pair_sel[:, p, :], gate_bias[:, l, :], start=False, stop=True)
                        G.end(mm)
                pe.wait_ge(conv_ready, l + 1)
                sum_features("a", ("a_mean", l), lambda k: conv_a[:, k, :], 3)
                pe.wait_ge(sq_ready, seen.next("sq"))
                sum_features("a", ("a_var", l), lambda k: squares[:, k, :], 3)
                pe.wait_ge(sq_ready, seen.next("sq"))
                for g in range(4):
                    bank = G.begin("a", ("group_ms", l, g))
                    for i in range(2):
                        mm = pe.matmul(bank[:, i * SEQ:(i + 1) * SEQ], half_ones[:, :], squares[:, 2 * g + i, :],
                                       start=True, stop=True)
                    G.end(mm)
                pe.wait_ge(y_ready, l + 1)
                linear(("mix_out", l), "v", 2, lambda k: yF[:, k, :], KT, dmas=4)

            def attention(l):
                pe.wait_ge(mem_ready, l + 1)
                linear(("k", l), "a", 2, lambda k: mem_g[:, k, :], KT)
                for half in range(2):
                    slot = G.tile()
                    for b in range(TB):
                        bank = G.begin("a", ("v", l, half, b))
                        for k in range(KT):
                            mm = pe.matmul(bank[:, :], mem_g[:, k, b * P:(b + 1) * P], weight(slot, KT, None)[:, k, :],
                                           start=(k == 0), stop=(k == KT - 1))
                        G.end(mm)
                    G.free()
                norm_sums(("x_ms", l))
                pe.wait_ge(x_ready, seen.next("x"))
                linear(("q", l), "a", 2, lambda k: xF[:, k, :], KT)
                pe.wait_ge(act_took, G.took[("q", l), 3])
                for h in range(HEADS):
                    bank = G.begin("a", ("scores", l, h))
                    for b in range(TB):
                        for j in range(2):
                            mm = pe.matmul(bank[:, b * SEQ:(b + 1) * SEQ], qF[:, 2 * h + j, b * P:(b + 1) * P],
                                           kF[:, 2 * h + j, :], start=(j == 0), stop=(j == 1))
                    G.end(mm)
                for h in range(HEADS):
                    pe.wait_ge(probs_ready, HEADS * l + h + 1)
                    transposes("v", ("probsT", l, h), [(m * SEQ + b * P, probs[:, h, b, m * P:(m + 1) * P])
                                                       for m in range(TB) for b in range(TB)])
                for h in range(HEADS):
                    pe.wait_ge(dve_took, G.took["probsT", l, h])
                    bank = G.begin("a", ("o", l, h))
                    for e in range(2):
                        for m in range(TB):
                            mm = pe.matmul(bank[:, e * SEQ:(e + 1) * SEQ], vM[:, m, h * HD + e * P:h * HD + (e + 1) * P],
                                           probsT[:, h, m, :], start=(m == 0), stop=(m == TB - 1))
                    G.end(mm)
                pe.wait_ge(act_took, G.took["o", l, HEADS - 1])
                linear(("xo", l), "v", 2, lambda k: oF[:, k, :], KT)

            def feed_forward():
                norm_sums("ffn_ms")
                pe.wait_ge(x_ready, seen.next("x"))
                for c in range(FT // 2):
                    slot = G.tile(2)
                    w = ring[:, slot, :].rearrange("p (a k n) -> p a k n", a=2, k=KT)
                    for a, who in ((0, "a"), (1, "v")):
                        bank = G.begin(who, ("ffn", a, c))
                        for i in range(2):
                            for k in range(KT):
                                mm = pe.matmul(bank[:, i * SEQ:(i + 1) * SEQ], w[:, a, k, i * P:(i + 1) * P], xF[:, k, :],
                                               start=(k == 0), stop=(k == KT - 1))
                        G.end(mm)
                    G.free()
                pe.wait_ge(dve_took, G.took["ffn", 1, FT // 2 - 1])
                for c in range(KT):
                    slot = G.tile()
                    w = ring[:, slot, 0:FT * P].rearrange("p (k n) -> p k n", k=FT)
                    if c % 2 == 0:
                        bank = G.begin("v", ("ffn_down", c // 2))
                    for k in range(FT):
                        mm = pe.matmul(bank[:, (c % 2) * SEQ:(c % 2 + 1) * SEQ], w[:, k, :], hid[:, k, :],
                                       start=(k == 0), stop=(k == FT - 1))
                    if c % 2 == 1:
                        G.end(mm)
                        G.free()
                        G.freed[-2] = G.freed[-1]

            def routing():
                norm_sums("moe_ms")
                pe.wait_ge(x_ready, seen.next("x"))
                bank = G.begin("v", "logits")
                for b in range(TB):
                    for k in range(KT):
                        mm = pe.matmul(bank[:, b * N_EXP:(b + 1) * N_EXP], xF[:, k, b * P:(b + 1) * P], router[:, k, :],
                                       start=(k == 0), stop=(k == KT - 1))
                G.end(mm)
                for b in range(TB):
                    for half in range(2):
                        transposes("a", ("xT", b, half), [(i * P, xF[:, 4 * half + i, b * P:(b + 1) * P]) for i in range(4)])
                pe.wait_ge(chosen_ready, 1)
                bank = G.begin("v", "places")
                pe.matmul(bank[:, 0:N_EXP], tri[:, :], chosen[:, 0, :], start=True, stop=True)
                pe.matmul(bank[:, N_EXP:2 * N_EXP], ones[:, :], chosen[:, 0, :], start=True, stop=False)
                pe.matmul(bank[:, N_EXP:2 * N_EXP], tri[:, :], chosen[:, 1, :], start=False, stop=True)
                pe.matmul(bank[:, 2 * N_EXP:3 * N_EXP], ones[:, :], chosen[:, 0, :], start=True, stop=False)
                G.end(pe.matmul(bank[:, 2 * N_EXP:3 * N_EXP], ones[:, :], chosen[:, 1, :], start=False, stop=True))

            def experts(n):
                g = passes[n]
                pe.wait_ge(weighted_ready, n + 1)
                for e in range(N_EXP):
                    bank = g.begin("v" if e < 4 else "a", ("put", e))
                    for b in range(TB):
                        mm = pe.transpose(bank[:, b * P:(b + 1) * P], weighted[:, b, e, :], ident[:, :])
                    g.end(mm)
                pe.wait_ge(g.took_sems["a"], g.took["put", N_EXP - 1])
                pe.wait_ge(g.took_sems["v"], g.took["put", 3])
                pe.wait_ge(act_took, G.took["xT", TB - 1, 1])
                pe.wait_ge(pick_ready, n + 1)
                def gather(e, key, groups=range(5)):
                    for i in groups:
                        tiles = ((0, 1), (2, 3), (4, 5), (6,), (7,))[i]
                        bank = g.begin("v", (key, i))
                        for j, k in enumerate(tiles):
                            for b in range(TB):
                                mm = pe.matmul(bank[:, j * P:(j + 1) * P], xT[:, b, k * P:(k + 1) * P],
                                               pick[:, b, bass.ds(e, 1), :].rearrange("p o s -> p (o s)"),
                                               start=(b == 0), stop=(b == TB - 1))
                        g.end(mm, (key, i))

                def parts(o, x_high, x_low, w_high, w_low, start, stop):
                    pe.matmul(o, x_high, w_high, start=start, stop=False)
                    pe.matmul(o, x_high, w_low, start=False, stop=False)
                    return pe.matmul(o, x_low, w_high, start=False, stop=stop)

                pe.sem_inc(g.marked, EXP_MARKS)
                gather(0, "first")
                pe.wait_ge(g.took_sems["v"], g.took["first", 4])
                with pe.Fori(0, N_EXP) as e:
                    g.loop(e)

                    def taken(who, key):
                        pe.wait_ge(g.took_sems[who], g.took[key] + e * (EXP_V if who == "v" else EXP_A))

                    def split(j, rows_):
                        pe.wait_ge(g.split, e * EXP_TILES + j + 1)
                        return (a.rearrange("p (k n) -> p k n", k=rows_) for a in (high_tile(j), low_tile(j)))

                    def mark(mm):
                        mm.then_inc(g.marked, 1)
                        g.marks += 1
                        g.used.append((g.marked, g.marks, EXP_MARKS))

                    def hidden_transposes(c, bank):
                        taken("v", ("up", c))
                        for i in range(4):
                            mm = pe.transpose(bank[:, i * P:(i + 1) * P], he[:, c % 2, i * P:(i + 1) * P], ident[:, :])
                        g.end(mm, ("hidden", c))

                    for c in range(CHUNKS):
                        for n_, (who, name) in enumerate((("a", "gate"), ("v", "up"))):
                            bank = g.begin(who, (name, c))
                            for half in range(2):
                                high, low = split(4 * c + 2 * n_ + half, KT // 2)
                                for i in range(KT // 2):
                                    k = half * (KT // 2) + i
                                    mm = parts(bank, xe_high[:, k, :], xe_low[:, k, :], high[:, i, :], low[:, i, :], k == 0, k == KT - 1)
                                if half == 0:
                                    mark(mm)
                            g.end(mm)
                            g.used.append((g.group_done, g.total, EXP_GROUPS))
                        if c >= 1:
                            hidden_transposes(c - 1, g.begin("a", ("hidden", c - 1)))
                    last_hidden = g.begin("a", ("hidden", CHUNKS - 1))
                    halves = [g.begin("a", ("down", h)) for h in range(2)]
                    for d in range(DOWN):
                        if d % 2 == 0:
                            pe.wait_ge(g.hidden_split, e * CHUNKS + d // 2 + 1)
                        high, low = split(GATE_UP + d, 2)
                        for i in range(2):
                            f = 2 * d + i
                            for h in range(2):
                                n_ = slice(h * 512, (h + 1) * 512)
                                mm = parts(halves[h], he_high[:, f, :], he_low[:, f, :], high[:, i, n_], low[:, i, n_], f == 0, f == ET - 1)
                                if f == ET - 1:
                                    g.end(mm, ("down", h))
                        if d < DOWN - 1:
                            mark(mm)
                        if d == 1:
                            hidden_transposes(CHUNKS - 1, last_hidden)
                        elif d == 4:
                            gather(e + 1, "gather", range(4))
                        elif d == 5:
                            gather(e + 1, "gather", (4,))
                    g.used.append((g.group_done, g.total, EXP_GROUPS))
                    taken("a", ("down", 1))
                    for k in range(KT):
                        if k % 2 == 0:
                            bank = g.begin("v", ("scatter", k // 2))
                        mm = pe.matmul(bank[:, (k % 2) * SEQ:(k % 2 + 1) * SEQ], ye[:, k * P:(k + 1) * P],
                                       put[:, bass.ds(e, 1), :].rearrange("p o s -> p (o s)"), start=True, stop=True)
                        if k % 2 == 1:
                            g.end(mm)
                    taken("v", ("gather", 4))
                g.close(N_EXP)

            for l in range(DEPTH):
                mixer(l)
                attention(l)
                if l == 0:
                    feed_forward()
            routing()
            passes[:] = [G, Groups(pe, banks, more_done, more_took, more_loads)]
            for g, name in zip(passes, ("experts", "more")):
                Experts(g, sem, name)
            G.before_experts = G.freed[-1]
            experts(0)
            G.experts_done, G.given_moe = G.total, G.given["v"]
            pe.wait_ge(routing_ready, 1)
            with pe.If(pe.value_load(extra_flag[0:1, 0:1], min_val=0, max_val=1) > 0):
                for who in "va":
                    pe.wait_ge(took_sems[who], G.given[who])
                experts(1)
                for who in "va":
                    pe.wait_ge(more_took[who], passes[1].given[who])

            def mlstm():
                norm_sums("final_ms")
                norm_sums("norm1_ms")
                pe.wait_ge(x_ready, seen.next("x"))
                x = lambda k: xF[:, k, :]
                slot = G.tile()
                bank = G.begin("v", "gates")
                w = ring[:, slot, 0:KT * 16].rearrange("p (k n) -> p k n", k=KT)
                for b in range(TB):
                    for k in range(KT):
                        mm = pe.matmul(bank[:, 16 * b:16 * b + 16], xF[:, k, b * P:(b + 1) * P], w[:, k, :],
                                       start=(k == 0), stop=(k == KT - 1))
                G.end(mm)
                G.free()
                linear("xm", "a", 2, x, KT)
                pe.wait_ge(gates_ready, 1)
                transposes("v", "gate_rows", [(g * SEQ + b * P, gate_cols[:, b, g, :]) for g in range(2) for b in range(TB)])
                pe.wait_ge(xm_act, 1)
                for name, dst in (("qM", qM), ("kM", kM)):
                    slot = G.tile()
                    w = ring[:, slot, 0:8 * HD].rearrange("p (k n) -> p k n", k=8)
                    for h in range(HEADS):
                        bank = G.begin("a", (name, h))
                        for e in range(2):
                            for j in range(2):
                                mm = pe.matmul(bank[:, e * SEQ:(e + 1) * SEQ], w[:, 2 * h + j, e * P:(e + 1) * P],
                                               xm_conv[:, 2 * h + j, :], start=(j == 0), stop=(j == 1))
                        G.end(mm)
                    G.free()
                slot = G.tile()
                w = ring[:, slot, 0:8 * HD].rearrange("p (k n) -> p k n", k=8)
                for b in range(TB):
                    for hp in range(2):
                        bank = G.begin("v", ("vL", b, hp))
                        for i in range(2):
                            h = 2 * hp + i
                            for j in range(2):
                                mm = pe.matmul(bank[:, i * HD:(i + 1) * HD], xm_pad[:, 2 * h + j, 2 + b * P:2 + (b + 1) * P],
                                               w[:, 2 * h + j, :], start=(j == 0), stop=(j == 1))
                        G.end(mm)
                G.free()
                linear("o_pre", "a", 2, x, KT)
                pe.wait_ge(a_ready, 1)
                transposes("v", "a_cols", [(64 * b, g_a[:, b * P:(b + 1) * P]) for b in range(TB)])

                def scores(h):
                    pe.wait_ge(act_took, G.took["kM", HEADS - 1])
                    bank = G.begin("a", ("scoresT", h))
                    for sblk in range(2):
                        for j in range(2):
                            mm = pe.matmul(bank[:, sblk * SEQ:(sblk + 1) * SEQ], kM[:, 2 * h + j, sblk * P:(sblk + 1) * P],
                                           qM[:, 2 * h + j, :], start=(j == 0), stop=(j == 1))
                    G.end(mm)

                def maxima(i):
                    h, d = divmod(i, 2)
                    bank = G.begin("a", ("maxima", i))
                    s = head_sel[0:64, 4 * d + h, :]
                    pe.matmul(bank[:, 0:SEQ], s, g_max, start=True, stop=True)
                    G.end(pe.matmul(bank[:, SEQ:2 * SEQ], s, g_sum, start=True, stop=True))

                pe.wait_ge(sel_ready, 1)
                pe.wait_ge(dve_took, G.took["vL", TB - 1, 1])
                scores(0)
                maxima(0)
                for i in range(2 * HEADS):
                    h, d = divmod(i, 2)
                    if i + 1 < 2 * HEADS:
                        if d == 1:
                            scores(h + 1)
                        maxima(i + 1)
                    pe.wait_ge(intra_ready, i + 1)
                    reach = ((0, 0, 2), (1, 1, 2)) if d == 0 else ((1, 0, 2), (0, 0, 1))
                    bank = G.begin("v", ("den", i))
                    for n_, (sblk, lo, hi) in enumerate(reach):
                        mm = pe.matmul(bank[:, lo * P:hi * P], ones[:, :], intra[:, sblk, lo:hi, :], start=(n_ == 0), stop=(n_ == 1))
                    G.end(mm)
                    bank = G.begin("v", ("num", i))
                    for e in range(2):
                        for n_, (sblk, lo, hi) in enumerate(reach):
                            mm = pe.matmul(bank[:, e * SEQ + lo * P:e * SEQ + hi * P], vL[:, sblk, h * HD + e * P:h * HD + (e + 1) * P],
                                           intra[:, sblk, lo:hi, :], start=(n_ == 0), stop=(n_ == 1))
                    G.end(mm)
                linear("merge_m", "a", 2, x, KT)
                pe.wait_ge(sq_ready, seen.next("sq"))
                for g in range(2):
                    bank = G.begin("a", ("head_ms", g))
                    for i in range(2):
                        for j in range(2):
                            mm = pe.matmul(bank[:, i * SEQ:(i + 1) * SEQ], ones[:, :], squares[:, 4 * g + 2 * i + j, :],
                                           start=(j == 0), stop=(j == 1))
                    G.end(mm)

            def lru():
                x = lambda k: xF[:, k, :]
                linear("xl", "a", 2, x, KT)
                pe.wait_ge(ym_ready, 1)
                linear("branch_m", "v", 2, lambda k: hM[:, k, :], KT)
                linear("gate_l", "a", 2, x, KT)
                wr, wi = G.tile(), G.tile()
                pe.wait_ge(xl_conv_ready, 1)
                for d in range(2):
                    for name, slot in (("r", wr), ("i", wi)):
                        w = ring[:, slot, 0:16 * P].rearrange("p (k n) -> p k n", k=16)
                        for g in range(4):
                            bank = G.begin("a", (name, d, g))
                            for i in range(2):
                                mm = pe.matmul(bank[:, i * SEQ:(i + 1) * SEQ], w[:, 8 * d + 2 * g + i, :], xl_conv[:, 2 * g + i, :],
                                               start=True, stop=True)
                            G.end(mm)
                        if d == 1:
                            G.free()
                G.freed[-2] = G.freed[-1]

            def merge():
                x = lambda k: xF[:, k, :]
                linear("merge_l", "a", 2, x, KT)
                pe.wait_ge(yl_ready, 1)
                linear("branch_l", "v", 2, lambda k: h_l[:, k, :], KT)
                pe.wait_ge(merged_ready, 4)
                linear("w_out", "v", 2, lambda k: merged[:, k, :], KT)

            def peer():
                norm_sums("norm2_ms")
                pe.wait_ge(x_ready, seen.next("x"))
                linear("pq", "a", 4, lambda k: xF[:, k, :], KT)
                slot = G.tile()
                keys = ring[:, slot, 0:16 * P].rearrange("p (k c) -> p k c", k=16)
                for g in range(4):
                    transposes("v", ("keysT", g), [(i * P, keys[:, 4 * g + i, :]) for i in range(4)])
                G.free()
                pe.wait_ge(act_took, G.took["pq", 7])
                pe.wait_ge(dve_took, G.took["keysT", 3])
                for b in range(TB):
                    for g in range(4):
                        bank = G.begin("a", ("key_scores", b, g))
                        for i in range(4):
                            mm = pe.matmul(bank[:, i * P:(i + 1) * P], qP[:, 4 * g + i, b * P:(b + 1) * P], keysT[:, 4 * g + i, :],
                                           start=True, stop=True)
                        G.end(mm)
                for b in range(TB):
                    for half in range(2):
                        transposes("v", ("tokens", b, half), [(i * P, xF[:, 4 * half + i, b * P:(b + 1) * P]) for i in range(4)])
                for b in range(TB):
                    halves = [G.begin("a", ("out", b, half)) for half in range(2)]
                    for k in range(KT):
                        pe.matmul(halves[k // 4][:, (k % 4) * P:(k % 4 + 1) * P], hF[:, k, b * P:(b + 1) * P], ident[:, :],
                                  start=(k % 4 == 0), stop=False)
                    with pe.Fori(b * ROUNDS, (b + 1) * ROUNDS) as r:
                        for q in range(BATCHES):
                            pe.wait_ge(diag_ready, r * BATCHES + q + 1)
                            pe.wait_ge(gathered[q], r * GATHERED + GATHERED * ((b + 1) * ROUNDS + 1))
                            for j in range(BATCH - 1):
                                for half in range(2):
                                    mm = pe.matmul(halves[half], diag[:, q, j, :],
                                                   gathered_rows[:, q * BATCH + j, half * 512:(half + 1) * 512], start=False, stop=False)
                            mm.then_inc(mix_done, 1)
                    pe.wait_ge(zero_ready, 1)
                    for half in range(2):
                        G.end(pe.matmul(halves[half], ones[0:1, :], zero_row, start=False, stop=True), ("out", b, half))

            mlstm()
            lru()
            merge()
            peer()

        @block.sync
        def _(sp):
            n = resume = 0

            def load(*parts):
                nonlocal n
                slot = n % RING
                if n - resume >= RING:
                    sp.wait_ge(*G.freed[n - RING])
                for place, src in parts:
                    sp.dma_start(place(ring[:, slot, :]), src).then_inc(loads[slot], 16)
                n += 1

            def by_rows(w, kts=KT):
                return w.rearrange("(k p) n -> p k n", p=P)

            def block_of(kts, n, off=0):
                return lambda s: s[:, off:off + kts * n].rearrange("p (k n) -> p k n", k=kts)

            def matrix(w, cols_n=512):
                for c in range(0, w.shape[1], cols_n):
                    load((block_of(KT, cols_n), by_rows(w[:, c:c + cols_n])))

            for l in range(DEPTH):
                w = t["w_in"][l]
                b0 = 2 * A_W
                for first, width in ((A_W, A_W), (0, A_W), (b0 + BC_W, BC_W), (b0 + 2 * BC_W, BC_W), (b0, BC_W),
                                     (b0 + 4 * BC_W, BC_W), (b0 + 3 * BC_W, BC_W)):
                    load((block_of(KT, width), by_rows(w[:, first:first + width])))
                w = t["w_mix_out"][l]
                for c in range(2):
                    s = slice(c * 512, (c + 1) * 512)

                    def at(a, b, lo=0, hi=P):
                        return lambda s_: s_[lo:hi, a * 512:b * 512].rearrange("p (k n) -> p k n", k=b - a)
                    load((at(0, 5), by_rows(w[0:640, s])), (at(5, 6, 0, 64), w[640:704, s].rearrange("(k p) n -> p k n", k=1)),
                         (at(5, 6, 64, P), w[960:1024, s].rearrange("(k p) n -> p k n", k=1)), (at(6, 8), by_rows(w[704:960, s])))
                matrix(t["w_xkv"][l])
                matrix(t["w_xq"][l])
                matrix(t["w_xo"][l])
                if l == 0:
                    for c in range(FT // 2):
                        s = slice(c * 256, (c + 1) * 256)
                        load((block_of(KT, 256), by_rows(t["ffn_w_gate"][0][:, s])),
                             (block_of(KT, 256, SLOT_F // 2), by_rows(t["ffn_w_up"][0][:, s])))
                    for c in range(KT):
                        load((block_of(FT, P), by_rows(t["ffn_w_down"][0][:, c * P:(c + 1) * P])))
            def expert_tiles(g, e, first, last):
                gate, up, down = (t[n_][0].rearrange("e (k p) n -> p (e k) n", p=P) for n_ in ("moe_w_gate", "moe_w_up", "moe_w_down"))
                for j in range(first, last):
                    wait_used(sp, g, e, j)
                    if j < GATE_UP:
                        c, half = j // 4, j % 2
                        src = (gate, up)[j // 2 % 2][:, bass.ds(e * KT + half * (KT // 2), KT // 2), c * 512:(c + 1) * 512]
                    else:
                        src = down[:, bass.ds(e * ET + 2 * (j - GATE_UP), 2), :]
                    sp.dma_start(raw_tile(j).rearrange("p (k n) -> p k n", k=src.shape[1]), src).then_inc(g.loads[j % RING], 16)

            def experts(g):
                expert_tiles(g, 0, 0, RING)
                with sp.Fori(0, N_EXP - 1) as e:
                    expert_tiles(g, e, RING, EXP_TILES)
                    expert_tiles(g, e + 1, 0, RING)
                expert_tiles(g, N_EXP - 1, RING, EXP_TILES)

            resume = n
            sp.wait_ge(*G.before_experts)
            experts(G)
            more = passes[1]
            sp.wait_ge(routing_ready, 1)
            with sp.If(sp.value_load(extra_flag[0:1, 0:1], min_val=0, max_val=1) > 0):
                sp.wait_ge(group_done, G.experts_done)
                experts(more)
                sp.wait_ge(more_done, more.total)
            sp.wait_ge(group_done, G.experts_done)
            n0 = 2 * D
            w = t["w_in_2"][0]
            load((block_of(KT, 16), by_rows(w[:, n0:n0 + 16])))
            matrix(w[:, 0:D])
            for name in ("q", "k", "v"):
                load((block_of(8, HD), t["mlstm_w_" + name + "_2"][0].rearrange("h (j p) e -> p (h j) e", p=P)))
            matrix(w[:, D:2 * D])
            matrix(w[:, n0 + 16 + 2 * D:n0 + 16 + 3 * D])
            matrix(w[:, n0 + 16:n0 + 16 + D])
            matrix(t["w_branch_mlstm_2"][0])
            matrix(w[:, n0 + 16 + D:n0 + 16 + 2 * D])
            for name in ("r", "i"):
                load((block_of(16, P), t["lru_w_" + name + "_2"][0].rearrange("s n c d -> c (s n) d")))
            matrix(w[:, n0 + 16 + 3 * D:n0 + 16 + 4 * D])
            matrix(t["w_branch_lru_2"][0])
            matrix(t["w_out_2"][0])
            matrix(t["peer_w_q_2"][0])
            load((block_of(16, P), t["peer_sub_keys_2"][0].rearrange("h s n c -> n (h s) c")))
            sp.wait_ge(x_ready, N_NORMS + 1)
            sp.dma_start(final_gain, t["final_norm_g_2"].partition_broadcast(P)).then_inc(gain_loaded, 16)
            for b in range(TB):
                sp.wait_ge(final_out, b + 1)
                sp.dma_start(out[0, b * P:(b + 1) * P, :], final_rows[:, b, :]).then_inc(out_done, 16)
            sp.wait_ge(out_done, 16 * TB)

        @block.gpsimd
        def _(pool):
            step = Steps(pool, pool_step)
            step.then(pool.memset(ident[:, :], 0.0))
            step.then(pool.memset(tri[:, :], 1.0))
            step.then(pool.memset(lower[:, :], 1.0))
            step.then(pool.memset(half_ones[:, :], 0.0))
            step.then(pool.memset(pair_sel[:, :, :], 1.0))
            pool.memset(ones[:, :], 1.0)
            pool.memset(eps[:, :], EPS)
            pool.iota(iota[:, :], [[1, P]], base=0, channel_multiplier=0, allow_small_or_imprecise_dtypes=True)
            step.settle()
            pool.affine_select(out=ident[:, :], in_=ident[:, :], compare_op=ALU.not_equal, fill=1.0, base=0,
                               pattern=[[-1, P]], channel_multiplier=1)
            step.now(pool.affine_select(out=tri[:, :], in_=tri[:, :], compare_op=ALU.is_ge, fill=0.0, base=0,
                                        pattern=[[1, P]], channel_multiplier=-1))
            step.now(pool.affine_select(out=lower[:, :], in_=lower[:, :], compare_op=ALU.is_ge, fill=0.0, base=0,
                                        pattern=[[-1, P]], channel_multiplier=1))
            step.now(pool.memset(half_ones[0:64, 0:64], 1.0))
            step.now(pool.memset(half_ones[64:P, 64:P], 1.0))
            for lo, hi, base in ((0, 2, 0), (2, 3, BC_W - P)):
                s = pair_sel[:, lo:hi, :]
                step.now(pool.affine_select(out=s, in_=s, compare_op=ALU.is_ge, fill=0.0, base=base,
                                            pattern=[[P, hi - lo], [1, P]], channel_multiplier=-64))
                step.now(pool.affine_select(out=s, in_=s, compare_op=ALU.is_ge, fill=0.0, base=63 - base,
                                            pattern=[[-P, hi - lo], [-1, P]], channel_multiplier=64))
            pool.memset(small[:, 0:1], 0.0).then_inc(consts_ready, 1)
            pool.wait_ge(x_ready, N_NORMS)
            s = head_sel[0:64, :, :]
            step.now(pool.memset(s, 0.0))
            pool.affine_select(out=s, in_=s, compare_op=ALU.not_equal, fill=1.0, base=0,
                               pattern=[[-32, 2], [-1, 4], [0, P]], channel_multiplier=1).then_inc(sel_ready, 1)

            def rows_of(phase):
                b, of_v = divmod(phase, 2)
                table = t[("peer_u_2", "peer_v_2")[of_v]][0]

                def freed(v, r, q):
                    if v:
                        pool.wait_ge(mix_done, r * BATCHES + q + 1)
                        pool.sem_inc(pool_turn, 1)
                        pool.wait_ge(add_done, r * BATCHES + q + 1)
                    else:
                        pool.wait_ge(dot_done, r * BATCHES + q + 1)
                    pool.sem_inc(pool_turn, 1)

                def gather(r, q):
                    pool.tensor_copy(stage[:, q * BATCH:(q + 1) * BATCH], rows_at[:, bass.ds(r * GATHER + q * BATCH, BATCH)]
                                     ).then_inc(staged, 1)
                    before = b * ROUNDS + of_v * ROUNDS
                    pool.wait_ge(staged, r * BATCHES + before * BATCHES + q + 1)
                    pool.sem_inc(pool_turn, 1)
                    for j in range(q * BATCH, (q + 1) * BATCH):
                        pool.indirect_dma_start(out=gathered_rows[:, j, :], out_offset=None, in_=table,
                                                in_offset=bass.IndirectOffsetOnAxis(ap=stage[:, j:j + 1], axis=0)
                                                ).then_inc(gathered[q], 16)

                for q in range(BATCHES):
                    if phase:
                        freed(not of_v, (b + of_v) * ROUNDS - 1, q)
                    gather(b * ROUNDS, q)
                with pool.Fori(b * ROUNDS + 1, (b + 1) * ROUNDS) as r:
                    for q in range(BATCHES):
                        freed(of_v, r - 1, q)
                        gather(r, q)

            pool.wait_ge(group_done, G.after["keysT", 3])
            for b in range(TB):
                pool.wait_ge(index_ready, b + 1)
                rows_of(2 * b)
                rows_of(2 * b + 1)

        @block.scalar
        def _(act):
            seen = Tally()
            step = Steps(act, act_step)

            def ready(key):
                act.wait_ge(group_done, G.after[key])

            def take(ins):
                ins.then_inc(act_took, 1)

            act.dma_start(x_in, t["x"].rearrange("o (b p) d -> p (o b) d", p=P)).then_inc(inputs_loaded, 16)
            act.dma_start(mem_in, t["mem"].rearrange("o (b p) d -> p (o b) d", p=P)).then_inc(inputs_loaded, 16)
            sent = 0

            def param(dst, src):
                nonlocal sent
                act.dma_start(dst, src).then_inc(params_loaded, 16)
                sent += 1

            def vec(r, set_, src):
                n = src.shape[0] // P
                param(rows[r:r + n, set_, :], src.rearrange("(k c) -> k c", c=P))

            for l in range(DEPTH):
                r = 49 * l
                vec(r + MIX_G, 0, t["norm_mix_g"][l])
                vec(r + X_G, 0, t["norm_x_g"][l])
                vec(r + MEM_G, 0, t["norm_mem_g"][l])
                vec(r + FFN_G, 0, t["norm_ffn_g"][l])
                g = t["mix_out_g"][l]
                vec(r + OUT_G, 0, g[0:640])
                param(rows[r + OUT_G + 5:r + OUT_G + 6, 0, 0:64], g[640:704].rearrange("(k c) -> k c", k=1))
                param(rows[r + OUT_G + 5:r + OUT_G + 6, 0, 64:P], g[960:1024].rearrange("(k c) -> k c", k=1))
                vec(r + OUT_G + 6, 0, g[704:960])
                vec(r + CONVA_B, 0, t["conv_a_b"][l])
                vec(r + LNA_G, 0, t["ln_a_g"][l])
                vec(r + LNA_B, 0, t["ln_a_b"][l])
                param(rows[0:93, 1 + l, :], t["conv_a_w"][l].rearrange("j (k c) -> (j k) c", c=P))
                param(bc_rows[5 * l:5 * l + 3, :], t["conv_b_w"][l])
                param(bc_rows[5 * l + 3:5 * l + 4, :], t["ln_c_g"][l].rearrange("(k c) -> k c", k=1))
                param(bc_rows[5 * l + 4:5 * l + 5, :], t["ln_c_b"][l].rearrange("(k c) -> k c", k=1))
                param(gate_bias[:, l, :], t["gmlp_b"][l])
                param(spatial_in[:, l, :, :], t["gmlp_ws"][l].rearrange("g i j -> i g j"))
            for r, name in ((N1_G, "norm1_g_2"), (MC_B, "mlstm_conv_b_2"), (MN_G, "mlstm_norm_g_2"), (LC_B, "lru_conv_b_2"),
                            (N2_G, "norm2_g_2")):
                vec(r, 3, t[name][0])
            for r, name in ((BR, "lru_b_r_2"), (BI, "lru_b_i_2"), (LAM, "lru_lambda_2")):
                param(rows[r:r + 16, 3, :], t[name][0].rearrange("s (k c) -> (s k) c", c=P))
            param(rows[MC_W:MC_W + 32, 3, :], t["mlstm_conv_w_2"][0].rearrange("j (k c) -> (j k) c", c=P))
            param(rows[LC_W:LC_W + 32, 4, :], t["lru_conv_w_2"][0].rearrange("j (k c) -> (j k) c", c=P))
            vec(FIN_G, 4, t["norm_final_g"])
            param(router[:, :, :], t["moe_router"][0].rearrange("(k p) e -> p k e", p=P))
            param(gate_row, t["b_gates_2"][0].partition_broadcast(P))
            assert sent == N_PARAMS, sent

            def square(src, n=KT):
                act.activation(squares[:, 0:n, :], src, ACT.Square).then_inc(sq_ready, 1)

            def std(key, n, rows_=P):
                ready(key)
                take(act.activation(std_row[:, :], banks_of(key)[:, 0:SEQ], ACT.Sqrt, bias=EPS_AP, scale=1.0 / n))

            def banks_of(key):
                return banks["a"][(G.took[key] - 1) % 4]

            def norm(key, h_taken):
                act.wait_ge(dve_took, h_taken)
                square(hF[:, :, :])
                std(key, D)

            for g in range(4):
                ready(("mem", g))
                take(act.activation(mem_hat[:, 2 * g:2 * g + 2, :], pair(banks_of(("mem", g))), ACT.Copy))
            for l in range(DEPTH):
                ready(("spatial", l, 0))
                take(act.activation(spatialT[:, l, 0:4, :], pair(banks_of(("spatial", l, 0)), 4, P), ACT.Copy))
            ready("spatial_last")
            take(act.activation(spatialT[:, :, 4, :], pair(banks_of("spatial_last"), DEPTH, P), ACT.Copy))
            act.wait_ge(act_took, G.took["mem", 3])
            square(mem_hat)
            std("mem_ms", D)
            act.wait_ge(mem_normed, 1)

            def mixer(l):
                norm(("mix_ms", l), G.took["cols"] if l == 0 else G.took["ffn_down", 3])

                def section(name, dst, func, ms, lo=0):
                    for g in range(2):
                        ready((name, l, g))
                        bank = banks_of((name, l, g))
                        if g == 0:
                            take(act.activation(dst[:, 0:2, :], pair(bank), func))
                        else:
                            take(act.activation(dst[lo:ms, 2, :], bank[lo:ms, 0:SEQ], func))

                section("a_gate", sig_a, ACT.Sigmoid, P)
                section("c_gate", c_gate, ACT.Copy, 64)
                section("b_gate", b_gate, ACT.Copy, 64)
                section("c_v", c_v, ACT.Gelu_apprx_tanh, 64)
                section("c_u", c_u, ACT.Gelu_apprx_tanh, P, 64)

                def layer_norm(name, n, src, last64):
                    ready((name + "_mean", l))
                    take(act.activation(mean_row[:, :], banks_of((name + "_mean", l))[:, 0:SEQ], ACT.Copy, scale=-1.0 / n))
                    act.wait_ge(centred, seen.next("centred"))
                    if last64:
                        step.then(act.activation(squares[:, 0:2, :], src[:, 0:2, :], ACT.Square))
                        act.activation(squares[0:64, 2, :], src[0:64, 2, :], ACT.Square).then_inc(sq_ready, 1)
                    else:
                        square(src, 3)
                    std((name + "_var", l), n)

                layer_norm("c", BC_W, c_v, True)
                layer_norm("a", A_W, conv_a, False)
                act.wait_ge(ln_ready, l + 1)
                for k in range(3):
                    ins = act.activation(yF[:, k, :], conv_a[:, k, :], ACT.Silu, scale=c_vec(l, LNA_G, k), bias=c_vec(l, LNA_B, k))
                ins.then_inc(ya_ready, 1)
                act.wait_ge(ya_ready, l + 1)
                act.wait_ge(y_all, l + 1)
                square(yF)
                for g in range(4):
                    ready(("group_ms", l, g))
                    take(act.activation(std8[:, 2 * g:2 * g + 2, :], pair(banks_of(("group_ms", l, g))), ACT.Sqrt,
                                        bias=EPS_AP, scale=1.0 / 64))

            def copies(key, dst, n=4, func=ACT.Copy, scale=1.0):
                for g in range(n):
                    ready((key, g))
                    take(act.activation(dst[:, 2 * g:2 * g + 2, :], pair(banks_of((key, g))), func, scale=scale))

            def attention(l):
                copies(("k", l), kF)
                for half in range(2):
                    for b in range(TB):
                        ready(("v", l, half, b))
                        take(act.activation(vM[:, b, half * 512:(half + 1) * 512], banks_of(("v", l, half, b))[:, :], ACT.Copy))
                norm(("x_ms", l), G.took[("mix_out", l), 3])
                copies(("q", l), qF)
                for h in range(HEADS):
                    act.wait_ge(max_ready, HEADS * l + h + 1)
                    bank = banks_of(("scores", l, h))
                    for b in range(TB):
                        c = h * TB + b
                        ins = act.activation(probs[:, h, b, :], bank[:, b * SEQ:(b + 1) * SEQ], ACT.Exp, bias=small[:, c:c + 1],
                                             scale=HD ** -0.5, accum_out=small[:, 8 + c:9 + c])
                    take(ins)
                for h in range(HEADS):
                    ready(("o", l, h))
                    take(act.activation(oF[:, 2 * h:2 * h + 2, :], pair(banks_of(("o", l, h))), ACT.Copy))

            def feed_forward():
                norm("ffn_ms", G.took[("xo", 0), 3])
                for c in range(FT // 2):
                    ready(("ffn", 0, c))
                    if c >= 2:
                        act.wait_ge(dve_took, G.took["ffn", 1, c - 2])
                    take(act.activation(sil[:, c % 2, :, :], pair(banks_of(("ffn", 0, c))), ACT.Silu))

            def routing():
                norm("moe_ms", G.took[("xo", 1), 3])
                for b in range(TB):
                    for half in range(2):
                        ready(("xT", b, half))
                        take(act.activation(xT[:, b, half * 512:(half + 1) * 512], banks_of(("xT", b, half))[:, :], ACT.Copy))
                act.wait_ge(gap_ready, 1)
                act.activation(ratio, gap, ACT.Exp).then_inc(ratio_ready, 1)

            def experts(n):
                g = passes[n]

                def bank_in(key):
                    return banks["a"][(g.took[key] - 1) % 4]

                def took_it(ins):
                    ins.then_inc(g.took_sems["a"], 1)

                for e in range(4, N_EXP):
                    act.wait_ge(g.group_done, g.after["put", e])
                    took_it(act.activation(put[:, e, :], bank_in(("put", e))[:, 0:SEQ], ACT.Copy))
                def round_tile(e, j):
                    wait_used(act, g, e, j)
                    act.wait_ge(g.loads[j % RING], g.loaded0[j % RING] + 16 * (j // RING + 1) + e * (16 * EXP_TILES // RING))
                    act.activation(high_tile(j), raw_tile(j), ACT.Copy).then_inc(g.high, 1)

                def expert(e, follow):
                    def done(key):
                        act.wait_ge(g.group_done, g.after[key] + e * EXP_GROUPS)

                    def gate(c):
                        done(("gate", c))
                        took_it(act.activation(he[:, c % 2, :], bank_in(("gate", c))[:, :], ACT.Silu))

                    def hidden(c):
                        done(("hidden", c))
                        s, bank = slice(4 * c, 4 * c + 4), pair(bank_in(("hidden", c)), 4, P)
                        act.activation(he_high[:, s, :], bank, ACT.Copy)
                        took_it(act.activation(he_all[:, s, :], bank, ACT.Copy))

                    for j in range(EXP_TILES):
                        if j + AHEAD < EXP_TILES:
                            round_tile(e, j + AHEAD)
                        elif follow:
                            round_tile(e + 1, j + AHEAD - EXP_TILES)
                        if j < GATE_UP and j % 4 == 1:
                            gate(j // 4)
                        elif j <= GATE_UP and j >= 8 and j % 4 == 0:
                            hidden(j // 4 - 2)
                        elif j == GATE_UP + 2:
                            hidden(CHUNKS - 1)
                    for h in range(2):
                        done(("down", h))
                        took_it(act.activation(ye[:, h * 512:(h + 1) * 512], bank_in(("down", h))[:, :], ACT.Copy))

                if n == 0:
                    act.wait_ge(*G.before_experts)
                else:
                    act.wait_ge(group_done, G.experts_done)
                for j in range(AHEAD):
                    round_tile(0, j)
                with act.Fori(0, N_EXP - 1) as e:
                    expert(e, True)
                expert(N_EXP - 1, False)

            for l in range(DEPTH):
                mixer(l)
                attention(l)
                if l == 0:
                    feed_forward()
            routing()
            experts(0)
            act.wait_ge(routing_ready, 1)
            with act.If(act.value_load(extra_flag[0:1, 0:1], min_val=0, max_val=1) > 0):
                experts(1)
                act.wait_ge(more_took["v"], passes[1].given["v"])

            def mlstm():
                norm("final_ms", G.given_moe)
                act.wait_ge(final_ready, 1)
                square(hF[:, :, :])
                std("norm1_ms", D)
                act.wait_ge(abs_ready, 1)
                act.activation(lam_t, lam_t, ACT.Exp, scale=-1.0).then_inc(exp_done, 1)
                for g in range(4):
                    ready(("xm", g))
                    take(act.activation(xm_pad[:, 2 * g:2 * g + 2, 2:2 + SEQ], pair(banks_of(("xm", g))), ACT.Copy))
                act.wait_ge(abs_ready, 2)
                act.activation(g_t, g_t, ACT.Exp, scale=-1.0).then_inc(exp_done, 1)
                act.wait_ge(xm_conv_ready, 1)
                act.activation(xm_conv, xm_conv, ACT.Silu).then_inc(xm_act, 1)
                for name, dst, scale in (("qM", qM, 1.0), ("kM", kM, HD ** -0.5)):
                    copies(name, dst, scale=scale)
                copies("o_pre", o_sig, func=ACT.Sigmoid)

                def scores(h):
                    ready(("scoresT", h))
                    take(act.activation(scoresT[:, h % 2, :, :, :].rearrange("p s t j -> p (s t j)"),
                                        banks_of(("scoresT", h))[:, :], ACT.Copy))

                def maxima(i):
                    act.wait_ge(arg_ready, i + 1)
                    for sblk, lo, hi in (((0, 0, 2), (1, 1, 2)) if i % 2 == 0 else ((1, 0, 2), (0, 0, 1))):
                        a = decay[:, sblk, lo:hi, :]
                        act.activation(a, a, ACT.Exp, scale=-1.0)
                    take(act.activation(floor_[:, i % 2, :], banks_of(("maxima", i))[:, SEQ:2 * SEQ], ACT.Exp, scale=-1.0))

                scores(0)
                maxima(0)
                for i in range(2 * HEADS - 1):
                    if i % 2 == 1:
                        scores(i // 2 + 1)
                    maxima(i + 1)
                copies("merge_m", g_m, func=ACT.Sigmoid)
                act.wait_ge(h_sum_ready, 1)
                square(hM)
                for g in range(2):
                    ready(("head_ms", g))
                    take(act.activation(std4[:, 2 * g:2 * g + 2, :], pair(banks_of(("head_ms", g))), ACT.Sqrt, bias=EPS_AP, scale=1.0 / HD))

            def lru():
                for g in range(4):
                    ready(("xl", g))
                    take(act.activation(xl_pad[:, 2 * g:2 * g + 2, 2:2 + SEQ], pair(banks_of(("xl", g))), ACT.Copy))
                act.wait_ge(dve_took, G.took["branch_m", 3])
                copies("gate_l", gate_l, func=ACT.Gelu)
                for d in range(2):
                    act.wait_ge(lru_free, d + 1)
                    for name, dst, bias in (("r", lru_a, BR), ("i", lru_u, BI)):
                        for g in range(4):
                            ready((name, d, g))
                            for i in range(2):
                                k = 2 * g + i
                                ins = act.activation(dst[:, k, :], banks_of((name, d, g))[:, i * SEQ:(i + 1) * SEQ], ACT.Sigmoid,
                                                     bias=col(C2 + bias + 8 * d + k))
                            take(ins)
                    act.wait_ge(lam_ready, 1)
                    act.wait_ge(act_took, G.took["r", d, 3])
                    for k in range(KT):
                        step.then(act.activation(lru_t[:, k, :], lru_a[:, k, :], ACT.Tanh, scale=lam_pos[:, 8 * d + k:8 * d + k + 1]))
                    step.settle()
                    for k in range(KT):
                        ins = act.activation(lru_a[:, k, :], lru_a[:, k, :], ACT.Exp, scale=lam_neg[:, 8 * d + k:8 * d + k + 1])
                    ins.then_inc(lru_a_ready, 1)
                    act.wait_ge(lru_v_ready, d + 1)
                    act.activation(lru_t[:, :, :], lru_t[:, :, :], ACT.Sqrt).then_inc(lru_s_ready, 1)

            def merge():
                act.wait_ge(gated_ready, 2)
                copies("merge_l", g_l, func=ACT.Sigmoid)

            def peer():
                norm("norm2_ms", G.took["w_out", 3])
                copies("pq", qP, 8)

                def scores(b):
                    for g in range(4):
                        ready(("key_scores", b, g))
                        take(act.activation(key_scores[:, 4 * g:4 * g + 4, :], pair(banks_of(("key_scores", b, g)), 4, P), ACT.Copy))

                def margins(b):
                    act.wait_ge(margin_ready, b + 1)
                    act.activation(gates[:, b, :, :], gates[:, b, :, :], ACT.Exp).then_inc(margin_exp, 1)

                def activations(b):
                    act.wait_ge(dots_kept, (b + 1) * ROUNDS)
                    s = acts[:, b * SLOTS:(b + 1) * SLOTS]
                    act.activation(s, s, ACT.Gelu).then_inc(act_ready, 1)

                def final(b):
                    act.wait_ge(v_summed, b + 1)
                    step.now(act.activation(final_sq, v_sum, ACT.Square, accum_out=final_ss[:, b:b + 1]))
                    act.activation(final_std[:, b:b + 1], final_ss[:, b:b + 1], ACT.Sqrt, bias=EPS_AP, scale=1.0 / D).then_inc(final_std_ready, 1)

                scores(0)
                margins(0)
                act.wait_ge(index_ready, 1)
                scores(1)
                activations(0)
                margins(1)
                final(0)
                activations(1)
                final(1)

            mlstm()
            lru()
            merge()
            peer()

        @block.vector
        def _(dve):
            seen = Tally()
            step = Steps(dve, dve_step)

            def ready(key):
                dve.wait_ge(group_done, G.after[key])

            def bank_of(key):
                return banks["v"][(G.took[key] - 1) % 4]

            def take(ins):
                ins.then_inc(dve_took, 1)

            def scaled(dst, src, gain, sem_):
                step.now(dve.reciprocal(rstd_row[:, :], std_row[:, :]))
                for k in range(KT):
                    ins = dve.scalar_tensor_tensor(dst[:, k, :], src[:, k, :], gain(k), rstd_row[:, :], ALU.mult, ALU.mult)
                    if k < KT - 1:
                        step.then(ins)
                ins.then_inc(sem_, 1)

            def norm(key, gain):
                dve.wait_ge(act_took, G.took[key])
                scaled(xF, hF, gain, x_ready)

            def add_to_residual(key, n=4):
                for g in range(n):
                    ready((key, g))
                    s = hF[:, 2 * g:2 * g + 2, :]
                    take(dve.tensor_tensor(s, pair(bank_of((key, g))), s, ALU.add))

            def conv(dst, src, taps, weight, bias, tiles):
                for j in range(taps):
                    for k, m in tiles:
                        a = src(k, j)
                        if j == 0 and bias is not None:
                            ins = dve.tensor_scalar(dst[0:m, k, :], a, weight(k, j), bias(k), ALU.mult, ALU.add)
                        elif j == 0:
                            ins = dve.tensor_scalar(dst[0:m, k, :], a, weight(k, j), None, ALU.mult)
                        else:
                            step.settle(len(tiles) - 1)
                            ins = dve.scalar_tensor_tensor(dst[0:m, k, :], a, weight(k, j), dst[0:m, k, :], ALU.mult, ALU.add)
                        step.then(ins)
                step.settle()

            for g in range(4):
                ready(("x", g))
                take(dve.tensor_copy(hF[:, 2 * g:2 * g + 2, :], pair(bank_of(("x", g)))))
            ready("cols")
            step.then(dve.tensor_copy(cols[:, 0:C4 + 20], bank_of("cols")[:, 0:C4 + 20]))
            take(dve.tensor_copy(cols[0:64, C4 + 20:C4 + 30], bank_of("cols")[0:64, C4 + 20:C4 + 30]))
            dve.wait_ge(dve_took, G.took["cols"])
            dve.wait_ge(act_took, G.took["spatial_last"])
            dve.memset(spatialT[64:P, :, :, 0:64], 0.0).then_inc(mask_ready, 1)
            dve.wait_ge(act_took, G.took["mem_ms"])
            step.now(dve.reciprocal(rstd_row[:, :], std_row[:, :]))
            dve.tensor_tensor(mem_hat, mem_hat, rstd_row[:, :].unsqueeze(1).to_broadcast([P, KT, SEQ]), ALU.mult).then_inc(mem_normed, 1)

            def mixer(l):
                norm(("mix_ms", l), lambda k: c_vec(l, MIX_G, k))
                step.then(dve.memset(ya_pad[:, :, 0:A_TAPS - 1], 0.0))
                step.then(dve.memset(yb_pad[:, :, 0:B_TAPS - 1], 0.0))
                dve.wait_ge(act_took, G.took["a_gate", l, 1])
                ready(("a_val", l, 0))
                take(dve.tensor_tensor(ya_pad[:, 0:2, A_TAPS - 1:], pair(bank_of(("a_val", l, 0))), sig_a[:, 0:2, :], ALU.mult))
                ready(("a_val", l, 1))
                take(dve.tensor_tensor(ya_pad[:, 2, A_TAPS - 1:], bank_of(("a_val", l, 1))[:, 0:SEQ], sig_a[:, 2, :], ALU.mult))
                dve.wait_ge(dve_took, G.took["a_val", l, 1])
                step.settle()
                conv(conv_a, lambda k, j: ya_pad[:, k, j:j + SEQ], A_TAPS, lambda k, j: col(C1 + 93 * l + 3 * j + k),
                     lambda k: c_vec(l, CONVA_B, k), ((0, P), (1, P), (2, P)))
                dve.engine_nop().then_inc(conv_ready, 1)
                dve.wait_ge(act_took, G.took["c_gate", l, 1])
                ready(("b_in", l, 0))
                take(dve.tensor_tensor(yb_pad[:, 0:2, B_TAPS - 1:], pair(bank_of(("b_in", l, 0))), c_gate[:, 0:2, :], ALU.mult))
                ready(("b_in", l, 1))
                take(dve.tensor_tensor(yb_pad[0:64, 2, B_TAPS - 1:], bank_of(("b_in", l, 1))[0:64, 0:SEQ], c_gate[0:64, 2, :], ALU.mult))
                dve.wait_ge(dve_took, G.took["b_in", l, 1])
                tiles = ((0, P), (1, P), (2, 64))
                conv(conv_b, lambda k, j: yb_pad[0:(P if k < 2 else 64), k, j:j + SEQ], B_TAPS, lambda k, j: bc_col(l, j, k), None, tiles)
                dve.wait_ge(act_took, G.took["b_gate", l, 1])
                step.then(dve.tensor_tensor(yF[:, 3:5, :], b_gate[:, 0:2, :], conv_b[:, 0:2, :], ALU.mult))
                step.then(dve.tensor_tensor(yF[0:64, 5, :], b_gate[0:64, 2, :], conv_b[0:64, 2, :], ALU.mult))

                def wide(ap, n):
                    return ap.unsqueeze(1).to_broadcast([P, n, SEQ])

                dve.wait_ge(act_took, G.took["c_mean", l])
                step.then(dve.tensor_tensor(c_v[:, 0:2, :], c_v[:, 0:2, :], wide(mean_row[:, :], 2), ALU.add))
                dve.tensor_tensor(c_v[0:64, 2, :], c_v[0:64, 2, :], mean_row[0:64, :], ALU.add).then_inc(centred, 1)
                dve.wait_ge(act_took, G.took["c_var", l])
                dve.wait_ge(centred, seen.next("centred"))
                step.now(dve.reciprocal(rstd_row[:, :], std_row[:, :]))
                for k, m in tiles:
                    step.then(dve.scalar_tensor_tensor(c_v[0:m, k, :], c_v[0:m, k, :], bc_col(l, 3, k), rstd_row[0:m, :], ALU.mult, ALU.mult))
                step.settle()
                for k, m in tiles:
                    ins = dve.tensor_scalar(c_v[0:m, k, :], c_v[0:m, k, :], bc_col(l, 4, k), None, ALU.add)
                    if k < 2:
                        step.then(ins)
                ins.then_inc(cv_ready, 1)
                for b in range(TB):
                    ready(("c_vT", l, b))
                    take(dve.tensor_copy(vT[:, b, :], bank_of(("c_vT", l, b))[:, 0:BC_W]))
                dve.wait_ge(act_took, G.took["c_u", l, 1])
                for p in range(3):
                    for b in range(TB):
                        ready(("mixed", l, p, b))
                        bank = bank_of(("mixed", l, p, b))
                        s = slice(b * P, (b + 1) * P)
                        if p < 2:
                            step.then(dve.tensor_tensor(yF[0:64, 6 + p, s], bank[0:64, 0:P], c_u[0:64, p, s], ALU.mult))
                            take(dve.tensor_tensor(yF[64:P, 6 + p, s], bank[64:P, P:2 * P], c_u[64:P, p, s], ALU.mult))
                        else:
                            take(dve.tensor_tensor(yF[64:P, 5, s], bank[64:P, 0:P], c_u[64:P, 2, s], ALU.mult))
                dve.engine_nop().then_inc(y_all, 1)
                dve.wait_ge(act_took, G.took["a_mean", l])
                dve.tensor_tensor(conv_a, conv_a, wide(mean_row[:, :], 3), ALU.add).then_inc(centred, 1)
                dve.wait_ge(act_took, G.took["a_var", l])
                dve.wait_ge(centred, seen.next("centred"))
                step.now(dve.reciprocal(rstd_row[:, :], std_row[:, :]))
                dve.tensor_tensor(conv_a, conv_a, wide(rstd_row[:, :], 3), ALU.mult).then_inc(ln_ready, 1)
                dve.wait_ge(act_took, G.took["group_ms", l, 3])
                dve.wait_ge(ya_ready, l + 1)
                dve.wait_ge(dve_took, G.took["mixed", l, 2, 1])
                step.now(dve.reciprocal(std8, std8))
                for k in range(KT):
                    ins = dve.scalar_tensor_tensor(yF[:, k, :], yF[:, k, :], c_vec(l, OUT_G, k), std8[:, k, :], ALU.mult, ALU.mult)
                    if k < KT - 1:
                        step.then(ins)
                ins.then_inc(y_ready, 1)
                add_to_residual(("mix_out", l))

            def attention(l):
                dve.wait_ge(mem_normed, 1)
                for k in range(KT):
                    ins = dve.tensor_scalar(mem_g[:, k, :], mem_hat[:, k, :], c_vec(l, MEM_G, k), None, ALU.mult)
                    if k < KT - 1:
                        step.then(ins)
                ins.then_inc(mem_ready, 1)
                norm(("x_ms", l), lambda k: c_vec(l, X_G, k))
                for h in range(HEADS):
                    ready(("scores", l, h))
                    bank = banks["a"][(G.took["scores", l, h] - 1) % 4]
                    s = small[:, h * TB:(h + 1) * TB]
                    step.now(dve.tensor_reduce(s, pair(bank), AX.X, ALU.max))
                    dve.tensor_scalar(s, s, -(HD ** -0.5), None, ALU.mult).then_inc(max_ready, 1)
                for h in range(HEADS):
                    dve.wait_ge(act_took, G.took["scores", l, h])
                    r = small[:, 16 + h * TB:16 + (h + 1) * TB]
                    step.now(dve.reciprocal(r, small[:, 8 + h * TB:8 + (h + 1) * TB]))
                    for b in range(TB):
                        ins = dve.tensor_scalar(probs[:, h, b, :], probs[:, h, b, :], r[:, b:b + 1], None, ALU.mult)
                        if b < TB - 1:
                            step.then(ins)
                    ins.then_inc(probs_ready, 1)
                for h in range(HEADS):
                    ready(("probsT", l, h))
                    take(dve.tensor_copy(probsT[:, h, :, :], pair(bank_of(("probsT", l, h)))))
                add_to_residual(("xo", l))

            def feed_forward():
                norm("ffn_ms", lambda k: c_vec(0, FFN_G, k))
                for c in range(FT // 2):
                    ready(("ffn", 1, c))
                    dve.wait_ge(act_took, G.took["ffn", 0, c])
                    take(dve.tensor_tensor(hid[:, 2 * c:2 * c + 2, :], pair(bank_of(("ffn", 1, c))), sil[:, c % 2, :, :], ALU.mult))
                add_to_residual("ffn_down")

            def routing():
                norm("moe_ms", lambda k: c_vec(1, FFN_G, k))
                ready("logits")
                b8 = bank_of("logits")[:, 0:TB * N_EXP].rearrange("p (b e) -> p b e", b=TB)
                take(dve.tensor_copy(logits, b8))
                dve.wait_ge(dve_took, G.took["logits"])
                for b in range(TB):
                    step.then(dve.max(top[:, b, :], logits[:, b, :]))
                step.settle()
                for b in range(TB):
                    step.then(dve.max_index(top_raw[:, b, :], top[:, b, :], logits[:, b, :]))
                step.settle()
                step.then(dve.tensor_copy(top_at, top_raw))
                dve.tensor_tensor(gap, top[:, :, 1], top[:, :, 0], ALU.subtract).then_inc(gap_ready, 1)
                step.settle()
                for b in range(TB):
                    for i, m in ((0, first), (1, second)):
                        step.then(dve.tensor_scalar(m[:, b, :], iota[:, 0:N_EXP], top_at[:, b, i:i + 1], None, ALU.is_equal))
                step.settle()
                dve.tensor_tensor(chosen, first, second, ALU.add).then_inc(chosen_ready, 1)
                dve.wait_ge(ratio_ready, 1)
                step.now(dve.tensor_scalar(total_w, ratio, 1.0, None, ALU.add))
                step.now(dve.reciprocal(w_first, total_w))
                step.now(dve.tensor_tensor(w_second, w_first, ratio, ALU.mult))
                for b in range(TB):
                    step.now(dve.tensor_scalar(share[:, b, :], first[:, b, :], w_first[:, b:b + 1], None, ALU.mult))
                    step.now(dve.scalar_tensor_tensor(share[:, b, :], second[:, b, :], w_second[:, b:b + 1], share[:, b, :], ALU.mult, ALU.add))
                ready("places")
                dve.wait_ge(chosen_ready, 1)
                bank = bank_of("places")
                p8 = bank[:, 0:TB * N_EXP].rearrange("p (b e) -> p b e", b=TB)
                step.now(dve.tensor_tensor(place, p8, chosen, ALU.mult))
                step.then(dve.tensor_scalar(place, place, -1.0, None, ALU.add))
                step.now(dve.tensor_reduce(most, bank[:, 2 * N_EXP:3 * N_EXP], AX.X, ALU.max))
                take(dve.tensor_scalar(extra_flag[:, 0:1], most, float(P), None, ALU.is_gt))
                dve.wait_ge(dve_took, G.took["places"])
                dve.engine_nop().then_inc(routing_ready, 1)

            def experts(n):
                g = passes[n]

                def bank_in(key):
                    return banks["v"][(g.took[key] - 1) % 4]

                def took_it(ins):
                    ins.then_inc(g.took_sems["v"], 1)

                if n:
                    dve.tensor_scalar(place, place, -float(P), None, ALU.add).then_inc(more_places, 1)
                    dve.wait_ge(more_places, 1)
                dve.memset(pick[:, :, N_EXP, :], 0.0)
                for scale, dst, sem_ in ((True, weighted, weighted_ready), (False, pick, pick_ready)):
                    for b in range(TB):
                        for e in range(N_EXP):
                            if scale:
                                ins = dve.tensor_scalar(dst[:, b, e, :], iota[:, :], place[:, b, e:e + 1], share[:, b, e:e + 1],
                                                        ALU.is_equal, ALU.mult)
                            else:
                                ins = dve.tensor_scalar(dst[:, b, e, :], iota[:, :], place[:, b, e:e + 1], None, ALU.is_equal)
                    ins.then_inc(sem_, 1)
                for e in range(4):
                    dve.wait_ge(g.group_done, g.after["put", e])
                    took_it(dve.tensor_copy(put[:, e, :], bank_in(("put", e))[:, 0:SEQ]))
                def low_part(e, j):
                    dve.wait_ge(g.high, e * EXP_TILES + j + 1)
                    dve.tensor_tensor(low_tile(j), raw_tile(j), high_tile(j).bitcast(F32), ALU.subtract).then_inc(g.split, 1)

                def gathered_tokens(n_, key, done):
                    for i, (k, m) in enumerate(((0, 2), (2, 2), (4, 2), (6, 1), (7, 1))):
                        done((key, i))
                        bank = pair(bank_in((key, i)), m, P)
                        dve.tensor_copy(xe_high[:, k:k + m, :], bank).then_inc(g.x_high, 1)
                        dve.wait_ge(g.x_high, n_ * 5 + i + 1)
                        took_it(dve.tensor_tensor(xe_low[:, k:k + m, :], bank, xe_high[:, k:k + m, :].bitcast(F32), ALU.subtract))

                def expert(e, follow):
                    def done(key):
                        dve.wait_ge(g.group_done, g.after[key] + e * EXP_GROUPS)

                    def up(c):
                        done(("up", c))
                        dve.wait_ge(g.took_sems["a"], g.took["gate", c] + e * EXP_A)
                        s = he[:, c % 2, :]
                        took_it(dve.tensor_tensor(s, bank_in(("up", c))[:, :], s, ALU.mult))

                    def hidden(c):
                        dve.wait_ge(g.took_sems["a"], g.took["hidden", c] + e * EXP_A)
                        s = slice(4 * c, 4 * c + 4)
                        dve.tensor_tensor(he_low[:, s, :], he_all[:, s, :], he_high[:, s, :].bitcast(F32), ALU.subtract).then_inc(g.hidden_split, 1)

                    for j in range(EXP_TILES):
                        if j + AHEAD < EXP_TILES:
                            low_part(e, j + AHEAD)
                        elif follow:
                            low_part(e + 1, j + AHEAD - EXP_TILES)
                        if j < GATE_UP and j % 4 == 3:
                            up(j // 4)
                        elif j <= GATE_UP + 1 and j >= 9 and j % 4 == 1:
                            hidden(j // 4 - 2)
                        elif j == GATE_UP + 3:
                            hidden(CHUNKS - 1)
                        elif j == GATE_UP + 5:
                            gathered_tokens(e + 1, "gather", done)
                    for k in range(4):
                        done(("scatter", k))
                        s = hF[:, 2 * k:2 * k + 2, :]
                        took_it(dve.tensor_tensor(s, pair(bank_in(("scatter", k))), s, ALU.add))

                for j in range(AHEAD):
                    low_part(0, j)
                gathered_tokens(0, "first", lambda key: dve.wait_ge(g.group_done, g.after[key]))
                with dve.Fori(0, N_EXP - 1) as e:
                    expert(e, True)
                expert(N_EXP - 1, False)

            for l in range(DEPTH):
                mixer(l)
                attention(l)
                if l == 0:
                    feed_forward()
            routing()
            experts(0)
            with dve.If(dve.value_load(extra_flag[0:1, 0:1], min_val=0, max_val=1) > 0):
                experts(1)

            def log1p(q, t_, z, w):
                step.now(dve.tensor_scalar(z, t_, 2.0, None, ALU.add))
                step.now(dve.reciprocal(z, z))
                step.now(dve.tensor_tensor(z, z, t_, ALU.mult))
                step.now(dve.tensor_tensor(w, z, z, ALU.mult))
                step.now(dve.tensor_scalar(q, w, 1.0 / 15, None, ALU.mult))
                for c in (13, 11, 9, 7, 5, 3):
                    step.now(dve.scalar_tensor_tensor(q, q, 1.0 / c, w, ALU.add, ALU.mult))
                step.now(dve.scalar_tensor_tensor(q, q, 1.0, z, ALU.add, ALU.mult))
                step.now(dve.tensor_scalar(q, q, 2.0, None, ALU.mult))

            def mlstm():
                dve.wait_ge(act_took, G.took["final_ms"])
                scaled(hF, hF, lambda k: col(C3 + FIN_G + k), final_ready)
                lam = cols[:, C2 + LAM:C2 + LAM + 16]
                dve.scalar_tensor_tensor(lam_t, lam, -1.0, lam, ALU.mult, ALU.max).then_inc(abs_ready, 1)
                dve.wait_ge(exp_done, 1)
                log1p(lam_q, lam_t, lam_z, lam_w)
                step.now(dve.tensor_scalar(lam_z, lam, -1.0, 0.0, ALU.mult, ALU.max))
                step.now(dve.tensor_tensor(lam_z, lam_z, lam_q, ALU.add))
                step.then(dve.tensor_scalar(lam_neg, lam_z, -LRU_C, None, ALU.mult))
                dve.tensor_scalar(lam_pos, lam_z, LRU_C, None, ALU.mult).then_inc(lam_ready, 1)
                norm("norm1_ms", lambda k: col(C2 + N1_G + k))
                dve.wait_ge(x_ready, N_NORMS)
                step.then(dve.memset(xm_pad[:, :, 0:2], 0.0))
                step.then(dve.memset(xm_pad[:, :, 2 + SEQ:], 0.0))
                ready("gates")
                step.now(dve.memset(gate_cols, 0.0))
                src = bank_of("gates")[:, 0:32].rearrange("p (b d g h) -> p b d g h", b=TB, d=2, g=2)
                bias = gate_row.rearrange("p (d g h) -> p d g h", d=2, g=2)
                for b in range(TB):
                    for d in range(2):
                        ins = dve.tensor_tensor(gate_cols[:, b, :, 32 * d:32 * d + HEADS], src[:, b, d, :, :], bias[:, d, :, :], ALU.add)
                        if (b, d) != (1, 1):
                            step.then(ins)
                take(ins)
                dve.wait_ge(dve_took, G.took["gates"])
                step.settle()
                dve.engine_nop().then_inc(gates_ready, 1)
                ready("gate_rows")
                step.then(dve.tensor_copy(g_fo, bank_of("gate_rows")[0:64, SEQ:2 * SEQ]))
                take(dve.tensor_copy(g_in, bank_of("gate_rows")[0:64, 0:SEQ]))
                dve.wait_ge(dve_took, G.took["gate_rows"])
                dve.scalar_tensor_tensor(g_t, g_fo, -1.0, g_fo, ALU.mult, ALU.max).then_inc(abs_ready, 1)
                dve.wait_ge(exp_done, 2)
                log1p(g_q, g_t, g_z, g_w)
                step.then(dve.memset(g_one, 1.0))
                step.then(dve.memset(g_zero, 0.0))
                step.now(dve.scalar_tensor_tensor(g_fo, g_fo, 0.0, g_q, ALU.min, ALU.subtract))
                fwd, bwd = slice(0, 32), slice(32, 64)
                step.then(dve.tensor_tensor_scan(g_b[fwd, :], g_one[fwd, :], g_fo[fwd, :], 0.0, ALU.mult, ALU.add))
                step.then(dve.tensor_tensor_scan(g_b[bwd, ::-1], g_one[bwd, ::-1], g_fo[bwd, ::-1], 0.0, ALU.mult, ALU.add))
                step.settle()
                step.now(dve.tensor_tensor(g_a, g_in, g_b, ALU.subtract))
                step.then(dve.tensor_tensor_scan(g_max[fwd, :], g_a[fwd, :], g_zero[fwd, :], 0.0, ALU.max, ALU.max))
                step.then(dve.tensor_tensor_scan(g_max[bwd, ::-1], g_a[bwd, ::-1], g_zero[bwd, ::-1], 0.0, ALU.max, ALU.max))
                step.settle()
                dve.tensor_tensor(g_sum, g_b, g_max, ALU.add).then_inc(a_ready, 1)
                dve.wait_ge(act_took, G.took["xm", 3])
                conv(xm_conv, lambda k, j: xm_pad[:, k, j:j + SEQ], C_TAPS, lambda k, j: col(C2 + MC_W + 8 * j + k),
                     lambda k: col(C2 + MC_B + k), tuple((k, P) for k in range(KT)))
                dve.engine_nop().then_inc(xm_conv_ready, 1)
                for b in range(TB):
                    for hp in range(2):
                        ready(("vL", b, hp))
                        take(dve.tensor_copy(vL[:, b, 512 * hp:512 * (hp + 1)], bank_of(("vL", b, hp))[:, :]))
                ready("a_cols")
                take(dve.tensor_copy(a_cols, pair(bank_of("a_cols"), TB, 64)))
                dve.wait_ge(dve_took, G.took["a_cols"])

                def argument(i):
                    h, d = divmod(i, 2)
                    ready(("maxima", i))
                    bank = banks["a"][(G.took["maxima", i] - 1) % 4][:, 0:SEQ].rearrange("p (t j) -> p t j", t=2)
                    for n_, (sblk, lo, hi) in enumerate(((0, 0, 2), (1, 1, 2)) if d == 0 else ((1, 0, 2), (0, 0, 1))):
                        ins = dve.tensor_scalar(decay[:, sblk, lo:hi, :], bank[:, lo:hi, :], a_cols[:, sblk, 32 * d + h:32 * d + h + 1],
                                                0.0, ALU.subtract, ALU.max)
                        if n_ == 0:
                            step.then(ins)
                    ins.then_inc(arg_ready, 1)

                argument(0)
                for i in range(2 * HEADS):
                    h, d = divmod(i, 2)
                    dve.wait_ge(act_took, G.took["maxima", i])
                    s4 = scoresT[:, h % 2, :, :, :].rearrange("p s t j -> p (s t) j")
                    w4, p4 = (a.rearrange("p s t j -> p (s t) j") for a in (decay, intra))
                    diag = slice(0, 4, 3)
                    other = 1 if d == 0 else 2
                    m = (tri if d == 0 else lower)[:, :].unsqueeze(1).to_broadcast([P, 2, P])
                    step.then(dve.tensor_tensor(p4[:, other, :], s4[:, other, :], w4[:, other, :], ALU.mult))
                    step.now(dve.tensor_tensor(p4[:, diag, :], s4[:, diag, :], m, ALU.mult))
                    dve.tensor_tensor(p4[:, diag, :], p4[:, diag, :], w4[:, diag, :], ALU.mult).then_inc(intra_ready, 1)
                    if i + 1 < 2 * HEADS:
                        dve.wait_ge(intra_ready, i + 1)
                        argument(i + 1)
                    ready(("den", i))
                    den = bank_of(("den", i))[:, 0:SEQ]
                    step.now(dve.tensor_tensor(rstd_row[:, :], den, floor_[:, i % 2, :], ALU.max))
                    take(dve.scalar_tensor_tensor(rstd_row[:, :], den, -1.0, rstd_row[:, :], ALU.mult, ALU.max))
                    dve.wait_ge(dve_took, G.took["den", i])
                    step.now(dve.reciprocal(rstd_row[:, :], rstd_row[:, :]))
                    r2 = rstd_row[:, :].unsqueeze(1).to_broadcast([P, 2, SEQ])
                    ready(("num", i))
                    part = hM[:, 2 * h:2 * h + 2, :]
                    if d == 0:
                        take(dve.tensor_tensor(part, pair(bank_of(("num", i))), r2, ALU.mult))
                    else:
                        num = bank_of(("num", i))
                        step.now(dve.tensor_tensor(pair(num), pair(num), r2, ALU.mult))
                        dve.wait_ge(dve_took, G.took["num", i - 1])
                        take(dve.tensor_tensor(part, part, pair(num), ALU.add))
                dve.wait_ge(dve_took, G.took["num", 2 * HEADS - 1])
                dve.engine_nop().then_inc(h_sum_ready, 1)
                dve.wait_ge(act_took, G.took["head_ms", 1])
                step.now(dve.reciprocal(std4, std4))
                for k in range(KT):
                    step.then(dve.scalar_tensor_tensor(hM[:, k, :], hM[:, k, :], col(C2 + MN_G + k), std4[:, k // 2, :], ALU.mult, ALU.mult))
                step.settle()
                dve.tensor_tensor(hM, hM, o_sig, ALU.mult).then_inc(ym_ready, 1)

            def lru():
                dve.wait_ge(ym_ready, 1)
                step.then(dve.memset(xl_pad[:, :, 0:2], 0.0))
                step.then(dve.memset(xl_pad[:, :, 2 + SEQ:], 0.0))
                dve.wait_ge(act_took, G.took["xl", 3])
                step.settle()
                conv(xl_conv, lambda k, j: xl_pad[:, k, j:j + SEQ], C_TAPS, lambda k, j: col(C3 + LC_W + 8 * j + k),
                     lambda k: col(C2 + LC_B + k), tuple((k, P) for k in range(KT)))
                dve.engine_nop().then_inc(xl_conv_ready, 1)
                dve.engine_nop().then_inc(lru_free, 1)
                for g in range(4):
                    ready(("branch_m", g))
                    take(dve.tensor_tensor(merged[:, 2 * g:2 * g + 2, :], pair(bank_of(("branch_m", g))), g_m[:, 2 * g:2 * g + 2, :], ALU.mult))
                for d in range(2):
                    dve.wait_ge(act_took, G.took["i", d, 3])
                    dve.tensor_tensor(lru_u, lru_u, xl_conv, ALU.mult).then_inc(gated_ready, 1)
                    dve.wait_ge(lru_a_ready, d + 1)
                    for i in range(2):
                        s = slice(4 * i, 4 * i + 4)
                        step.now(dve.tensor_tensor(half_tmp, lru_a[:, s, :], lru_a[:, s, :], ALU.mult))
                        ins = dve.scalar_tensor_tensor(lru_t[:, s, :], half_tmp, 1.0, lru_t[:, s, :], ALU.add, ALU.mult)
                        if i == 0:
                            step.now(ins)
                    ins.then_inc(lru_v_ready, 1)
                    edge = 0 if d == 0 else SEQ - 1
                    step.then(dve.memset(lru_a[:, :, edge:edge + 1], 0.0))
                    dve.wait_ge(lru_s_ready, d + 1)
                    dve.wait_ge(gated_ready, d + 1)
                    step.now(dve.tensor_tensor(lru_u, lru_u, lru_t[:, :, :], ALU.mult))
                    a, u, h, h2 = (x_.rearrange("p k s -> p (k s)") for x_ in (lru_a, lru_u, h_l, lru_t[:, :, :]))
                    if d == 0:
                        dve.wait_ge(group_done, G.after["branch_m", 3])
                        step.now(dve.tensor_tensor_scan(h, a, u, 0.0, ALU.mult, ALU.add))
                        dve.engine_nop().then_inc(lru_free, 1)
                    else:
                        step.now(dve.tensor_tensor_scan(h2[:, ::-1], a[:, ::-1], u[:, ::-1], 0.0, ALU.mult, ALU.add))
                step.now(dve.tensor_tensor(h_l, h_l, lru_t[:, :, :], ALU.add))
                dve.wait_ge(act_took, G.took["gate_l", 3])
                dve.tensor_tensor(h_l, h_l, gate_l, ALU.mult).then_inc(yl_ready, 1)

            def merge():
                dve.wait_ge(yl_ready, 1)
                dve.wait_ge(act_took, G.took["merge_l", 3])
                dve.wait_ge(dve_took, G.took["branch_m", 3])
                for g in range(4):
                    ready(("branch_l", g))
                    if g:
                        dve.wait_ge(merged_ready, g)
                    s = slice(2 * g, 2 * g + 2)
                    take(dve.tensor_tensor(pair_tmp, pair(bank_of(("branch_l", g))), g_l[:, s, :], ALU.mult))
                    dve.wait_ge(dve_took, G.took["branch_l", g])
                    dve.tensor_tensor(merged[:, s, :], merged[:, s, :], pair_tmp, ALU.add).then_inc(merged_ready, 1)
                add_to_residual("w_out")

            def top16(top, at, values, rest, n):
                lo, hi = slice(0, 8), slice(8, 16)
                for i in range(n):
                    step.then(dve.max(top[:, i, lo], values[:, i, :]))
                step.settle()
                for i in range(n):
                    step.then(dve.max_index(at[:, i, lo], top[:, i, lo], values[:, i, :]))
                    step.then(dve.match_replace(rest[:, i, :], top[:, i, lo], values[:, i, :], NEG))
                step.settle()
                for i in range(n):
                    step.then(dve.max(top[:, i, hi], rest[:, i, :]))
                step.settle()
                for i in range(n):
                    step.then(dve.max_index(at[:, i, hi], top[:, i, hi], rest[:, i, :]))
                step.settle()

            def choose_keys(b):
                dve.wait_ge(act_took, G.took["key_scores", b, 3])
                top16(key_top, key_at, key_scores, key_rest, 2 * PHEADS)
                step.then(dve.tensor_copy(key_at_f.rearrange("p h s k -> p (h s) k"), key_at))
                t4 = key_top.rearrange("p (h s) k -> p h s k", s=2)
                shape = [P, PHEADS, TOPK, TOPK]
                step.then(dve.tensor_tensor(pairs_.rearrange("p h (i j) -> p h i j", i=TOPK), t4[:, :, 0, :].unsqueeze(3).to_broadcast(shape),
                                            t4[:, :, 1, :].unsqueeze(2).to_broadcast(shape), ALU.add))
                step.settle()

            def choose_pairs(b):
                shape = [P, PHEADS, TOPK, TOPK]
                top16(best, best_at, pairs_, pairs_rest, PHEADS)
                at = best_at.rearrange("p h k -> p (h k)")
                step.then(dve.tensor_scalar(half_raw[0], at, 4, None, ALU.logical_shift_right))
                step.then(dve.tensor_scalar(half_raw[1], at, TOPK - 1, None, ALU.bitwise_and))
                step.settle()
                for i in range(2):
                    step.now(dve.tensor_copy(half_at[i], half_raw[i]))
                    wide = [P, SLOTS, TOPK]
                    step.now(dve.tensor_tensor(match, half_at[i].unsqueeze(2).to_broadcast(wide),
                                               iota[:, 0:TOPK].unsqueeze(1).to_broadcast(wide), ALU.is_equal))
                    m4 = match.rearrange("p (h k) j -> p h k j", h=PHEADS)
                    step.now(dve.tensor_tensor(m4, m4, key_at_f[:, :, i, :].unsqueeze(2).to_broadcast(shape), ALU.mult))
                    step.now(dve.tensor_reduce(half_key[i], match, AX.X, ALU.add))
                dve.scalar_tensor_tensor(rows_at[:, b * SLOTS:(b + 1) * SLOTS], half_key[0], float(PK), half_key[1],
                                         ALU.mult, ALU.add).then_inc(index_ready, 1)
                g = gates[:, b, :, :]
                dve.tensor_tensor(g, best, best[:, :, 0:1].to_broadcast([P, PHEADS, TOPK]), ALU.subtract).then_inc(margin_ready, 1)
                dve.wait_ge(margin_exp, b + 1)
                step.now(dve.tensor_reduce(gate_sum, g, AX.X, ALU.add))
                step.now(dve.reciprocal(gate_inv, gate_sum))
                step.now(dve.tensor_tensor(g, g, gate_inv.unsqueeze(2).to_broadcast([P, PHEADS, TOPK]), ALU.mult))

            def peer():
                norm("norm2_ms", lambda k: col(C2 + N2_G + k))
                for g in range(4):
                    ready(("keysT", g))
                    take(dve.tensor_copy(keysT[:, 4 * g:4 * g + 4, :], pair(bank_of(("keysT", g)), 4, P)))

                def u_rows(b):
                    ready(("tokens", b, 1))
                    n = (G.took["tokens", b, 0] - 1) % 4
                    assert n % 2 == 0
                    x = psum_all[:, n:n + 2, :].rearrange("p h d -> p (h d)")
                    with dve.Fori(b * ROUNDS, (b + 1) * ROUNDS) as r:
                        for q in range(BATCHES):
                            dve.wait_ge(gathered[q], r * GATHERED + GATHERED * (b * ROUNDS + 1))
                            for j in range(q * BATCH, (q + 1) * BATCH):
                                row = gathered_rows[:, j, :]
                                ins = dve.tensor_tensor_reduce(row, row, x, 1.0, 0.0, ALU.mult, ALU.add, dots[:, j:j + 1])
                            ins.then_inc(dot_done, 1)
                        dve.wait_ge(dot_done, r * BATCHES + BATCHES)
                        dve.tensor_copy(acts[:, bass.ds(r * GATHER, GATHER)], dots).then_inc(dots_kept, 1)
                        dve.wait_ge(dots_kept, r + 1)

                def weights(b):
                    dve.wait_ge(act_ready, b + 1)
                    s = acts[:, b * SLOTS:(b + 1) * SLOTS]
                    dve.tensor_tensor(s, s, gates[:, b, :, :].rearrange("p h k -> p (h k)"), ALU.mult).then_inc(weight_ready, 1)
                    if b:
                        dve.wait_ge(final_out, b)
                    dve.memset(v_sum, 0.0).then_inc(v_zeroed, 1)
                    dve.wait_ge(weight_ready, b + 1)
                    dve.wait_ge(v_zeroed, b + 1)

                def v_rows(b, first, last):
                    def batches(r, free):
                        for q in range(BATCHES):
                            if free:
                                dve.wait_ge(mix_done, (r - 1) * BATCHES + q + 1)
                            shape = [P, BATCH - 1, P]
                            dve.tensor_tensor(diag[:, q, :, :], ident[:, :].unsqueeze(1).to_broadcast(shape),
                                              acts[:, bass.ds(r * GATHER + q * BATCH, BATCH - 1)].unsqueeze(2).to_broadcast(shape), ALU.mult
                                              ).then_inc(diag_ready, 1)
                            dve.wait_ge(gathered[q], r * GATHERED + GATHERED * ((b + 1) * ROUNDS + 1))
                            if free or q:
                                dve.wait_ge(add_done, r * BATCHES + q)
                            dve.scalar_tensor_tensor(v_sum, gathered_rows[:, (q + 1) * BATCH - 1, :],
                                                     acts[:, bass.ds(r * GATHER + (q + 1) * BATCH - 1, 1)], v_sum, ALU.mult, ALU.add
                                                     ).then_inc(add_done, 1)

                    if b == 0 and first == 0:
                        batches(0, False)
                        first = 1
                    with dve.Fori(b * ROUNDS + first, b * ROUNDS + last) as r:
                        batches(r, True)

                def finish(b):
                    ready(("out", b, 1))
                    n = 4 + (G.took["out", b, 0] - 1) % 4
                    dve.wait_ge(add_done, (b + 1) * ROUNDS * BATCHES)
                    dve.tensor_tensor(v_sum, psum_all[:, n:n + 2, :].rearrange("p h d -> p (h d)"), v_sum, ALU.add).then_inc(v_summed, 1)
                    dve.wait_ge(final_std_ready, b + 1)
                    step.now(dve.reciprocal(final_rstd[:, b:b + 1], final_std[:, b:b + 1]))
                    dve.wait_ge(gain_loaded, 16)
                    dve.scalar_tensor_tensor(final_rows[:, b, :], v_sum, final_rstd[:, b:b + 1], final_gain, ALU.mult, ALU.mult
                                             ).then_inc(final_out, 1)

                choose_keys(0)
                choose_pairs(0)
                u_rows(0)
                choose_keys(1)
                dve.memset(zero_row, 0.0).then_inc(zero_ready, 1)
                weights(0)
                v_rows(0, 0, ROUNDS // 2)
                choose_pairs(1)
                v_rows(0, ROUNDS // 2, ROUNDS)
                finish(0)
                u_rows(1)
                weights(1)
                v_rows(1, 0, ROUNDS)
                finish(1)

            mlstm()
            lru()
            merge()
            peer()


_OUT = ((1, SEQ, D), "float32")


def kernel(**inputs):
    import numpy as _np
    import concourse.bacc as _bacc
    from concourse import mybir as _mybir
    from concourse.bass_utils import run_bass_kernel_spmd as _run

    nc = _bacc.Bacc("TRN2", target_bir_lowering=False, num_devices=1)
    arrays, t = {}, {}
    for name, a in inputs.items():
        a = _np.ascontiguousarray(a)
        arrays[f"in_{name}"] = a
        t[name] = nc.dram_tensor(f"in_{name}", a.shape, _mybir.dt.from_np(a.dtype), kind="ExternalInput").ap()
    out = nc.dram_tensor("out_0", _OUT[0], F32, kind="ExternalOutput").ap()
    two_blocks(nc, t, out)
    r = _run(nc, [arrays], core_ids=[0])
    return r.results[0]["out_0"]
```

```python
from contextlib import ExitStack

import concourse.bass as bass
from concourse import mybir
from concourse.alu_op_type import AluOpType as ALU

ACT = mybir.ActivationFunctionType
AX = mybir.AxisListType
F32 = mybir.dt.float32
I32 = mybir.dt.int32
F32R = mybir.dt.float32r
U32 = mybir.dt.uint32

P = 128
EPS = 1e-6
DEPTH, D, SEQ = 2, 1024, 256
KT, TB = D // P, SEQ // P
A_W, BC_W = 384, 320
A_TAPS, B_TAPS, C_TAPS = 31, 3, 4
HEADS, HD = 4, 256
FF, N_EXP, EXP_W = 2816, 8, 3584
FT, ET = FF // P, EXP_W // P
LRU_C = 8.0
PK, PHEADS, TOPK = 128, 8, 16
SLOTS = PHEADS * TOPK
NEG = -3.0e38
RING = 5
EXP_RING = 7
SLOT_F = KT * 512
GATHER, BATCH = 16, 4
BATCHES = GATHER // BATCH
GATHERED = 16 * BATCH
ROUNDS = SLOTS // GATHER
HALVES = 2
CHUNKS = EXP_W // 512
GATE_UP, DOWN = 4 * CHUNKS, ET // 2
EXP_TILES = GATE_UP + DOWN
FFN_GATE_UP, FFN_DOWN = FT, FT // 2
FFN_TILES = FFN_GATE_UP + FFN_DOWN
FFN_HIGH = 3
AHEAD = 2
EXP_GROUPS, EXP_V, EXP_A = 32, 16, 16
EXP_MARKS = 2 * CHUNKS + DOWN - 1


class Groups:

    def __init__(self, pe, banks, group_done, took_sems, loads):
        self.pe, self.banks, self.group_done, self.took_sems = pe, banks, group_done, took_sems
        self.total, self.given = 0, {"v": 0, "a": 0}
        self.after, self.took, self.open = {}, {}, []
        self.loads, self.loaded, self.slots = loads, [0] * RING, []
        self.freed, self.need = [], []
        self.turn = None

    def begin(self, who, key):
        n = self.given[who]
        if n >= 4:
            extra = 0 if self.turn is None else self.turn * EXP_V
            self.pe.wait_ge(self.took_sems[who], n - 3 + extra)
        self.given[who] = n + 1
        self.took[key] = n + 1
        self.open.append(key)
        return self.banks[who][n % 4]

    def end(self, mm, key=None):
        key = key or self.open[0]
        self.open.remove(key)
        self.total += 1
        self.after[key] = self.total
        mm.then_inc(self.group_done, 1)

    def tile(self, dmas=1):
        n = len(self.need)
        slot = n % RING
        self.loaded[slot] += 16 * dmas
        self.need.append(self.loaded[slot])
        self.freed.append(None)
        self.pe.wait_ge(self.loads[slot], self.loaded[slot])
        return slot

    def free(self):
        self.freed[-1] = (self.group_done, self.total)

    def loop(self, turn):
        self.turn, self.start = turn, (self.total, dict(self.given))

    def close(self, turns):
        total, given = self.start
        assert self.total - total == EXP_GROUPS and len(self.used) == EXP_TILES and self.marks == 2 * EXP_MARKS
        assert self.given["v"] - given["v"] == EXP_V and self.given["a"] - given["a"] == EXP_A
        self.turn = None
        self.total += EXP_GROUPS * (turns - 1)
        self.given["v"] += EXP_V * (turns - 1)
        self.given["a"] += EXP_A * (turns - 1)


class Experts:

    def __init__(self, groups, sem, name):
        groups.split, groups.high, groups.marked = (sem(f"{name}_{x}") for x in ("tiles_split", "tiles_rounded", "tile_used"))
        groups.x_high, groups.hidden_split = sem(f"{name}_x_rounded"), sem(f"{name}_hidden_split")
        groups.raw_loads = [sem(f"{name}_tile_loaded{i}") for i in range(EXP_RING)]
        groups.used, groups.marks = [], EXP_MARKS


class Steps:

    def __init__(self, eng, sem):
        self.eng, self.sem, self.n, self.turn, self.per = eng, sem, 0, None, 0

    def value(self, n):
        return n if self.turn is None else n + self.turn * self.per

    def then(self, ins):
        ins.then_inc(self.sem, 1)
        self.n += 1

    def settle(self, back=0):
        if self.n > back:
            self.eng.wait_ge(self.sem, self.value(self.n - back))

    def now(self, ins):
        self.then(ins)
        self.settle()


class Tally:
    def __init__(self):
        self.n = {}

    def next(self, name):
        self.n[name] = self.n.get(name, 0) + 1
        return self.n[name]


def two_blocks(nc, t, out):
    with ExitStack() as ctx:
        def sb(name, shape, dt=F32):
            return ctx.enter_context(nc.sbuf_tensor(name, shape, dt))

        def sem(name):
            return ctx.enter_context(nc.semaphore(name))

        def sb_under(name, shape):
            with nc.sbuf_tensor(name, shape, F32) as under:
                return under

        EXTRA = EXP_RING * SLOT_F - RING * SLOT_F
        dense = sb_under("dense_weights", [P, RING * SLOT_F + EXTRA])
        ring = dense[:, 0:RING * SLOT_F].rearrange("p (s f) -> p s f", s=RING)
        raw_tiles = sb_under("expert_tiles", [P, EXP_RING, SLOT_F // 2])
        low_tiles, high_tiles = (sb(f"expert_tiles_{x}", [P, EXP_RING, SLOT_F // 2], F32R) for x in ("low", "high"))
        hF = sb("residual", [P, KT, SEQ])
        xF = sb_under("normed", [P, KT, SEQ])
        xe_parts = sb("gathered_parts", [P, 2, KT, P], F32R)
        squares = sb("squares", [P, KT, SEQ])
        ident = sb("ident", [P, P])
        ones = sb("ones", [P, P])
        lower = sb("lower", [P, P])
        half_ones = sb("half_ones", [P, P])
        tri = sb("tri", [P, P])
        iota = sb("iota", [P, P])
        pair_sel = sb("pair_sel", [5, 3, P])
        gate_bias = sb("gmlp_bias", [5, DEPTH, P])
        spatialT = sb("spatialT", [P, DEPTH, 5, P])
        cols = sb("cols", [P, 474])
        mean_row = sb("neg_mean", [P, SEQ])
        std_row = sb("std", [P, SEQ])
        rstd_row = sb("rstd", [P, SEQ])
        eps = sb("eps", [P, 1])
        router = sb("router", [P, KT, N_EXP])
        small = sb("small", [P, 256])
        extra_flag = sb("extra_flag", [P, 1], I32)
        WORK = 13848
        work = sb_under("work", [P, WORK])
        work_parts = sb("work_parts", [P, WORK], F32R)

        def view(off, *shape, extra=False):
            n = 1
            for s in shape:
                n *= s
            assert off + n <= (EXTRA if extra else WORK), (off, shape)
            flat = dense[:, RING * SLOT_F + off:RING * SLOT_F + off + n] if extra else work[:, off:off + n]
            if len(shape) == 1:
                return flat
            names = "abcd"[:len(shape)]
            kw = {c: s for c, s in zip(names, shape)}
            return flat.rearrange(f"p ({' '.join(names)}) -> p {' '.join(names)}", **kw)

        psum_all = ctx.enter_context(nc.psum_tensor("banks", [P, 8, 512], F32))
        psum = [psum_all[:, i, :] for i in range(8)]
        banks = {"v": psum[0:4], "a": psum[4:8]}

        def pair(bank, n=2, w=SEQ):
            return bank[:, 0:n * w].rearrange("p (a b) -> p a b", a=n)

        def c_vec(l, which, k):
            return cols[:, 49 * l + which + k:49 * l + which + k + 1]
        MIX_G, X_G, MEM_G, FFN_G, OUT_G, CONVA_B, LNA_G, LNA_B = 0, 8, 16, 24, 32, 40, 43, 46
        C1, C2 = 98, 98 + 2 * 93
        N1_G, MC_B, MN_G, LC_B, BR, BI, LAM, N2_G, MC_W = 0, 8, 16, 24, 32, 48, 64, 80, 88
        C3 = C2 + 120
        LC_W, FIN_G = 0, 32
        C4 = C3 + 40

        def col(i, rows=P):
            return cols[0:rows, i:i + 1]

        def bc_col(l, which, k):
            return col(C4 + 10 * k + 5 * l + which, P if k < 2 else 64)

        MEM = WORK - KT * SEQ
        mem_hat = view(MEM, KT, SEQ)
        x_in, mem_in = view(0, TB, D), view(2048, TB, D)
        rows = view(4096, 5, P)
        bc_rows = view(4736, 320)
        spatial_in = view(5056, DEPTH, 5, P)
        sig_a = view(0, 3, SEQ)
        ya_pad = view(768, 3, SEQ + A_TAPS - 1)
        conv_a = view(1626, 3, SEQ)
        c_gate = view(2394, 3, SEQ)
        yb_pad = view(3162, 3, SEQ + B_TAPS - 1)
        b_gate = view(3936, 3, SEQ)
        conv_b = view(4704, 3, SEQ)
        c_u = view(5472, 3, SEQ)
        c_v = view(6240, 3, SEQ)
        vT = view(7008, TB, BC_W)
        yF = view(7648, KT, SEQ)
        std8 = view(9696, KT, SEQ)
        mem_g, kF, vM = view(0, KT, SEQ, extra=True), view(2048, KT, SEQ, extra=True), view(4096, TB, D, extra=True)
        qF = view(2048, KT, SEQ)
        probs = view(8192, HEADS, TB, SEQ)
        probsT = squares[:, :, :].rearrange("p (h m) s -> p h m s", h=HEADS)
        oF = view(0, KT, SEQ)
        def raw_tile(j):
            return raw_tiles[:, j % EXP_RING, :]

        def low_tile(j):
            return low_tiles[:, j % EXP_RING, :]

        def high_tile(j):
            return high_tiles[:, j % EXP_RING, :]

        x_high, x_low = (high_tiles[:, FFN_HIGH + i, :].rearrange("p (k s) -> p k s", k=KT) for i in range(2))
        hid_high, hid_low = (work_parts[:, i * FT * SEQ:(i + 1) * FT * SEQ].rearrange("p (f s) -> p f s", f=FT) for i in range(2))
        sil, hid = view(4096, 2, 2, SEQ, extra=True), view(5120, 2, 2, SEQ, extra=True)
        xT = view(0, TB, D)
        pick = view(2048, TB, N_EXP + 1, P)
        put = squares[:, :, :]
        he = view(4352, 2, 512)
        xe_high, xe_low = xe_parts[:, 0, :, :], xe_parts[:, 1, :, :]
        he_high, he_low = (work_parts[:, 5376 + i * EXP_W:5376 + (i + 1) * EXP_W].rearrange("p (a b) -> p a b", b=P) for i in range(2))
        he_all = view(5376 + EXP_W, ET, P)
        ye = view(12544, D)
        weighted = view(5376, TB, N_EXP, P)
        def pairs_of(off):
            return small[:, off:off + TB * N_EXP].rearrange("p (b e) -> p b e", b=TB)
        logits, top, top_at, first, second, chosen, share, place = (pairs_of(16 * i) for i in range(8))
        gap, ratio, total_w, w_first, w_second = (small[:, 128 + 2 * i:130 + 2 * i] for i in range(5))
        counts, most = small[:, 144:152], small[:, 152:153]
        top_raw = small[:, 160:176].bitcast(U32).rearrange("p (b e) -> p b e", b=TB)

        xm_pad = view(0, KT, SEQ + C_TAPS - 1)
        xm_conv = view(2072, KT, SEQ)
        qM, kM = view(4120, KT, SEQ), view(6168, KT, SEQ)
        vL = view(8216, TB, D)
        scoresT = view(10264, 2, 2, 2, P)
        decay = view(11288, 2, 2, P)
        intra = view(11800, 2, 2, P)
        floor_ = view(12312, 2, SEQ)
        head_sel = view(12824, 8, P)
        gate_cols = squares[:, 0, :].rearrange("p (b g r) -> p b g r", b=TB, g=2)
        g_in, g_fo, g_t, g_z, g_w, g_q, g_b, g_a = (squares[0:64, i, :] for i in range(8))
        g_max, g_sum, g_zero, g_one = g_t, g_z, g_w, mean_row[0:64, :]
        a_cols = small[:, 96:224].rearrange("p (b r) -> p b r", b=TB)
        gate_row = small[:, 240:256]
        hM = view(2072, KT, SEQ)
        o_sig = view(0, KT, SEQ, extra=True)
        std4 = view(10520, HEADS, SEQ)
        g_m, merged = view(4120, KT, SEQ), view(6168, KT, SEQ)
        xl_pad = view(8216, KT, SEQ + C_TAPS - 1)
        xl_conv = view(0, KT, SEQ)
        h_l = view(2072, KT, SEQ)
        gate_l = view(4120, KT, SEQ)
        lru_a, lru_u = view(8216, KT, SEQ), view(10264, KT, SEQ)
        lru_t = squares
        half_tmp = view(12312, 4, SEQ)
        g_l = view(0, KT, SEQ)
        pair_tmp = view(12312, 2, SEQ)
        lam_t, lam_z, lam_w, lam_q, lam_neg, lam_pos = (small[:, 16 * i:16 * i + 16] for i in range(6))

        qP, keysT = view(0, 2 * PHEADS, SEQ), view(4096, 2 * PHEADS, PK)
        key_scores, key_rest = view(6144, 2 * PHEADS, PK), view(8192, 2 * PHEADS, PK)
        pairs_, pairs_rest = view(6144, PHEADS, TOPK * TOPK), view(8192, PHEADS, TOPK * TOPK)
        key_top, key_at = view(10240, 2 * PHEADS, TOPK), view(10496, 2 * PHEADS, TOPK).bitcast(U32)
        key_at_f = view(10752, PHEADS, 2, TOPK)
        best, best_at = view(11008, PHEADS, TOPK), view(11136, PHEADS, TOPK).bitcast(U32)
        half_raw = [view(11264 + SLOTS * i, SLOTS).bitcast(U32) for i in range(2)]
        half_at = [view(11520 + SLOTS * i, SLOTS) for i in range(2)]
        half_key = [view(11776 + SLOTS * i, SLOTS) for i in range(2)]
        gates = view(12032, TB, PHEADS, TOPK)
        rows_at = view(12288, TB * SLOTS).bitcast(U32)
        acts = view(12544, TB * SLOTS)
        final_gain = view(12800, D)
        match = squares[:, :, :].rearrange("p k s -> p (k s)").rearrange("p (a j) -> p a j", j=TOPK)
        gathered_rows = ring[:, 0:GATHER * D // SLOT_F, :].rearrange("p s (r d) -> p (s r) d", d=D)
        diag = view(0, BATCHES, BATCH - 1, P)
        zero_row = view(1536, 512)[0:1, :]
        final_sq, v_sum = view(4096, D), view(5120, D)
        final_rows = view(6144, TB, D)
        stage = sb("gather_stage", [P, GATHER], U32)
        dots = small[:, 0:GATHER]
        gate_sum, gate_inv = small[:, 16:24], small[:, 24:32]
        final_ss, final_std, final_rstd = (small[:, 32 + 2 * i:34 + 2 * i] for i in range(3))

        loads = [sem(f"weights_loaded{i}") for i in range(RING)]
        group_done = sem("pe_group_done")
        dve_took, act_took = sem("dve_took"), sem("act_took")
        took_sems = {"v": dve_took, "a": act_took}
        dve_step, act_step, pool_step = sem("dve_step"), sem("act_step"), sem("pool_step")
        inputs_loaded = sem("inputs_loaded")
        params_loaded = sem("params_loaded")
        consts_ready = sem("consts_ready")
        sq_ready = sem("squares_ready")
        x_ready = sem("normed_ready")
        conv_ready = sem("conv_ready")
        centred = sem("centred")
        ln_ready = sem("ln_ready")
        ya_ready = sem("ya_ready")
        y_all = sem("y_all_ready")
        y_ready = sem("y_ready")
        cv_ready = sem("cv_ready")
        mask_ready = sem("spatial_masked")
        mem_normed = sem("mem_normed")
        mem_ready = sem("mem_ready")
        max_ready = sem("max_ready")
        probs_ready = sem("probs_ready")
        exp_ready = sem("exp_ready")
        out_done = sem("out_stored")
        routing_ready = sem("routing_ready")
        chosen_ready = sem("chosen_ready")
        gap_ready = sem("logit_gap_ready")
        ratio_ready = sem("expert_ratio_ready")
        weighted_ready = sem("weighted_ready")
        pick_ready = sem("pick_ready")
        final_ready = sem("first_block_normed")
        gates_ready = sem("gate_columns_ready")
        abs_ready, exp_done = sem("abs_ready"), sem("exp_done")
        a_ready = sem("gate_rows_ready")
        sel_ready = sem("head_sel_ready")
        xm_conv_ready, xm_act = sem("xm_conv_ready"), sem("xm_activated")
        arg_ready = sem("decay_argument_ready")
        intra_ready = sem("intra_ready")
        h_sum_ready = sem("mlstm_sum_ready")
        ym_ready = sem("y_mlstm_ready")
        xl_conv_ready = sem("xl_conv_ready")
        lam_ready = sem("lam_ready")
        gated_ready = sem("lru_input_gated")
        lru_a_ready = sem("lru_decay_ready")
        lru_v_ready, lru_s_ready = sem("lru_scale_squared_ready"), sem("lru_scale_ready")
        lru_free = sem("lru_buffers_free")
        yl_ready = sem("y_lru_ready")
        merged_ready = sem("merged_ready")
        index_ready = sem("peer_index_ready")
        margin_ready, margin_exp = sem("gate_margin_ready"), sem("gate_margin_exp")
        gathered = [sem(f"rows_gathered{i}") for i in range(BATCHES)]
        staged, pool_turn = sem("indices_staged"), sem("pool_turn")
        dot_done, dots_kept = sem("dot_batch_done"), sem("dots_kept")
        act_ready, weight_ready = sem("peer_activation_ready"), sem("peer_weight_ready")
        diag_ready, mix_done, add_done = sem("diag_ready"), sem("mix_batch_done"), sem("add_batch_done")
        v_zeroed, v_summed = sem("v_sum_zeroed"), sem("v_summed")
        zero_ready = sem("zero_row_ready")
        gain_loaded = sem("final_gain_loaded")
        final_std_ready, final_out = sem("final_std_ready"), sem("final_rows_ready")
        ffn_loads = [sem(f"ffn_tile_loaded{i}") for i in range(EXP_RING)]
        ffn_high, ffn_split, ffn_marked = sem("ffn_tiles_rounded"), sem("ffn_tiles_split"), sem("ffn_tile_used")
        ffn_x_split, ffn_hid_split = sem("ffn_x_split"), sem("ffn_hidden_split")
        more_places = sem("more_places")
        more_done = sem("more_groups_done")
        more_took = {"v": sem("more_dve_took"), "a": sem("more_act_took")}

        EPS_AP = eps[:, 0:1]
        G = None
        passes = []
        N_NORMS = 3 * DEPTH + 1
        N_PARAMS = DEPTH * 17 + 13
        def wait_used(eng, g, e, j):
            if j >= EXP_RING:
                used, count, per = g.used[j - EXP_RING]
                eng.wait_ge(used, count + e * per)
            elif not isinstance(e, int) or e > 0:
                used, count, per = g.used[j + EXP_TILES - EXP_RING]
                eng.wait_ge(used, count + (e - 1) * per)

        block = ctx.enter_context(nc.Block())

        @block.tensor
        def _(pe):
            nonlocal G
            G = Groups(pe, banks, group_done, took_sems, loads)
            seen = Tally()
            kv_slot = None

            def transposes(who, key, parts):
                bank = G.begin(who, key)
                for off, a in parts:
                    k, m = a.shape[0], a.shape[1]
                    mm = pe.transpose(bank[0:m, off:off + k], a, ident[0:k, 0:k])
                G.end(mm)

            def sum_features(who, key, src, n=KT, weights=None, w=SEQ):
                bank = G.begin(who, key)
                for k in range(n):
                    a = src(k)
                    mm = pe.matmul(bank[:, 0:w], (weights or ones)[0:a.shape[0], :], a,
                                   start=(k == 0), stop=(k == n - 1))
                G.end(mm)

            def norm_sums(key, parts=4):
                arrived = set()

                def square(k):
                    if k // (KT // parts) not in arrived:
                        arrived.add(k // (KT // parts))
                        pe.wait_ge(sq_ready, seen.next("sq"))
                    return squares[:, k, :]

                sum_features("a", key, square)

            def normed():
                n, arrived = seen.next("x") - 1, set()

                def x(k):
                    if k not in arrived:
                        arrived.add(k)
                        pe.wait_ge(x_ready, KT * n + k + 1)
                    return xF[:, k, :]

                return x

            def linear(key, who, n_tiles, x, kts, widths=(0, P, 2 * P, 3 * P), per_group=2, dmas=1, ms=None):
                c = 0
                for tile in range(n_tiles):
                    slot = G.tile(dmas)
                    for i, off in enumerate(widths):
                        m = P if ms is None else ms[i]
                        if c % per_group == 0:
                            bank = G.begin(who, (key, c // per_group))
                        o = bank[0:m, (c % per_group) * SEQ:(c % per_group + 1) * SEQ]
                        for k in range(kts):
                            mm = pe.matmul(o, weight(slot, kts, widths)[:, k, off:off + m], x(k),
                                           start=(k == 0), stop=(k == kts - 1))
                        c += 1
                        if c % per_group == 0 or (tile == n_tiles - 1 and i == len(widths) - 1):
                            G.end(mm)
                    G.free()

            def weight(slot, kts, widths, cols_n=None):
                n = cols_n or 512
                return ring[:, slot, 0:kts * n].rearrange("p (k n) -> p k n", k=kts)

            pe.wait_ge(consts_ready, 1)
            pe.wait_ge(inputs_loaded, 32)
            for who, src, name in (("v", x_in, "x"), ("a", mem_in, "mem")):
                for g in range(4):
                    transposes(who, (name, g), [((k % 2) * SEQ + b * P, src[:, b, k * P:(k + 1) * P])
                                                for k in (2 * g, 2 * g + 1) for b in range(TB)])
            pe.wait_ge(params_loaded, 16 * N_PARAMS)
            parts = [(0, rows[0:98, 0, :]), (C1, rows[0:93, 1, :]), (C1 + 93, rows[0:93, 2, :]),
                     (C2, rows[0:120, 3, :]), (C3, rows[0:40, 4, :])]
            parts += [(C4 + 10 * k, bc_rows[0:10, k * P:min((k + 1) * P, 320)]) for k in range(3)]
            transposes("v", "cols", parts)
            for l in range(DEPTH):
                transposes("a", ("spatial", l, 0), [(g * P, spatial_in[:, l, g, :]) for g in range(4)])
            transposes("a", "spatial_last", [(l * P, spatial_in[:, l, 4, :]) for l in range(DEPTH)])
            norm_sums("mem_ms", 1)

            def mixer(l):
                norm_sums(("mix_ms", l), 4 if l else 1)
                x = normed()

                def section(name, who, width, offs, ms):
                    slot = G.tile()
                    w = ring[:, slot, 0:KT * width].rearrange("p (k n) -> p k n", k=KT)
                    for g, tiles in enumerate(((0, 1), (2,))):
                        bank = G.begin(who, (name, l, g))
                        for i, c in enumerate(tiles):
                            for k in range(KT):
                                mm = pe.matmul(bank[0:ms[c], i * SEQ:(i + 1) * SEQ], w[:, k, offs[c]:offs[c] + ms[c]],
                                               x(k), start=(k == 0), stop=(k == KT - 1))
                        G.end(mm)
                    G.free()

                section("a_gate", "a", A_W, (0, P, 2 * P), (P, P, P))
                section("a_val", "v", A_W, (0, P, 2 * P), (P, P, P))
                section("c_gate", "a", BC_W, (0, P, 2 * P), (P, P, 64))
                section("b_in", "v", BC_W, (0, P, 2 * P), (P, P, 64))
                section("b_gate", "a", BC_W, (0, P, 2 * P), (P, P, 64))
                section("c_v", "a", BC_W, (0, P, 2 * P), (P, P, 64))
                section("c_u", "a", BC_W, (0, P, BC_W - P), (P, P, P))

                def three(src):
                    return lambda k: src[0:(P if k < 2 else 64), k, :]

                pe.wait_ge(act_took, G.took["c_v", l, 1])
                sum_features("a", ("c_mean", l), three(c_v), 3)
                pe.wait_ge(mem_ready, l + 1)
                key_value(l, 0)
                pe.wait_ge(sq_ready, seen.next("sq"))
                sum_features("a", ("c_var", l), three(squares), 3)
                key_value(l, 1)
                pe.wait_ge(cv_ready, l + 1)
                for b in range(TB):
                    transposes("v", ("c_vT", l, b), [(k * P, three(c_v)(k)[:, b * P:(b + 1) * P]) for k in range(3)])
                pe.wait_ge(dve_took, G.took["c_vT", l, 1])
                pe.wait_ge(mask_ready, 1)
                for p in range(3):
                    n = 2 if p < 2 else 1
                    first = p * P if p < 2 else BC_W - P
                    for b in range(TB):
                        bank = G.begin("v", ("mixed", l, p, b))
                        for i in range(n):
                            o = bank[:, i * P:(i + 1) * P]
                            pe.matmul(o, vT[:, b, first:first + P], spatialT[:, l, 2 * p + i, :], start=True, stop=False)
                            mm = pe.matmul(o, pair_sel[:, p, :], gate_bias[:, l, :], start=False, stop=True)
                        G.end(mm)
                pe.wait_ge(conv_ready, l + 1)
                sum_features("a", ("a_mean", l), lambda k: conv_a[:, k, :], 3)
                key_value(l, 2)
                pe.wait_ge(sq_ready, seen.next("sq"))
                sum_features("a", ("a_var", l), lambda k: squares[:, k, :], 3)
                key_value(l, 3)
                key_value(l, 4)
                pe.wait_ge(sq_ready, seen.next("sq"))
                for g in range(4):
                    bank = G.begin("a", ("group_ms", l, g))
                    for i in range(2):
                        mm = pe.matmul(bank[:, i * SEQ:(i + 1) * SEQ], half_ones[:, :], squares[:, 2 * g + i, :],
                                       start=True, stop=True)
                    G.end(mm)
                for i in (5, 6, 7):
                    key_value(l, i)
                pe.wait_ge(y_ready, l + 1)
                linear(("mix_out", l), "v", 2, lambda k: yF[:, k, :], KT, dmas=4)

            def key_value(l, i):
                nonlocal kv_slot
                tile, part = divmod(i, 2)
                if part == 0:
                    kv_slot = G.tile()
                w = weight(kv_slot, KT, None)
                bank = G.begin("a", ("kv", l, i))
                if tile < 2:
                    for c in range(2):
                        for k in range(KT):
                            mm = pe.matmul(bank[:, c * SEQ:(c + 1) * SEQ], w[:, k, (2 * part + c) * P:(2 * part + c + 1) * P],
                                           mem_g[:, k, :], start=(k == 0), stop=(k == KT - 1))
                else:
                    for k in range(KT):
                        mm = pe.matmul(bank[:, :], mem_g[:, k, part * P:(part + 1) * P], w[:, k, :], start=(k == 0), stop=(k == KT - 1))
                G.end(mm)
                if part == 1:
                    G.free()

            def attention(l):
                norm_sums(("x_ms", l))
                linear(("q", l), "a", 2, normed(), KT)
                pe.wait_ge(act_took, G.took[("q", l), 3])
                for h in range(HEADS):
                    bank = G.begin("a", ("scores", l, h))
                    for b in range(TB):
                        for j in range(2):
                            mm = pe.matmul(bank[:, b * SEQ:(b + 1) * SEQ], qF[:, 2 * h + j, b * P:(b + 1) * P],
                                           kF[:, 2 * h + j, :], start=(j == 0), stop=(j == 1))
                    G.end(mm)
                for h in range(HEADS):
                    pe.wait_ge(probs_ready, HEADS * l + h + 1)
                    transposes("v", ("probsT", l, h), [(m * SEQ + b * P, probs[:, h, b, m * P:(m + 1) * P])
                                                       for m in range(TB) for b in range(TB)])
                for h in range(HEADS):
                    pe.wait_ge(dve_took, G.took["probsT", l, h])
                    bank = G.begin("a", ("o", l, h))
                    for e in range(2):
                        for m in range(TB):
                            mm = pe.matmul(bank[:, e * SEQ:(e + 1) * SEQ], vM[:, m, h * HD + e * P:h * HD + (e + 1) * P],
                                           probsT[:, h, m, :], start=(m == 0), stop=(m == TB - 1))
                    G.end(mm)
                pe.wait_ge(act_took, G.took["o", l, HEADS - 1])
                linear(("xo", l), "v", 2, lambda k: oF[:, k, :], KT)

            def parts(o, a_high, a_low, b_high, b_low, start, stop):
                pe.matmul(o, a_high, b_high, start=start, stop=False)
                pe.matmul(o, a_high, b_low, start=False, stop=False)
                return pe.matmul(o, a_low, b_high, start=False, stop=stop)

            def feed_forward():
                G.newest = [G.freed[max(m for m in range(len(G.freed)) if m % RING == s)] for s in range(RING)]
                G.ffn_used = []
                norm_sums("ffn_ms")
                seen.next("x")

                def split(j, k):
                    pe.wait_ge(ffn_split, j + 1)
                    return (a.rearrange("p (k n) -> p k n", k=k) for a in (high_tiles[:, j % FFN_HIGH, :], low_tile(j)))

                for j in range(FFN_GATE_UP):
                    c, a = divmod(j, 2)
                    bank = G.begin("av"[a], ("ffn", a, c))
                    high, low = split(j, KT)
                    for i in range(2):
                        o, n_ = bank[:, i * SEQ:(i + 1) * SEQ], slice(i * P, (i + 1) * P)
                        for k in range(KT):
                            if j == 0 and i == 0:
                                pe.wait_ge(ffn_x_split, k + 1)
                            mm = parts(o, high[:, k, n_], low[:, k, n_], x_high[:, k, :], x_low[:, k, :], k == 0, k == KT - 1)
                    G.end(mm)
                    G.ffn_used.append((group_done, G.total))
                down = [G.begin("v", ("ffn_down", g)) for g in range(4)]
                for i in range(FFN_DOWN):
                    pe.wait_ge(ffn_hid_split, i + 1)
                    high, low = split(FFN_GATE_UP + i, 2)
                    for r in range(2):
                        f = 2 * i + r
                        for c in range(KT):
                            n_ = slice(c * P, (c + 1) * P)
                            mm = parts(down[c // 2][:, (c % 2) * SEQ:(c % 2 + 1) * SEQ], high[:, r, n_], low[:, r, n_],
                                       hid_high[:, f, :], hid_low[:, f, :], f == 0 and c % 2 == 0, f == FT - 1 and c % 2 == 1)
                            if f == FT - 1 and c % 2 == 1:
                                G.end(mm, ("ffn_down", c // 2))
                    if i < FFN_DOWN - 1:
                        mm.then_inc(ffn_marked, 1)
                        G.ffn_used.append((ffn_marked, i + 1))
                G.ffn_used.append((group_done, G.total))

            def routing():
                norm_sums("moe_ms")
                x = normed()
                bank = G.begin("v", "logits")
                for b in range(TB):
                    for k in range(KT):
                        mm = pe.matmul(bank[:, b * N_EXP:(b + 1) * N_EXP], x(k)[:, b * P:(b + 1) * P], router[:, k, :],
                                       start=(k == 0), stop=(k == KT - 1))
                G.end(mm)
                for b in range(TB):
                    for half in range(2):
                        transposes("a", ("xT", b, half), [(i * P, xF[:, 4 * half + i, b * P:(b + 1) * P]) for i in range(4)])
                pe.wait_ge(chosen_ready, 1)
                bank = G.begin("v", "places")
                pe.matmul(bank[:, 0:N_EXP], tri[:, :], chosen[:, 0, :], start=True, stop=True)
                pe.matmul(bank[:, N_EXP:2 * N_EXP], ones[:, :], chosen[:, 0, :], start=True, stop=False)
                pe.matmul(bank[:, N_EXP:2 * N_EXP], tri[:, :], chosen[:, 1, :], start=False, stop=True)
                pe.matmul(bank[:, 2 * N_EXP:3 * N_EXP], ones[:, :], chosen[:, 0, :], start=True, stop=False)
                G.end(pe.matmul(bank[:, 2 * N_EXP:3 * N_EXP], ones[:, :], chosen[:, 1, :], start=False, stop=True))

            def experts(n):
                g = passes[n]
                pe.wait_ge(weighted_ready, n + 1)
                for e in range(N_EXP):
                    bank = g.begin("v" if e < 4 else "a", ("put", e))
                    for b in range(TB):
                        mm = pe.transpose(bank[:, b * P:(b + 1) * P], weighted[:, b, e, :], ident[:, :])
                    g.end(mm)
                pe.wait_ge(g.took_sems["a"], g.took["put", N_EXP - 1])
                pe.wait_ge(g.took_sems["v"], g.took["put", 3])
                pe.wait_ge(act_took, G.took["xT", TB - 1, 1])
                pe.wait_ge(pick_ready, n + 1)
                def gather(e, key, groups=range(5)):
                    for i in groups:
                        tiles = ((0, 1), (2, 3), (4, 5), (6,), (7,))[i]
                        bank = g.begin("v", (key, i))
                        for j, k in enumerate(tiles):
                            for b in range(TB):
                                mm = pe.matmul(bank[:, j * P:(j + 1) * P], xT[:, b, k * P:(k + 1) * P],
                                               pick[:, b, bass.ds(e, 1), :].rearrange("p o s -> p (o s)"),
                                               start=(b == 0), stop=(b == TB - 1))
                        g.end(mm, (key, i))

                pe.sem_inc(g.marked, EXP_MARKS)
                gather(0, "first")
                pe.wait_ge(g.took_sems["v"], g.took["first", 4])
                with pe.Fori(0, N_EXP) as e:
                    g.loop(e)

                    def taken(who, key):
                        pe.wait_ge(g.took_sems[who], g.took[key] + e * (EXP_V if who == "v" else EXP_A))

                    def split(j, rows_):
                        pe.wait_ge(g.split, e * EXP_TILES + j + 1)
                        return (a.rearrange("p (k n) -> p k n", k=rows_) for a in (high_tile(j), low_tile(j)))

                    def mark(mm):
                        mm.then_inc(g.marked, 1)
                        g.marks += 1
                        g.used.append((g.marked, g.marks, EXP_MARKS))

                    def hidden_transposes(c, bank):
                        taken("v", ("up", c))
                        for i in range(4):
                            mm = pe.transpose(bank[:, i * P:(i + 1) * P], he[:, c % 2, i * P:(i + 1) * P], ident[:, :])
                        g.end(mm, ("hidden", c))

                    for c in range(CHUNKS):
                        for n_, (who, name) in enumerate((("a", "gate"), ("v", "up"))):
                            bank = g.begin(who, (name, c))
                            for half in range(2):
                                high, low = split(4 * c + 2 * n_ + half, KT // 2)
                                for i in range(KT // 2):
                                    k = half * (KT // 2) + i
                                    mm = parts(bank, xe_high[:, k, :], xe_low[:, k, :], high[:, i, :], low[:, i, :], k == 0, k == KT - 1)
                                if half == 0:
                                    mark(mm)
                            g.end(mm)
                            g.used.append((g.group_done, g.total, EXP_GROUPS))
                        if c >= 1:
                            hidden_transposes(c - 1, g.begin("a", ("hidden", c - 1)))
                    last_hidden = g.begin("a", ("hidden", CHUNKS - 1))
                    halves = [g.begin("a", ("down", h)) for h in range(2)]
                    for d in range(DOWN):
                        if d % 2 == 0:
                            pe.wait_ge(g.hidden_split, e * CHUNKS + d // 2 + 1)
                        high, low = split(GATE_UP + d, 2)
                        for i in range(2):
                            f = 2 * d + i
                            for h in range(2):
                                n_ = slice(h * 512, (h + 1) * 512)
                                mm = parts(halves[h], he_high[:, f, :], he_low[:, f, :], high[:, i, n_], low[:, i, n_], f == 0, f == ET - 1)
                                if f == ET - 1:
                                    g.end(mm, ("down", h))
                        if d < DOWN - 1:
                            mark(mm)
                        if d == 1:
                            hidden_transposes(CHUNKS - 1, last_hidden)
                        elif d == 4:
                            gather(e + 1, "gather", range(4))
                        elif d == 5:
                            gather(e + 1, "gather", (4,))
                    g.used.append((g.group_done, g.total, EXP_GROUPS))
                    taken("a", ("down", 1))
                    for k in range(KT):
                        if k % 2 == 0:
                            bank = g.begin("v", ("scatter", k // 2))
                        mm = pe.matmul(bank[:, (k % 2) * SEQ:(k % 2 + 1) * SEQ], ye[:, k * P:(k + 1) * P],
                                       put[:, bass.ds(e, 1), :].rearrange("p o s -> p (o s)"), start=True, stop=True)
                        if k % 2 == 1:
                            g.end(mm)
                    taken("v", ("gather", 4))
                g.close(N_EXP)

            for l in range(DEPTH):
                mixer(l)
                attention(l)
                if l == 0:
                    feed_forward()
            routing()
            passes[:] = [G, Groups(pe, banks, more_done, more_took, [])]
            for g, name in zip(passes, ("experts", "more")):
                Experts(g, sem, name)
            G.before_experts = G.freed[-1]
            experts(0)
            G.experts_done, G.given_moe = G.total, G.given["v"]
            pe.wait_ge(routing_ready, 1)
            with pe.If(pe.value_load(extra_flag[0:1, 0:1], min_val=0, max_val=1) > 0):
                for who in "va":
                    pe.wait_ge(took_sems[who], G.given[who])
                experts(1)
                for who in "va":
                    pe.wait_ge(more_took[who], passes[1].given[who])

            def mlstm():
                norm_sums("final_ms", 1)
                norm_sums("norm1_ms")
                x = normed()
                slot = G.tile()
                bank = G.begin("v", "gates")
                w = ring[:, slot, 0:KT * 16].rearrange("p (k n) -> p k n", k=KT)
                for b in range(TB):
                    for k in range(KT):
                        mm = pe.matmul(bank[:, 16 * b:16 * b + 16], x(k)[:, b * P:(b + 1) * P], w[:, k, :],
                                       start=(k == 0), stop=(k == KT - 1))
                G.end(mm)
                G.free()
                linear("xm", "a", 2, x, KT)
                pe.wait_ge(gates_ready, 1)
                transposes("v", "gate_rows", [(g * SEQ + b * P, gate_cols[:, b, g, :]) for g in range(2) for b in range(TB)])
                linear("o_pre", "a", 2, x, KT)
                pe.wait_ge(xm_act, 1)
                for name, dst in (("qM", qM), ("kM", kM)):
                    slot = G.tile()
                    w = ring[:, slot, 0:8 * HD].rearrange("p (k n) -> p k n", k=8)
                    for h in range(HEADS):
                        bank = G.begin("a", (name, h))
                        for e in range(2):
                            for j in range(2):
                                mm = pe.matmul(bank[:, e * SEQ:(e + 1) * SEQ], w[:, 2 * h + j, e * P:(e + 1) * P],
                                               xm_conv[:, 2 * h + j, :], start=(j == 0), stop=(j == 1))
                        G.end(mm)
                    G.free()
                slot = G.tile()
                w = ring[:, slot, 0:8 * HD].rearrange("p (k n) -> p k n", k=8)
                for b in range(TB):
                    for hp in range(2):
                        bank = G.begin("v", ("vL", b, hp))
                        for i in range(2):
                            h = 2 * hp + i
                            for j in range(2):
                                mm = pe.matmul(bank[:, i * HD:(i + 1) * HD], xm_pad[:, 2 * h + j, 2 + b * P:2 + (b + 1) * P],
                                               w[:, 2 * h + j, :], start=(j == 0), stop=(j == 1))
                        G.end(mm)
                G.free()
                pe.wait_ge(a_ready, 1)
                transposes("v", "a_cols", [(64 * b, g_a[:, b * P:(b + 1) * P]) for b in range(TB)])

                def scores(h):
                    pe.wait_ge(act_took, G.took["kM", HEADS - 1])
                    bank = G.begin("a", ("scoresT", h))
                    for sblk in range(2):
                        for j in range(2):
                            mm = pe.matmul(bank[:, sblk * SEQ:(sblk + 1) * SEQ], kM[:, 2 * h + j, sblk * P:(sblk + 1) * P],
                                           qM[:, 2 * h + j, :], start=(j == 0), stop=(j == 1))
                    G.end(mm)

                def maxima(i):
                    h, d = divmod(i, 2)
                    bank = G.begin("a", ("maxima", i))
                    s = head_sel[0:64, 4 * d + h, :]
                    pe.matmul(bank[:, 0:SEQ], s, g_max, start=True, stop=True)
                    G.end(pe.matmul(bank[:, SEQ:2 * SEQ], s, g_sum, start=True, stop=True))

                pe.wait_ge(sel_ready, 1)
                pe.wait_ge(dve_took, G.took["vL", TB - 1, 1])
                scores(0)
                maxima(0)
                for i in range(2 * HEADS):
                    h, d = divmod(i, 2)
                    if i + 1 < 2 * HEADS:
                        if d == 1:
                            scores(h + 1)
                        maxima(i + 1)
                    pe.wait_ge(intra_ready, i + 1)
                    reach = ((0, 0, 2), (1, 1, 2)) if d == 0 else ((1, 0, 2), (0, 0, 1))
                    bank = G.begin("v", ("den", i))
                    for n_, (sblk, lo, hi) in enumerate(reach):
                        mm = pe.matmul(bank[:, lo * P:hi * P], ones[:, :], intra[:, sblk, lo:hi, :], start=(n_ == 0), stop=(n_ == 1))
                    G.end(mm)
                    bank = G.begin("v", ("num", i))
                    for e in range(2):
                        for n_, (sblk, lo, hi) in enumerate(reach):
                            mm = pe.matmul(bank[:, e * SEQ + lo * P:e * SEQ + hi * P], vL[:, sblk, h * HD + e * P:h * HD + (e + 1) * P],
                                           intra[:, sblk, lo:hi, :], start=(n_ == 0), stop=(n_ == 1))
                    G.end(mm)
                linear("merge_m", "a", 2, x, KT)
                pe.wait_ge(sq_ready, seen.next("sq"))
                for g in range(2):
                    bank = G.begin("a", ("head_ms", g))
                    for i in range(2):
                        for j in range(2):
                            mm = pe.matmul(bank[:, i * SEQ:(i + 1) * SEQ], ones[:, :], squares[:, 4 * g + 2 * i + j, :],
                                           start=(j == 0), stop=(j == 1))
                    G.end(mm)

            def lru():
                x = lambda k: xF[:, k, :]
                linear("xl", "a", 2, x, KT)
                pe.wait_ge(ym_ready, 1)
                linear("branch_m", "v", 2, lambda k: hM[:, k, :], KT)
                wr, wi = G.tile(), G.tile()
                gates_at = len(G.freed)
                pe.wait_ge(xl_conv_ready, 1)
                for d in range(2):
                    for name, slot in (("r", wr), ("i", wi)):
                        w = ring[:, slot, 0:16 * P].rearrange("p (k n) -> p k n", k=16)
                        for g in range(4):
                            bank = G.begin("a", (name, d, g))
                            for i in range(2):
                                mm = pe.matmul(bank[:, i * SEQ:(i + 1) * SEQ], w[:, 8 * d + 2 * g + i, :], xl_conv[:, 2 * g + i, :],
                                               start=True, stop=True)
                            G.end(mm)
                    if d == 0:
                        linear("gate_l", "a", 2, x, KT)
                G.freed[gates_at - 2] = G.freed[gates_at - 1] = (group_done, G.total)

            def merge():
                x = lambda k: xF[:, k, :]
                linear("merge_l", "a", 2, x, KT)
                pe.wait_ge(yl_ready, 1)
                linear("branch_l", "v", 2, lambda k: h_l[:, k, :], KT)
                pe.wait_ge(merged_ready, 4)
                linear("w_out", "v", 2, lambda k: merged[:, k, :], KT)

            def peer():
                norm_sums("norm2_ms")
                slot = G.tile()
                keys = ring[:, slot, 0:16 * P].rearrange("p (k c) -> p k c", k=16)
                for g in range(4):
                    transposes("v", ("keysT", g), [(i * P, keys[:, 4 * g + i, :]) for i in range(4)])
                G.free()

                def scores(b, g):
                    pe.wait_ge(act_took, G.took[("pq", g), 1])
                    pe.wait_ge(dve_took, G.took["keysT", g])
                    bank = G.begin("a", ("key_scores", b, g))
                    for i in range(4):
                        mm = pe.matmul(bank[:, i * P:(i + 1) * P], qP[:, 4 * g + i, b * P:(b + 1) * P], keysT[:, 4 * g + i, :],
                                       start=True, stop=True)
                    G.end(mm)

                x = normed()
                for g in range(4):
                    linear(("pq", g), "a", 1, x, KT)
                    if g >= 1:
                        scores(0, g - 1)
                scores(0, 3)
                for g in range(4):
                    scores(1, g)
                for b in range(TB):
                    for half in range(2):
                        transposes("v", ("tokens", b, half), [(i * P, xF[:, 4 * half + i, b * P:(b + 1) * P]) for i in range(4)])
                for b in range(TB):
                    halves = [G.begin("a", ("out", b, half)) for half in range(2)]
                    for k in range(KT):
                        pe.matmul(halves[k // 4][:, (k % 4) * P:(k % 4 + 1) * P], hF[:, k, b * P:(b + 1) * P], ident[:, :],
                                  start=(k % 4 == 0), stop=False)
                    with pe.Fori(b * ROUNDS, (b + 1) * ROUNDS) as r:
                        for q in range(BATCHES):
                            pe.wait_ge(diag_ready, r * BATCHES + q + 1)
                            pe.wait_ge(gathered[q], r * GATHERED + GATHERED * ((b + 1) * ROUNDS + 1))
                            for j in range(BATCH - 1):
                                for half in range(2):
                                    mm = pe.matmul(halves[half], diag[:, q, j, :],
                                                   gathered_rows[:, q * BATCH + j, half * 512:(half + 1) * 512], start=False, stop=False)
                            mm.then_inc(mix_done, 1)
                    pe.wait_ge(zero_ready, 1)
                    for half in range(2):
                        G.end(pe.matmul(halves[half], ones[0:1, :], zero_row, start=False, stop=True), ("out", b, half))

            mlstm()
            lru()
            merge()
            peer()

        @block.sync
        def _(sp):
            n = resume = 0

            def load(*parts):
                nonlocal n
                slot = n % RING
                if n - resume >= RING:
                    sp.wait_ge(*G.freed[n - RING])
                for place, src in parts:
                    sp.dma_start(place(ring[:, slot, :]), src).then_inc(loads[slot], 16)
                n += 1

            def by_rows(w, kts=KT):
                return w.rearrange("(k p) n -> p k n", p=P)

            def block_of(kts, n, off=0):
                return lambda s: s[:, off:off + kts * n].rearrange("p (k n) -> p k n", k=kts)

            def matrix(w, cols_n=512):
                for c in range(0, w.shape[1], cols_n):
                    load((block_of(KT, cols_n), by_rows(w[:, c:c + cols_n])))

            for l in range(DEPTH):
                w = t["w_in"][l]
                b0 = 2 * A_W
                for first, width in ((A_W, A_W), (0, A_W), (b0 + BC_W, BC_W), (b0 + 2 * BC_W, BC_W), (b0, BC_W),
                                     (b0 + 4 * BC_W, BC_W), (b0 + 3 * BC_W, BC_W)):
                    load((block_of(KT, width), by_rows(w[:, first:first + width])))
                matrix(t["w_xkv"][l])
                w = t["w_mix_out"][l]
                for c in range(2):
                    s = slice(c * 512, (c + 1) * 512)

                    def at(a, b, lo=0, hi=P):
                        return lambda s_: s_[lo:hi, a * 512:b * 512].rearrange("p (k n) -> p k n", k=b - a)
                    load((at(0, 5), by_rows(w[0:640, s])), (at(5, 6, 0, 64), w[640:704, s].rearrange("(k p) n -> p k n", k=1)),
                         (at(5, 6, 64, P), w[960:1024, s].rearrange("(k p) n -> p k n", k=1)), (at(6, 8), by_rows(w[704:960, s])))
                matrix(t["w_xq"][l])
                matrix(t["w_xo"][l])
                if l == 0:
                    for j in range(FFN_TILES):
                        if j < EXP_RING:
                            sp.wait_ge(*G.newest[j // 2])
                        else:
                            sp.wait_ge(*G.ffn_used[j - EXP_RING])
                        if j < FFN_GATE_UP:
                            c = j // 2
                            src = by_rows(t[("ffn_w_gate", "ffn_w_up")[j % 2]][0][:, c * 256:(c + 1) * 256])
                        else:
                            i = j - FFN_GATE_UP
                            src = by_rows(t["ffn_w_down"][0][2 * i * P:2 * (i + 1) * P, :])
                        sp.dma_start(raw_tile(j).rearrange("p (k n) -> p k n", k=src.shape[1]), src).then_inc(ffn_loads[j % EXP_RING], 16)
                    sp.wait_ge(*G.ffn_used[-1])
                    resume = n

            def expert_tiles(g, e, first, last):
                gate, up, down = (t[n_][0].rearrange("e (k p) n -> p (e k) n", p=P) for n_ in ("moe_w_gate", "moe_w_up", "moe_w_down"))
                for j in range(first, last):
                    wait_used(sp, g, e, j)
                    if j < GATE_UP:
                        c, half = j // 4, j % 2
                        src = (gate, up)[j // 2 % 2][:, bass.ds(e * KT + half * (KT // 2), KT // 2), c * 512:(c + 1) * 512]
                    else:
                        src = down[:, bass.ds(e * ET + 2 * (j - GATE_UP), 2), :]
                    sp.dma_start(raw_tile(j).rearrange("p (k n) -> p k n", k=src.shape[1]), src).then_inc(g.raw_loads[j % EXP_RING], 16)

            def experts(g):
                expert_tiles(g, 0, 0, EXP_RING)
                with sp.Fori(0, N_EXP - 1) as e:
                    expert_tiles(g, e, EXP_RING, EXP_TILES)
                    expert_tiles(g, e + 1, 0, EXP_RING)
                expert_tiles(g, N_EXP - 1, EXP_RING, EXP_TILES)

            resume = n
            sp.wait_ge(*G.before_experts)
            experts(G)
            more = passes[1]
            sp.wait_ge(routing_ready, 1)
            with sp.If(sp.value_load(extra_flag[0:1, 0:1], min_val=0, max_val=1) > 0):
                sp.wait_ge(group_done, G.experts_done)
                experts(more)
                sp.wait_ge(more_done, more.total)
            sp.wait_ge(group_done, G.experts_done)
            n0 = 2 * D
            w = t["w_in_2"][0]
            load((block_of(KT, 16), by_rows(w[:, n0:n0 + 16])))
            matrix(w[:, 0:D])
            matrix(w[:, D:2 * D])
            for name in ("q", "k", "v"):
                load((block_of(8, HD), t["mlstm_w_" + name + "_2"][0].rearrange("h (j p) e -> p (h j) e", p=P)))
            matrix(w[:, n0 + 16 + 2 * D:n0 + 16 + 3 * D])
            matrix(w[:, n0 + 16:n0 + 16 + D])
            matrix(t["w_branch_mlstm_2"][0])
            for name in ("r", "i"):
                load((block_of(16, P), t["lru_w_" + name + "_2"][0].rearrange("s n c d -> c (s n) d")))
            matrix(w[:, n0 + 16 + D:n0 + 16 + 2 * D])
            matrix(w[:, n0 + 16 + 3 * D:n0 + 16 + 4 * D])
            matrix(t["w_branch_lru_2"][0])
            matrix(t["w_out_2"][0])
            load((block_of(16, P), t["peer_sub_keys_2"][0].rearrange("h s n c -> n (h s) c")))
            matrix(t["peer_w_q_2"][0])
            sp.wait_ge(x_ready, KT * (N_NORMS + 1))
            sp.dma_start(final_gain, t["final_norm_g_2"].partition_broadcast(P)).then_inc(gain_loaded, 16)
            for b in range(TB):
                sp.wait_ge(final_out, b + 1)
                sp.dma_start(out[0, b * P:(b + 1) * P, :], final_rows[:, b, :]).then_inc(out_done, 16)
            sp.wait_ge(out_done, 16 * TB)

        @block.gpsimd
        def _(pool):
            step = Steps(pool, pool_step)
            step.then(pool.memset(ident[:, :], 0.0))
            step.then(pool.memset(tri[:, :], 1.0))
            step.then(pool.memset(lower[:, :], 1.0))
            step.then(pool.memset(half_ones[:, :], 0.0))
            step.then(pool.memset(pair_sel[:, :, :], 1.0))
            pool.memset(ones[:, :], 1.0)
            pool.memset(eps[:, :], EPS)
            pool.iota(iota[:, :], [[1, P]], base=0, channel_multiplier=0, allow_small_or_imprecise_dtypes=True)
            step.settle()
            pool.affine_select(out=ident[:, :], in_=ident[:, :], compare_op=ALU.not_equal, fill=1.0, base=0,
                               pattern=[[-1, P]], channel_multiplier=1)
            step.now(pool.affine_select(out=tri[:, :], in_=tri[:, :], compare_op=ALU.is_ge, fill=0.0, base=0,
                                        pattern=[[1, P]], channel_multiplier=-1))
            step.now(pool.affine_select(out=lower[:, :], in_=lower[:, :], compare_op=ALU.is_ge, fill=0.0, base=0,
                                        pattern=[[-1, P]], channel_multiplier=1))
            step.now(pool.memset(half_ones[0:64, 0:64], 1.0))
            step.now(pool.memset(half_ones[64:P, 64:P], 1.0))
            for lo, hi, base in ((0, 2, 0), (2, 3, BC_W - P)):
                s = pair_sel[:, lo:hi, :]
                step.now(pool.affine_select(out=s, in_=s, compare_op=ALU.is_ge, fill=0.0, base=base,
                                            pattern=[[P, hi - lo], [1, P]], channel_multiplier=-64))
                step.now(pool.affine_select(out=s, in_=s, compare_op=ALU.is_ge, fill=0.0, base=63 - base,
                                            pattern=[[-P, hi - lo], [-1, P]], channel_multiplier=64))
            pool.memset(small[:, 0:1], 0.0).then_inc(consts_ready, 1)
            pool.wait_ge(x_ready, KT * N_NORMS)
            s = head_sel[0:64, :, :]
            step.now(pool.memset(s, 0.0))
            pool.affine_select(out=s, in_=s, compare_op=ALU.not_equal, fill=1.0, base=0,
                               pattern=[[-32, 2], [-1, 4], [0, P]], channel_multiplier=1).then_inc(sel_ready, 1)

            def rows_of(phase):
                b, of_v = divmod(phase, 2)
                table = t[("peer_u_2", "peer_v_2")[of_v]][0]

                def freed(v, r, q):
                    if v:
                        pool.wait_ge(mix_done, r * BATCHES + q + 1)
                        pool.sem_inc(pool_turn, 1)
                        pool.wait_ge(add_done, r * BATCHES + q + 1)
                    else:
                        pool.wait_ge(dot_done, r * BATCHES + q + 1)
                    pool.sem_inc(pool_turn, 1)

                def gather(r, q):
                    pool.tensor_copy(stage[:, q * BATCH:(q + 1) * BATCH], rows_at[:, bass.ds(r * GATHER + q * BATCH, BATCH)]
                                     ).then_inc(staged, 1)
                    before = b * ROUNDS + of_v * ROUNDS
                    pool.wait_ge(staged, r * BATCHES + before * BATCHES + q + 1)
                    pool.sem_inc(pool_turn, 1)
                    for j in range(q * BATCH, (q + 1) * BATCH):
                        pool.indirect_dma_start(out=gathered_rows[:, j, :], out_offset=None, in_=table,
                                                in_offset=bass.IndirectOffsetOnAxis(ap=stage[:, j:j + 1], axis=0)
                                                ).then_inc(gathered[q], 16)

                for q in range(BATCHES):
                    if phase:
                        freed(not of_v, (b + of_v) * ROUNDS - 1, q)
                    gather(b * ROUNDS, q)
                for half in range(HALVES):
                    if half and not of_v:
                        pool.wait_ge(index_ready, HALVES * b + half + 1)
                    n_ = ROUNDS // HALVES
                    with pool.Fori(b * ROUNDS + max(half * n_, 1), b * ROUNDS + (half + 1) * n_) as r:
                        for q in range(BATCHES):
                            freed(of_v, r - 1, q)
                            gather(r, q)

            pool.wait_ge(group_done, G.after[("pq", 3), 1])
            for b in range(TB):
                pool.wait_ge(index_ready, HALVES * b + 1)
                rows_of(2 * b)
                rows_of(2 * b + 1)

        @block.scalar
        def _(act):
            seen = Tally()
            step = Steps(act, act_step)

            def ready(key):
                act.wait_ge(group_done, G.after[key])

            def take(ins):
                ins.then_inc(act_took, 1)

            act.dma_start(x_in, t["x"].rearrange("o (b p) d -> p (o b) d", p=P)).then_inc(inputs_loaded, 16)
            act.dma_start(mem_in, t["mem"].rearrange("o (b p) d -> p (o b) d", p=P)).then_inc(inputs_loaded, 16)
            sent = 0

            def param(dst, src):
                nonlocal sent
                act.dma_start(dst, src).then_inc(params_loaded, 16)
                sent += 1

            def vec(r, set_, src):
                n = src.shape[0] // P
                param(rows[r:r + n, set_, :], src.rearrange("(k c) -> k c", c=P))

            for l in range(DEPTH):
                r = 49 * l
                vec(r + MIX_G, 0, t["norm_mix_g"][l])
                vec(r + X_G, 0, t["norm_x_g"][l])
                vec(r + MEM_G, 0, t["norm_mem_g"][l])
                vec(r + FFN_G, 0, t["norm_ffn_g"][l])
                g = t["mix_out_g"][l]
                vec(r + OUT_G, 0, g[0:640])
                param(rows[r + OUT_G + 5:r + OUT_G + 6, 0, 0:64], g[640:704].rearrange("(k c) -> k c", k=1))
                param(rows[r + OUT_G + 5:r + OUT_G + 6, 0, 64:P], g[960:1024].rearrange("(k c) -> k c", k=1))
                vec(r + OUT_G + 6, 0, g[704:960])
                vec(r + CONVA_B, 0, t["conv_a_b"][l])
                vec(r + LNA_G, 0, t["ln_a_g"][l])
                vec(r + LNA_B, 0, t["ln_a_b"][l])
                param(rows[0:93, 1 + l, :], t["conv_a_w"][l].rearrange("j (k c) -> (j k) c", c=P))
                param(bc_rows[5 * l:5 * l + 3, :], t["conv_b_w"][l])
                param(bc_rows[5 * l + 3:5 * l + 4, :], t["ln_c_g"][l].rearrange("(k c) -> k c", k=1))
                param(bc_rows[5 * l + 4:5 * l + 5, :], t["ln_c_b"][l].rearrange("(k c) -> k c", k=1))
                param(gate_bias[:, l, :], t["gmlp_b"][l])
                param(spatial_in[:, l, :, :], t["gmlp_ws"][l].rearrange("g i j -> i g j"))
            for r, name in ((N1_G, "norm1_g_2"), (MC_B, "mlstm_conv_b_2"), (MN_G, "mlstm_norm_g_2"), (LC_B, "lru_conv_b_2"),
                            (N2_G, "norm2_g_2")):
                vec(r, 3, t[name][0])
            for r, name in ((BR, "lru_b_r_2"), (BI, "lru_b_i_2"), (LAM, "lru_lambda_2")):
                param(rows[r:r + 16, 3, :], t[name][0].rearrange("s (k c) -> (s k) c", c=P))
            param(rows[MC_W:MC_W + 32, 3, :], t["mlstm_conv_w_2"][0].rearrange("j (k c) -> (j k) c", c=P))
            param(rows[LC_W:LC_W + 32, 4, :], t["lru_conv_w_2"][0].rearrange("j (k c) -> (j k) c", c=P))
            vec(FIN_G, 4, t["norm_final_g"])
            param(router[:, :, :], t["moe_router"][0].rearrange("(k p) e -> p k e", p=P))
            param(gate_row, t["b_gates_2"][0].partition_broadcast(P))
            assert sent == N_PARAMS, sent

            def square(src, n=KT):
                act.activation(squares[:, 0:n, :], src, ACT.Square).then_inc(sq_ready, 1)

            def std(key, n, rows_=P):
                ready(key)
                take(act.activation(std_row[:, :], banks_of(key)[:, 0:SEQ], ACT.Sqrt, bias=EPS_AP, scale=1.0 / n))

            def banks_of(key):
                return banks["a"][(G.took[key] - 1) % 4]

            def square_parts():
                return [(squares[:, 2 * g:2 * g + 2, :], hF[:, 2 * g:2 * g + 2, :]) for g in range(4)]

            def norm(key, h_taken, whole=False):
                if whole:
                    act.wait_ge(dve_took, h_taken)
                    square(hF[:, :, :])
                else:
                    for g, (dst, src) in enumerate(square_parts()):
                        act.wait_ge(dve_took, h_taken - 3 + g)
                        act.activation(dst, src, ACT.Square).then_inc(sq_ready, 1)
                std(key, D)

            for g in range(4):
                ready(("mem", g))
                take(act.activation(mem_hat[:, 2 * g:2 * g + 2, :], pair(banks_of(("mem", g))), ACT.Copy))
            for l in range(DEPTH):
                ready(("spatial", l, 0))
                take(act.activation(spatialT[:, l, 0:4, :], pair(banks_of(("spatial", l, 0)), 4, P), ACT.Copy))
            ready("spatial_last")
            take(act.activation(spatialT[:, :, 4, :], pair(banks_of("spatial_last"), DEPTH, P), ACT.Copy))
            act.wait_ge(act_took, G.took["mem", 3])
            square(mem_hat)
            std("mem_ms", D)
            act.wait_ge(mem_normed, 1)

            def mixer(l):
                norm(("mix_ms", l), G.took["cols"] if l == 0 else G.took["ffn_down", 3], l == 0)

                def section(name, dst, func, ms, lo=0):
                    for g in range(2):
                        ready((name, l, g))
                        bank = banks_of((name, l, g))
                        if g == 0:
                            take(act.activation(dst[:, 0:2, :], pair(bank), func))
                        else:
                            take(act.activation(dst[lo:ms, 2, :], bank[lo:ms, 0:SEQ], func))

                section("a_gate", sig_a, ACT.Sigmoid, P)
                section("c_gate", c_gate, ACT.Copy, 64)
                section("b_gate", b_gate, ACT.Copy, 64)
                section("c_v", c_v, ACT.Gelu_apprx_tanh, 64)
                section("c_u", c_u, ACT.Gelu_apprx_tanh, P, 64)

                def key_value(*parts):
                    for i in parts:
                        ready(("kv", l, i))
                        bank = banks_of(("kv", l, i))
                        half, b = divmod(i - 4, 2)
                        if i < 4:
                            take(act.activation(kF[:, 2 * i:2 * i + 2, :], pair(bank), ACT.Copy))
                        else:
                            take(act.activation(vM[:, b, half * 512:(half + 1) * 512], bank[:, :], ACT.Copy))

                def layer_norm(name, n, src, last64, kv):
                    ready((name + "_mean", l))
                    take(act.activation(mean_row[:, :], banks_of((name + "_mean", l))[:, 0:SEQ], ACT.Copy, scale=-1.0 / n))
                    act.wait_ge(centred, seen.next("centred"))
                    if last64:
                        step.then(act.activation(squares[:, 0:2, :], src[:, 0:2, :], ACT.Square))
                        act.activation(squares[0:64, 2, :], src[0:64, 2, :], ACT.Square).then_inc(sq_ready, 1)
                    else:
                        square(src, 3)
                    key_value(kv)
                    std((name + "_var", l), n)

                layer_norm("c", BC_W, c_v, True, 0)
                key_value(1)
                layer_norm("a", A_W, conv_a, False, 2)
                act.wait_ge(ln_ready, l + 1)
                for k in range(3):
                    ins = act.activation(yF[:, k, :], conv_a[:, k, :], ACT.Silu, scale=c_vec(l, LNA_G, k), bias=c_vec(l, LNA_B, k))
                ins.then_inc(ya_ready, 1)
                act.wait_ge(ya_ready, l + 1)
                act.wait_ge(y_all, l + 1)
                square(yF)
                key_value(3, 4)
                for g in range(4):
                    ready(("group_ms", l, g))
                    take(act.activation(std8[:, 2 * g:2 * g + 2, :], pair(banks_of(("group_ms", l, g))), ACT.Sqrt,
                                        bias=EPS_AP, scale=1.0 / 64))
                key_value(5, 6, 7)

            def copies(key, dst, n=4, func=ACT.Copy, scale=1.0):
                for g in range(n):
                    ready((key, g))
                    take(act.activation(dst[:, 2 * g:2 * g + 2, :], pair(banks_of((key, g))), func, scale=scale))

            def attention(l):
                norm(("x_ms", l), G.took[("mix_out", l), 3])
                copies(("q", l), qF)
                for h in range(HEADS):
                    act.wait_ge(max_ready, HEADS * l + h + 1)
                    bank = banks_of(("scores", l, h))
                    for b in range(TB):
                        c = h * TB + b
                        ins = act.activation(probs[:, h, b, :], bank[:, b * SEQ:(b + 1) * SEQ], ACT.Exp, bias=small[:, c:c + 1],
                                             scale=HD ** -0.5, accum_out=small[:, 8 + c:9 + c])
                    take(ins)
                for h in range(HEADS):
                    ready(("o", l, h))
                    take(act.activation(oF[:, 2 * h:2 * h + 2, :], pair(banks_of(("o", l, h))), ACT.Copy))

            def feed_forward():
                def round_tile(j):
                    if j < FFN_HIGH:
                        act.wait_ge(*G.newest[3])
                        act.wait_ge(*G.newest[4])
                    else:
                        act.wait_ge(*G.ffn_used[j - FFN_HIGH])
                    act.wait_ge(ffn_loads[j % EXP_RING], 16 * (j // EXP_RING + 1))
                    act.activation(high_tiles[:, j % FFN_HIGH, :], raw_tile(j), ACT.Copy).then_inc(ffn_high, 1)

                for j in range(AHEAD):
                    round_tile(j)
                norm("ffn_ms", G.took[("xo", 0), 3])
                for j in range(FFN_TILES):
                    if j + AHEAD < FFN_TILES:
                        round_tile(j + AHEAD)
                    if j < FFN_GATE_UP and j % 2 == 0:
                        c = j // 2
                        ready(("ffn", 0, c))
                        if c >= 2:
                            act.wait_ge(dve_took, G.took["ffn", 1, c - 2])
                        take(act.activation(sil[:, c % 2, :, :], pair(banks_of(("ffn", 0, c))), ACT.Silu))

            def routing():
                norm("moe_ms", G.took[("xo", 1), 3])
                for b in range(TB):
                    for half in range(2):
                        ready(("xT", b, half))
                        take(act.activation(xT[:, b, half * 512:(half + 1) * 512], banks_of(("xT", b, half))[:, :], ACT.Copy))
                act.wait_ge(gap_ready, 1)
                act.activation(ratio, gap, ACT.Exp).then_inc(ratio_ready, 1)

            def experts(n):
                g = passes[n]

                def bank_in(key):
                    return banks["a"][(g.took[key] - 1) % 4]

                def took_it(ins):
                    ins.then_inc(g.took_sems["a"], 1)

                for e in range(4, N_EXP):
                    act.wait_ge(g.group_done, g.after["put", e])
                    took_it(act.activation(put[:, e, :], bank_in(("put", e))[:, 0:SEQ], ACT.Copy))
                def round_tile(e, j):
                    wait_used(act, g, e, j)
                    act.wait_ge(g.raw_loads[j % EXP_RING], 16 * (j // EXP_RING + 1) + e * (16 * EXP_TILES // EXP_RING))
                    act.activation(high_tile(j), raw_tile(j), ACT.Copy).then_inc(g.high, 1)

                def expert(e, follow):
                    def done(key):
                        act.wait_ge(g.group_done, g.after[key] + e * EXP_GROUPS)

                    def gate(c):
                        done(("gate", c))
                        took_it(act.activation(he[:, c % 2, :], bank_in(("gate", c))[:, :], ACT.Silu))

                    def hidden(c):
                        done(("hidden", c))
                        s, bank = slice(4 * c, 4 * c + 4), pair(bank_in(("hidden", c)), 4, P)
                        act.activation(he_high[:, s, :], bank, ACT.Copy)
                        took_it(act.activation(he_all[:, s, :], bank, ACT.Copy))

                    for j in range(EXP_TILES):
                        if j + AHEAD < EXP_TILES:
                            round_tile(e, j + AHEAD)
                        elif follow:
                            round_tile(e + 1, j + AHEAD - EXP_TILES)
                        if j < GATE_UP and j % 4 == 1:
                            gate(j // 4)
                        elif j <= GATE_UP and j >= 8 and j % 4 == 0:
                            hidden(j // 4 - 2)
                        elif j == GATE_UP + 2:
                            hidden(CHUNKS - 1)
                    for h in range(2):
                        done(("down", h))
                        took_it(act.activation(ye[:, h * 512:(h + 1) * 512], bank_in(("down", h))[:, :], ACT.Copy))

                if n == 0:
                    act.wait_ge(*G.before_experts)
                else:
                    act.wait_ge(group_done, G.experts_done)
                for j in range(AHEAD):
                    round_tile(0, j)
                with act.Fori(0, N_EXP - 1) as e:
                    expert(e, True)
                expert(N_EXP - 1, False)

            for l in range(DEPTH):
                mixer(l)
                attention(l)
                if l == 0:
                    feed_forward()
            routing()
            experts(0)
            act.wait_ge(routing_ready, 1)
            with act.If(act.value_load(extra_flag[0:1, 0:1], min_val=0, max_val=1) > 0):
                experts(1)
                act.wait_ge(more_took["v"], passes[1].given["v"])

            def mlstm():
                norm("final_ms", G.given_moe, True)
                for g, (dst, src) in enumerate(square_parts()):
                    act.wait_ge(final_ready, 2 * g + 2)
                    act.activation(dst, src, ACT.Square).then_inc(sq_ready, 1)
                std("norm1_ms", D)
                act.wait_ge(abs_ready, 1)
                act.activation(lam_t, lam_t, ACT.Exp, scale=-1.0).then_inc(exp_done, 1)
                for g in range(4):
                    ready(("xm", g))
                    take(act.activation(xm_pad[:, 2 * g:2 * g + 2, 2:2 + SEQ], pair(banks_of(("xm", g))), ACT.Copy))
                act.wait_ge(abs_ready, 2)
                act.activation(g_t, g_t, ACT.Exp, scale=-1.0).then_inc(exp_done, 1)
                copies("o_pre", o_sig, func=ACT.Sigmoid)
                act.wait_ge(xm_conv_ready, 1)
                act.activation(xm_conv, xm_conv, ACT.Silu).then_inc(xm_act, 1)
                for name, dst, scale in (("qM", qM, 1.0), ("kM", kM, HD ** -0.5)):
                    copies(name, dst, scale=scale)

                def scores(h):
                    ready(("scoresT", h))
                    take(act.activation(scoresT[:, h % 2, :, :, :].rearrange("p s t j -> p (s t j)"),
                                        banks_of(("scoresT", h))[:, :], ACT.Copy))

                def maxima(i):
                    act.wait_ge(arg_ready, i + 1)
                    for sblk, lo, hi in (((0, 0, 2), (1, 1, 2)) if i % 2 == 0 else ((1, 0, 2), (0, 0, 1))):
                        a = decay[:, sblk, lo:hi, :]
                        act.activation(a, a, ACT.Exp, scale=-1.0)
                    take(act.activation(floor_[:, i % 2, :], banks_of(("maxima", i))[:, SEQ:2 * SEQ], ACT.Exp, scale=-1.0))

                scores(0)
                maxima(0)
                for i in range(2 * HEADS - 1):
                    if i % 2 == 1:
                        scores(i // 2 + 1)
                    maxima(i + 1)
                copies("merge_m", g_m, func=ACT.Sigmoid)
                act.wait_ge(h_sum_ready, 1)
                square(hM)
                for g in range(2):
                    ready(("head_ms", g))
                    take(act.activation(std4[:, 2 * g:2 * g + 2, :], pair(banks_of(("head_ms", g))), ACT.Sqrt, bias=EPS_AP, scale=1.0 / HD))

            def lru():
                for g in range(4):
                    ready(("xl", g))
                    take(act.activation(xl_pad[:, 2 * g:2 * g + 2, 2:2 + SEQ], pair(banks_of(("xl", g))), ACT.Copy))
                for d in range(2):
                    act.wait_ge(lru_free, d + 1)
                    for name, dst, bias in (("r", lru_a, BR), ("i", lru_u, BI)):
                        for g in range(4):
                            ready((name, d, g))
                            for i in range(2):
                                k = 2 * g + i
                                ins = act.activation(dst[:, k, :], banks_of((name, d, g))[:, i * SEQ:(i + 1) * SEQ], ACT.Sigmoid,
                                                     bias=col(C2 + bias + 8 * d + k))
                            take(ins)
                    act.wait_ge(lam_ready, 1)
                    act.wait_ge(act_took, G.took["r", d, 3])
                    for k in range(KT):
                        step.then(act.activation(lru_t[:, k, :], lru_a[:, k, :], ACT.Tanh, scale=lam_pos[:, 8 * d + k:8 * d + k + 1]))
                    step.settle()
                    for k in range(KT):
                        ins = act.activation(lru_a[:, k, :], lru_a[:, k, :], ACT.Exp, scale=lam_neg[:, 8 * d + k:8 * d + k + 1])
                    ins.then_inc(lru_a_ready, 1)
                    act.wait_ge(lru_v_ready, d + 1)
                    act.activation(lru_t[:, :, :], lru_t[:, :, :], ACT.Sqrt).then_inc(lru_s_ready, 1)
                    if d == 0:
                        act.wait_ge(dve_took, G.took["branch_m", 3])
                        copies("gate_l", gate_l, func=ACT.Gelu)

            def merge():
                act.wait_ge(gated_ready, 2)
                copies("merge_l", g_l, func=ACT.Sigmoid)

            def peer():
                norm("norm2_ms", G.took["w_out", 3])

                def scores(b, g):
                    ready(("key_scores", b, g))
                    take(act.activation(key_scores[:, 4 * g:4 * g + 4, :], pair(banks_of(("key_scores", b, g)), 4, P), ACT.Copy))

                def margins(b):
                    act.wait_ge(margin_ready, HALVES * (b + 1))
                    act.activation(gates[:, b, :, :], gates[:, b, :, :], ACT.Exp).then_inc(margin_exp, 1)

                def activations(b):
                    act.wait_ge(dots_kept, (b + 1) * ROUNDS)
                    s = acts[:, b * SLOTS:(b + 1) * SLOTS]
                    act.activation(s, s, ACT.Gelu).then_inc(act_ready, 1)

                def final(b):
                    act.wait_ge(v_summed, b + 1)
                    step.now(act.activation(final_sq, v_sum, ACT.Square, accum_out=final_ss[:, b:b + 1]))
                    act.activation(final_std[:, b:b + 1], final_ss[:, b:b + 1], ACT.Sqrt, bias=EPS_AP, scale=1.0 / D).then_inc(final_std_ready, 1)

                for g in range(4):
                    copies(("pq", g), qP[:, 4 * g:4 * g + 4, :], 2)
                    if g >= 1:
                        scores(0, g - 1)
                scores(0, 3)
                margins(0)
                act.wait_ge(index_ready, HALVES)
                for g in range(4):
                    scores(1, g)
                activations(0)
                margins(1)
                final(0)
                activations(1)
                final(1)

            mlstm()
            lru()
            merge()
            peer()

        @block.vector
        def _(dve):
            seen = Tally()
            step = Steps(dve, dve_step)

            def ready(key):
                dve.wait_ge(group_done, G.after[key])

            def bank_of(key):
                return banks["v"][(G.took[key] - 1) % 4]

            def take(ins):
                ins.then_inc(dve_took, 1)

            def scaled(dst, src, gain, sem_):
                step.now(dve.reciprocal(rstd_row[:, :], std_row[:, :]))
                for k in range(KT):
                    dve.scalar_tensor_tensor(dst[:, k, :], src[:, k, :], gain(k), rstd_row[:, :], ALU.mult, ALU.mult).then_inc(sem_, 1)

            def norm(key, gain):
                dve.wait_ge(act_took, G.took[key])
                scaled(xF, hF, gain, x_ready)

            def add_to_residual(key, groups=range(4)):
                for g in groups:
                    ready((key, g))
                    s = hF[:, 2 * g:2 * g + 2, :]
                    take(dve.tensor_tensor(s, pair(bank_of((key, g))), s, ALU.add))

            def conv(dst, src, taps, weight, bias, tiles):
                for j in range(taps):
                    for k, m in tiles:
                        a = src(k, j)
                        if j == 0 and bias is not None:
                            ins = dve.tensor_scalar(dst[0:m, k, :], a, weight(k, j), bias(k), ALU.mult, ALU.add)
                        elif j == 0:
                            ins = dve.tensor_scalar(dst[0:m, k, :], a, weight(k, j), None, ALU.mult)
                        else:
                            step.settle(len(tiles) - 1)
                            ins = dve.scalar_tensor_tensor(dst[0:m, k, :], a, weight(k, j), dst[0:m, k, :], ALU.mult, ALU.add)
                        step.then(ins)
                step.settle()

            for g in range(4):
                ready(("x", g))
                take(dve.tensor_copy(hF[:, 2 * g:2 * g + 2, :], pair(bank_of(("x", g)))))
            ready("cols")
            step.then(dve.tensor_copy(cols[:, 0:C4 + 20], bank_of("cols")[:, 0:C4 + 20]))
            take(dve.tensor_copy(cols[0:64, C4 + 20:C4 + 30], bank_of("cols")[0:64, C4 + 20:C4 + 30]))
            dve.wait_ge(dve_took, G.took["cols"])
            dve.wait_ge(act_took, G.took["spatial_last"])
            dve.memset(spatialT[64:P, :, :, 0:64], 0.0).then_inc(mask_ready, 1)
            dve.wait_ge(act_took, G.took["mem_ms"])
            step.now(dve.reciprocal(rstd_row[:, :], std_row[:, :]))
            dve.tensor_tensor(mem_hat, mem_hat, rstd_row[:, :].unsqueeze(1).to_broadcast([P, KT, SEQ]), ALU.mult).then_inc(mem_normed, 1)

            def mixer(l):
                norm(("mix_ms", l), lambda k: c_vec(l, MIX_G, k))
                dve.wait_ge(mem_normed, 1)
                for k in range(KT):
                    ins = dve.tensor_scalar(mem_g[:, k, :], mem_hat[:, k, :], c_vec(l, MEM_G, k), None, ALU.mult)
                    if k < KT - 1:
                        step.then(ins)
                ins.then_inc(mem_ready, 1)
                step.then(dve.memset(ya_pad[:, :, 0:A_TAPS - 1], 0.0))
                step.then(dve.memset(yb_pad[:, :, 0:B_TAPS - 1], 0.0))
                dve.wait_ge(act_took, G.took["a_gate", l, 1])
                ready(("a_val", l, 0))
                take(dve.tensor_tensor(ya_pad[:, 0:2, A_TAPS - 1:], pair(bank_of(("a_val", l, 0))), sig_a[:, 0:2, :], ALU.mult))
                ready(("a_val", l, 1))
                take(dve.tensor_tensor(ya_pad[:, 2, A_TAPS - 1:], bank_of(("a_val", l, 1))[:, 0:SEQ], sig_a[:, 2, :], ALU.mult))
                dve.wait_ge(dve_took, G.took["a_val", l, 1])
                step.settle()
                conv(conv_a, lambda k, j: ya_pad[:, k, j:j + SEQ], A_TAPS, lambda k, j: col(C1 + 93 * l + 3 * j + k),
                     lambda k: c_vec(l, CONVA_B, k), ((0, P), (1, P), (2, P)))
                dve.engine_nop().then_inc(conv_ready, 1)
                dve.wait_ge(act_took, G.took["c_gate", l, 1])
                ready(("b_in", l, 0))
                take(dve.tensor_tensor(yb_pad[:, 0:2, B_TAPS - 1:], pair(bank_of(("b_in", l, 0))), c_gate[:, 0:2, :], ALU.mult))
                ready(("b_in", l, 1))
                take(dve.tensor_tensor(yb_pad[0:64, 2, B_TAPS - 1:], bank_of(("b_in", l, 1))[0:64, 0:SEQ], c_gate[0:64, 2, :], ALU.mult))
                dve.wait_ge(dve_took, G.took["b_in", l, 1])
                tiles = ((0, P), (1, P), (2, 64))
                conv(conv_b, lambda k, j: yb_pad[0:(P if k < 2 else 64), k, j:j + SEQ], B_TAPS, lambda k, j: bc_col(l, j, k), None, tiles)
                dve.wait_ge(act_took, G.took["b_gate", l, 1])
                step.then(dve.tensor_tensor(yF[:, 3:5, :], b_gate[:, 0:2, :], conv_b[:, 0:2, :], ALU.mult))
                step.then(dve.tensor_tensor(yF[0:64, 5, :], b_gate[0:64, 2, :], conv_b[0:64, 2, :], ALU.mult))

                def wide(ap, n):
                    return ap.unsqueeze(1).to_broadcast([P, n, SEQ])

                dve.wait_ge(act_took, G.took["c_mean", l])
                step.then(dve.tensor_tensor(c_v[:, 0:2, :], c_v[:, 0:2, :], wide(mean_row[:, :], 2), ALU.add))
                dve.tensor_tensor(c_v[0:64, 2, :], c_v[0:64, 2, :], mean_row[0:64, :], ALU.add).then_inc(centred, 1)
                dve.wait_ge(act_took, G.took["c_var", l])
                dve.wait_ge(centred, seen.next("centred"))
                step.now(dve.reciprocal(rstd_row[:, :], std_row[:, :]))
                for k, m in tiles:
                    step.then(dve.scalar_tensor_tensor(c_v[0:m, k, :], c_v[0:m, k, :], bc_col(l, 3, k), rstd_row[0:m, :], ALU.mult, ALU.mult))
                step.settle()
                for k, m in tiles:
                    ins = dve.tensor_scalar(c_v[0:m, k, :], c_v[0:m, k, :], bc_col(l, 4, k), None, ALU.add)
                    if k < 2:
                        step.then(ins)
                ins.then_inc(cv_ready, 1)
                for b in range(TB):
                    ready(("c_vT", l, b))
                    take(dve.tensor_copy(vT[:, b, :], bank_of(("c_vT", l, b))[:, 0:BC_W]))
                dve.wait_ge(act_took, G.took["c_u", l, 1])
                for p in range(3):
                    for b in range(TB):
                        ready(("mixed", l, p, b))
                        bank = bank_of(("mixed", l, p, b))
                        s = slice(b * P, (b + 1) * P)
                        if p < 2:
                            step.then(dve.tensor_tensor(yF[0:64, 6 + p, s], bank[0:64, 0:P], c_u[0:64, p, s], ALU.mult))
                            take(dve.tensor_tensor(yF[64:P, 6 + p, s], bank[64:P, P:2 * P], c_u[64:P, p, s], ALU.mult))
                        else:
                            take(dve.tensor_tensor(yF[64:P, 5, s], bank[64:P, 0:P], c_u[64:P, 2, s], ALU.mult))
                dve.engine_nop().then_inc(y_all, 1)
                dve.wait_ge(act_took, G.took["a_mean", l])
                dve.tensor_tensor(conv_a, conv_a, wide(mean_row[:, :], 3), ALU.add).then_inc(centred, 1)
                dve.wait_ge(act_took, G.took["a_var", l])
                dve.wait_ge(centred, seen.next("centred"))
                step.now(dve.reciprocal(rstd_row[:, :], std_row[:, :]))
                dve.tensor_tensor(conv_a, conv_a, wide(rstd_row[:, :], 3), ALU.mult).then_inc(ln_ready, 1)
                dve.wait_ge(act_took, G.took["group_ms", l, 3])
                dve.wait_ge(ya_ready, l + 1)
                dve.wait_ge(dve_took, G.took["mixed", l, 2, 1])
                step.now(dve.reciprocal(std8, std8))
                for k in range(KT):
                    ins = dve.scalar_tensor_tensor(yF[:, k, :], yF[:, k, :], c_vec(l, OUT_G, k), std8[:, k, :], ALU.mult, ALU.mult)
                    if k < KT - 1:
                        step.then(ins)
                ins.then_inc(y_ready, 1)
                add_to_residual(("mix_out", l))

            def attention(l):
                norm(("x_ms", l), lambda k: c_vec(l, X_G, k))
                for h in range(HEADS):
                    ready(("scores", l, h))
                    bank = banks["a"][(G.took["scores", l, h] - 1) % 4]
                    s = small[:, h * TB:(h + 1) * TB]
                    step.now(dve.tensor_reduce(s, pair(bank), AX.X, ALU.max))
                    dve.tensor_scalar(s, s, -(HD ** -0.5), None, ALU.mult).then_inc(max_ready, 1)
                for h in range(HEADS):
                    dve.wait_ge(act_took, G.took["scores", l, h])
                    r = small[:, 16 + h * TB:16 + (h + 1) * TB]
                    step.now(dve.reciprocal(r, small[:, 8 + h * TB:8 + (h + 1) * TB]))
                    for b in range(TB):
                        ins = dve.tensor_scalar(probs[:, h, b, :], probs[:, h, b, :], r[:, b:b + 1], None, ALU.mult)
                        if b < TB - 1:
                            step.then(ins)
                    ins.then_inc(probs_ready, 1)
                for h in range(HEADS):
                    ready(("probsT", l, h))
                    take(dve.tensor_copy(probsT[:, h, :, :], pair(bank_of(("probsT", l, h)))))
                if l == 0:
                    add_to_residual(("xo", l), range(3))
                    ffn_low_part(0)
                    add_to_residual(("xo", l), (3,))
                else:
                    add_to_residual(("xo", l))

            def ffn_low_part(j):
                dve.wait_ge(ffn_high, j + 1)
                dve.tensor_tensor(low_tile(j), raw_tile(j), high_tiles[:, j % FFN_HIGH, :].bitcast(F32), ALU.subtract).then_inc(ffn_split, 1)

            def feed_forward():
                norm("ffn_ms", lambda k: c_vec(0, FFN_G, k))
                for k in range(KT):
                    dve.wait_ge(x_ready, KT * 2 + k + 1)
                    step.now(dve.tensor_copy(x_high[:, k, :], xF[:, k, :]))
                    dve.tensor_tensor(x_low[:, k, :], xF[:, k, :], x_high[:, k, :].bitcast(F32), ALU.subtract).then_inc(ffn_x_split, 1)
                ffn_low_part(1)
                for j in range(FFN_TILES):
                    if j + AHEAD < FFN_TILES:
                        ffn_low_part(j + AHEAD)
                    if j < FFN_GATE_UP and j % 2 == 1:
                        c = j // 2
                        ready(("ffn", 1, c))
                        dve.wait_ge(act_took, G.took["ffn", 0, c])
                        h, s = hid[:, c % 2, :, :], slice(2 * c, 2 * c + 2)
                        take(dve.tensor_tensor(h, pair(bank_of(("ffn", 1, c))), sil[:, c % 2, :, :], ALU.mult))
                        dve.wait_ge(dve_took, G.took["ffn", 1, c])
                        step.now(dve.tensor_copy(hid_high[:, s, :], h))
                        dve.tensor_tensor(hid_low[:, s, :], h, hid_high[:, s, :].bitcast(F32), ALU.subtract).then_inc(ffn_hid_split, 1)
                add_to_residual("ffn_down")

            def routing():
                norm("moe_ms", lambda k: c_vec(1, FFN_G, k))
                ready("logits")
                b8 = bank_of("logits")[:, 0:TB * N_EXP].rearrange("p (b e) -> p b e", b=TB)
                take(dve.tensor_copy(logits, b8))
                dve.wait_ge(dve_took, G.took["logits"])
                for b in range(TB):
                    step.then(dve.max(top[:, b, :], logits[:, b, :]))
                step.settle()
                for b in range(TB):
                    step.then(dve.max_index(top_raw[:, b, :], top[:, b, :], logits[:, b, :]))
                step.settle()
                step.then(dve.tensor_copy(top_at, top_raw))
                dve.tensor_tensor(gap, top[:, :, 1], top[:, :, 0], ALU.subtract).then_inc(gap_ready, 1)
                step.settle()
                for b in range(TB):
                    for i, m in ((0, first), (1, second)):
                        step.then(dve.tensor_scalar(m[:, b, :], iota[:, 0:N_EXP], top_at[:, b, i:i + 1], None, ALU.is_equal))
                step.settle()
                dve.tensor_tensor(chosen, first, second, ALU.add).then_inc(chosen_ready, 1)
                dve.wait_ge(ratio_ready, 1)
                step.now(dve.tensor_scalar(total_w, ratio, 1.0, None, ALU.add))
                step.now(dve.reciprocal(w_first, total_w))
                step.now(dve.tensor_tensor(w_second, w_first, ratio, ALU.mult))
                for b in range(TB):
                    step.now(dve.tensor_scalar(share[:, b, :], first[:, b, :], w_first[:, b:b + 1], None, ALU.mult))
                    step.now(dve.scalar_tensor_tensor(share[:, b, :], second[:, b, :], w_second[:, b:b + 1], share[:, b, :], ALU.mult, ALU.add))
                ready("places")
                dve.wait_ge(chosen_ready, 1)
                bank = bank_of("places")
                p8 = bank[:, 0:TB * N_EXP].rearrange("p (b e) -> p b e", b=TB)
                step.now(dve.tensor_tensor(place, p8, chosen, ALU.mult))
                step.then(dve.tensor_scalar(place, place, -1.0, None, ALU.add))
                step.now(dve.tensor_reduce(most, bank[:, 2 * N_EXP:3 * N_EXP], AX.X, ALU.max))
                take(dve.tensor_scalar(extra_flag[:, 0:1], most, float(P), None, ALU.is_gt))
                dve.wait_ge(dve_took, G.took["places"])
                dve.engine_nop().then_inc(routing_ready, 1)

            def experts(n):
                g = passes[n]

                def bank_in(key):
                    return banks["v"][(g.took[key] - 1) % 4]

                def took_it(ins):
                    ins.then_inc(g.took_sems["v"], 1)

                if n:
                    dve.tensor_scalar(place, place, -float(P), None, ALU.add).then_inc(more_places, 1)
                    dve.wait_ge(more_places, 1)
                dve.memset(pick[:, :, N_EXP, :], 0.0)
                for scale, dst, sem_ in ((True, weighted, weighted_ready), (False, pick, pick_ready)):
                    for b in range(TB):
                        for e in range(N_EXP):
                            if scale:
                                ins = dve.tensor_scalar(dst[:, b, e, :], iota[:, :], place[:, b, e:e + 1], share[:, b, e:e + 1],
                                                        ALU.is_equal, ALU.mult)
                            else:
                                ins = dve.tensor_scalar(dst[:, b, e, :], iota[:, :], place[:, b, e:e + 1], None, ALU.is_equal)
                    ins.then_inc(sem_, 1)
                for e in range(4):
                    dve.wait_ge(g.group_done, g.after["put", e])
                    took_it(dve.tensor_copy(put[:, e, :], bank_in(("put", e))[:, 0:SEQ]))
                def low_part(e, j):
                    dve.wait_ge(g.high, e * EXP_TILES + j + 1)
                    dve.tensor_tensor(low_tile(j), raw_tile(j), high_tile(j).bitcast(F32), ALU.subtract).then_inc(g.split, 1)

                def gathered_tokens(n_, key, done):
                    for i, (k, m) in enumerate(((0, 2), (2, 2), (4, 2), (6, 1), (7, 1))):
                        done((key, i))
                        bank = pair(bank_in((key, i)), m, P)
                        dve.tensor_copy(xe_high[:, k:k + m, :], bank).then_inc(g.x_high, 1)
                        dve.wait_ge(g.x_high, n_ * 5 + i + 1)
                        took_it(dve.tensor_tensor(xe_low[:, k:k + m, :], bank, xe_high[:, k:k + m, :].bitcast(F32), ALU.subtract))

                def expert(e, follow):
                    def done(key):
                        dve.wait_ge(g.group_done, g.after[key] + e * EXP_GROUPS)

                    def up(c):
                        done(("up", c))
                        dve.wait_ge(g.took_sems["a"], g.took["gate", c] + e * EXP_A)
                        s = he[:, c % 2, :]
                        took_it(dve.tensor_tensor(s, bank_in(("up", c))[:, :], s, ALU.mult))

                    def hidden(c):
                        dve.wait_ge(g.took_sems["a"], g.took["hidden", c] + e * EXP_A)
                        s = slice(4 * c, 4 * c + 4)
                        dve.tensor_tensor(he_low[:, s, :], he_all[:, s, :], he_high[:, s, :].bitcast(F32), ALU.subtract).then_inc(g.hidden_split, 1)

                    for j in range(EXP_TILES):
                        if j + AHEAD < EXP_TILES:
                            low_part(e, j + AHEAD)
                        elif follow:
                            low_part(e + 1, j + AHEAD - EXP_TILES)
                        if j < GATE_UP and j % 4 == 3:
                            up(j // 4)
                        elif j <= GATE_UP + 1 and j >= 9 and j % 4 == 1:
                            hidden(j // 4 - 2)
                        elif j == GATE_UP + 3:
                            hidden(CHUNKS - 1)
                        elif j == GATE_UP + 5:
                            gathered_tokens(e + 1, "gather", done)
                    for k in range(4):
                        done(("scatter", k))
                        s = hF[:, 2 * k:2 * k + 2, :]
                        took_it(dve.tensor_tensor(s, pair(bank_in(("scatter", k))), s, ALU.add))

                for j in range(AHEAD):
                    low_part(0, j)
                gathered_tokens(0, "first", lambda key: dve.wait_ge(g.group_done, g.after[key]))
                with dve.Fori(0, N_EXP - 1) as e:
                    expert(e, True)
                expert(N_EXP - 1, False)

            for l in range(DEPTH):
                mixer(l)
                attention(l)
                if l == 0:
                    feed_forward()
            routing()
            experts(0)
            with dve.If(dve.value_load(extra_flag[0:1, 0:1], min_val=0, max_val=1) > 0):
                experts(1)

            def log1p(q, t_, z, w):
                step.now(dve.tensor_scalar(z, t_, 2.0, None, ALU.add))
                step.now(dve.reciprocal(z, z))
                step.now(dve.tensor_tensor(z, z, t_, ALU.mult))
                step.now(dve.tensor_tensor(w, z, z, ALU.mult))
                step.now(dve.tensor_scalar(q, w, 1.0 / 15, None, ALU.mult))
                for c in (13, 11, 9, 7, 5, 3):
                    step.now(dve.scalar_tensor_tensor(q, q, 1.0 / c, w, ALU.add, ALU.mult))
                step.now(dve.scalar_tensor_tensor(q, q, 1.0, z, ALU.add, ALU.mult))
                step.now(dve.tensor_scalar(q, q, 2.0, None, ALU.mult))

            def mlstm():
                dve.wait_ge(act_took, G.took["final_ms"])
                scaled(hF, hF, lambda k: col(C3 + FIN_G + k), final_ready)
                lam = cols[:, C2 + LAM:C2 + LAM + 16]
                dve.scalar_tensor_tensor(lam_t, lam, -1.0, lam, ALU.mult, ALU.max).then_inc(abs_ready, 1)
                dve.wait_ge(exp_done, 1)
                log1p(lam_q, lam_t, lam_z, lam_w)
                step.now(dve.tensor_scalar(lam_z, lam, -1.0, 0.0, ALU.mult, ALU.max))
                step.now(dve.tensor_tensor(lam_z, lam_z, lam_q, ALU.add))
                step.then(dve.tensor_scalar(lam_neg, lam_z, -LRU_C, None, ALU.mult))
                dve.tensor_scalar(lam_pos, lam_z, LRU_C, None, ALU.mult).then_inc(lam_ready, 1)
                norm("norm1_ms", lambda k: col(C2 + N1_G + k))
                dve.wait_ge(x_ready, KT * N_NORMS)
                step.then(dve.memset(xm_pad[:, :, 0:2], 0.0))
                step.then(dve.memset(xm_pad[:, :, 2 + SEQ:], 0.0))
                ready("gates")
                step.now(dve.memset(gate_cols, 0.0))
                src = bank_of("gates")[:, 0:32].rearrange("p (b d g h) -> p b d g h", b=TB, d=2, g=2)
                bias = gate_row.rearrange("p (d g h) -> p d g h", d=2, g=2)
                for b in range(TB):
                    for d in range(2):
                        ins = dve.tensor_tensor(gate_cols[:, b, :, 32 * d:32 * d + HEADS], src[:, b, d, :, :], bias[:, d, :, :], ALU.add)
                        if (b, d) != (1, 1):
                            step.then(ins)
                take(ins)
                dve.wait_ge(dve_took, G.took["gates"])
                step.settle()
                dve.engine_nop().then_inc(gates_ready, 1)
                ready("gate_rows")
                step.then(dve.tensor_copy(g_fo, bank_of("gate_rows")[0:64, SEQ:2 * SEQ]))
                take(dve.tensor_copy(g_in, bank_of("gate_rows")[0:64, 0:SEQ]))
                dve.wait_ge(dve_took, G.took["gate_rows"])
                dve.scalar_tensor_tensor(g_t, g_fo, -1.0, g_fo, ALU.mult, ALU.max).then_inc(abs_ready, 1)
                dve.wait_ge(exp_done, 2)
                log1p(g_q, g_t, g_z, g_w)
                step.then(dve.memset(g_one, 1.0))
                step.then(dve.memset(g_zero, 0.0))
                step.now(dve.scalar_tensor_tensor(g_fo, g_fo, 0.0, g_q, ALU.min, ALU.subtract))
                fwd, bwd = slice(0, 32), slice(32, 64)
                step.then(dve.tensor_tensor_scan(g_b[fwd, :], g_one[fwd, :], g_fo[fwd, :], 0.0, ALU.mult, ALU.add))
                step.then(dve.tensor_tensor_scan(g_b[bwd, ::-1], g_one[bwd, ::-1], g_fo[bwd, ::-1], 0.0, ALU.mult, ALU.add))
                step.settle()
                step.now(dve.tensor_tensor(g_a, g_in, g_b, ALU.subtract))
                step.then(dve.tensor_tensor_scan(g_max[fwd, :], g_a[fwd, :], g_zero[fwd, :], 0.0, ALU.max, ALU.max))
                step.then(dve.tensor_tensor_scan(g_max[bwd, ::-1], g_a[bwd, ::-1], g_zero[bwd, ::-1], 0.0, ALU.max, ALU.max))
                step.settle()
                dve.tensor_tensor(g_sum, g_b, g_max, ALU.add).then_inc(a_ready, 1)
                dve.wait_ge(act_took, G.took["xm", 3])
                conv(xm_conv, lambda k, j: xm_pad[:, k, j:j + SEQ], C_TAPS, lambda k, j: col(C2 + MC_W + 8 * j + k),
                     lambda k: col(C2 + MC_B + k), tuple((k, P) for k in range(KT)))
                dve.engine_nop().then_inc(xm_conv_ready, 1)
                for b in range(TB):
                    for hp in range(2):
                        ready(("vL", b, hp))
                        take(dve.tensor_copy(vL[:, b, 512 * hp:512 * (hp + 1)], bank_of(("vL", b, hp))[:, :]))
                ready("a_cols")
                take(dve.tensor_copy(a_cols, pair(bank_of("a_cols"), TB, 64)))
                dve.wait_ge(dve_took, G.took["a_cols"])

                def argument(i):
                    h, d = divmod(i, 2)
                    ready(("maxima", i))
                    bank = banks["a"][(G.took["maxima", i] - 1) % 4][:, 0:SEQ].rearrange("p (t j) -> p t j", t=2)
                    for n_, (sblk, lo, hi) in enumerate(((0, 0, 2), (1, 1, 2)) if d == 0 else ((1, 0, 2), (0, 0, 1))):
                        ins = dve.tensor_scalar(decay[:, sblk, lo:hi, :], bank[:, lo:hi, :], a_cols[:, sblk, 32 * d + h:32 * d + h + 1],
                                                0.0, ALU.subtract, ALU.max)
                        if n_ == 0:
                            step.then(ins)
                    ins.then_inc(arg_ready, 1)

                argument(0)
                for i in range(2 * HEADS):
                    h, d = divmod(i, 2)
                    dve.wait_ge(act_took, G.took["maxima", i])
                    s4 = scoresT[:, h % 2, :, :, :].rearrange("p s t j -> p (s t) j")
                    w4, p4 = (a.rearrange("p s t j -> p (s t) j") for a in (decay, intra))
                    diag = slice(0, 4, 3)
                    other = 1 if d == 0 else 2
                    m = (tri if d == 0 else lower)[:, :].unsqueeze(1).to_broadcast([P, 2, P])
                    step.then(dve.tensor_tensor(p4[:, other, :], s4[:, other, :], w4[:, other, :], ALU.mult))
                    step.now(dve.tensor_tensor(p4[:, diag, :], s4[:, diag, :], m, ALU.mult))
                    dve.tensor_tensor(p4[:, diag, :], p4[:, diag, :], w4[:, diag, :], ALU.mult).then_inc(intra_ready, 1)
                    if i + 1 < 2 * HEADS:
                        dve.wait_ge(intra_ready, i + 1)
                        argument(i + 1)
                    ready(("den", i))
                    den = bank_of(("den", i))[:, 0:SEQ]
                    step.now(dve.tensor_tensor(rstd_row[:, :], den, floor_[:, i % 2, :], ALU.max))
                    take(dve.scalar_tensor_tensor(rstd_row[:, :], den, -1.0, rstd_row[:, :], ALU.mult, ALU.max))
                    dve.wait_ge(dve_took, G.took["den", i])
                    step.now(dve.reciprocal(rstd_row[:, :], rstd_row[:, :]))
                    r2 = rstd_row[:, :].unsqueeze(1).to_broadcast([P, 2, SEQ])
                    ready(("num", i))
                    part = hM[:, 2 * h:2 * h + 2, :]
                    if d == 0:
                        take(dve.tensor_tensor(part, pair(bank_of(("num", i))), r2, ALU.mult))
                    else:
                        num = bank_of(("num", i))
                        step.now(dve.tensor_tensor(pair(num), pair(num), r2, ALU.mult))
                        dve.wait_ge(dve_took, G.took["num", i - 1])
                        take(dve.tensor_tensor(part, part, pair(num), ALU.add))
                dve.wait_ge(dve_took, G.took["num", 2 * HEADS - 1])
                dve.engine_nop().then_inc(h_sum_ready, 1)
                dve.wait_ge(act_took, G.took["head_ms", 1])
                step.now(dve.reciprocal(std4, std4))
                for k in range(KT):
                    step.then(dve.scalar_tensor_tensor(hM[:, k, :], hM[:, k, :], col(C2 + MN_G + k), std4[:, k // 2, :], ALU.mult, ALU.mult))
                step.settle()
                dve.tensor_tensor(hM, hM, o_sig, ALU.mult).then_inc(ym_ready, 1)

            def lru():
                dve.wait_ge(ym_ready, 1)
                step.then(dve.memset(xl_pad[:, :, 0:2], 0.0))
                step.then(dve.memset(xl_pad[:, :, 2 + SEQ:], 0.0))
                dve.wait_ge(act_took, G.took["xl", 3])
                step.settle()
                conv(xl_conv, lambda k, j: xl_pad[:, k, j:j + SEQ], C_TAPS, lambda k, j: col(C3 + LC_W + 8 * j + k),
                     lambda k: col(C2 + LC_B + k), tuple((k, P) for k in range(KT)))
                dve.engine_nop().then_inc(xl_conv_ready, 1)
                dve.engine_nop().then_inc(lru_free, 1)
                for g in range(4):
                    ready(("branch_m", g))
                    take(dve.tensor_tensor(merged[:, 2 * g:2 * g + 2, :], pair(bank_of(("branch_m", g))), g_m[:, 2 * g:2 * g + 2, :], ALU.mult))
                for d in range(2):
                    dve.wait_ge(act_took, G.took["i", d, 3])
                    dve.tensor_tensor(lru_u, lru_u, xl_conv, ALU.mult).then_inc(gated_ready, 1)
                    dve.wait_ge(lru_a_ready, d + 1)
                    for i in range(2):
                        s = slice(4 * i, 4 * i + 4)
                        step.now(dve.tensor_tensor(half_tmp, lru_a[:, s, :], lru_a[:, s, :], ALU.mult))
                        ins = dve.scalar_tensor_tensor(lru_t[:, s, :], half_tmp, 1.0, lru_t[:, s, :], ALU.add, ALU.mult)
                        if i == 0:
                            step.now(ins)
                    ins.then_inc(lru_v_ready, 1)
                    edge = 0 if d == 0 else SEQ - 1
                    step.then(dve.memset(lru_a[:, :, edge:edge + 1], 0.0))
                    dve.wait_ge(lru_s_ready, d + 1)
                    dve.wait_ge(gated_ready, d + 1)
                    step.now(dve.tensor_tensor(lru_u, lru_u, lru_t[:, :, :], ALU.mult))
                    a, u, h, h2 = (x_.rearrange("p k s -> p (k s)") for x_ in (lru_a, lru_u, h_l, lru_t[:, :, :]))
                    if d == 0:
                        dve.wait_ge(group_done, G.after["branch_m", 3])
                        step.now(dve.tensor_tensor_scan(h, a, u, 0.0, ALU.mult, ALU.add))
                        dve.engine_nop().then_inc(lru_free, 1)
                    else:
                        step.now(dve.tensor_tensor_scan(h2[:, ::-1], a[:, ::-1], u[:, ::-1], 0.0, ALU.mult, ALU.add))
                step.now(dve.tensor_tensor(h_l, h_l, lru_t[:, :, :], ALU.add))
                dve.wait_ge(act_took, G.took["gate_l", 3])
                dve.tensor_tensor(h_l, h_l, gate_l, ALU.mult).then_inc(yl_ready, 1)

            def merge():
                dve.wait_ge(yl_ready, 1)
                dve.wait_ge(act_took, G.took["merge_l", 3])
                dve.wait_ge(dve_took, G.took["branch_m", 3])
                for g in range(4):
                    ready(("branch_l", g))
                    if g:
                        dve.wait_ge(merged_ready, g)
                    s = slice(2 * g, 2 * g + 2)
                    take(dve.tensor_tensor(pair_tmp, pair(bank_of(("branch_l", g))), g_l[:, s, :], ALU.mult))
                    dve.wait_ge(dve_took, G.took["branch_l", g])
                    dve.tensor_tensor(merged[:, s, :], merged[:, s, :], pair_tmp, ALU.add).then_inc(merged_ready, 1)
                add_to_residual("w_out")

            def top16(top, at, values, rest, n):
                lo, hi = slice(0, 8), slice(8, 16)
                for i in range(n):
                    step.then(dve.max(top[:, i, lo], values[:, i, :]))
                step.settle()
                for i in range(n):
                    step.then(dve.max_index(at[:, i, lo], top[:, i, lo], values[:, i, :]))
                    step.then(dve.match_replace(rest[:, i, :], top[:, i, lo], values[:, i, :], NEG))
                step.settle()
                for i in range(n):
                    step.then(dve.max(top[:, i, hi], rest[:, i, :]))
                step.settle()
                for i in range(n):
                    step.then(dve.max_index(at[:, i, hi], top[:, i, hi], rest[:, i, :]))
                step.settle()

            def choose_keys(b, half):
                n = PHEADS // HALVES
                for g in (2 * half, 2 * half + 1):
                    dve.wait_ge(act_took, G.took["key_scores", b, g])
                    s = slice(4 * g, 4 * g + 4)
                    top16(key_top[:, s, :], key_at[:, s, :], key_scores[:, s, :], key_rest[:, s, :], 4)
                h, s = slice(n * half, n * half + n), slice(2 * n * half, 2 * n * (half + 1))
                step.then(dve.tensor_copy(key_at_f[:, h, :, :].rearrange("p h s k -> p (h s) k"), key_at[:, s, :]))
                t4 = key_top.rearrange("p (h s) k -> p h s k", s=2)[:, h, :, :]
                shape = [P, n, TOPK, TOPK]
                step.then(dve.tensor_tensor(pairs_[:, h, :].rearrange("p h (i j) -> p h i j", i=TOPK),
                                            t4[:, :, 0, :].unsqueeze(3).to_broadcast(shape),
                                            t4[:, :, 1, :].unsqueeze(2).to_broadcast(shape), ALU.add))
                step.settle()

            def choose_pairs(b, half):
                n = PHEADS // HALVES
                h, s = slice(n * half, n * half + n), slice(n * TOPK * half, n * TOPK * (half + 1))
                shape = [P, n, TOPK, TOPK]
                top16(best[:, h, :], best_at[:, h, :], pairs_[:, h, :], pairs_rest[:, h, :], n)
                at = best_at[:, h, :].rearrange("p h k -> p (h k)")
                step.then(dve.tensor_scalar(half_raw[0][:, s], at, 4, None, ALU.logical_shift_right))
                step.then(dve.tensor_scalar(half_raw[1][:, s], at, TOPK - 1, None, ALU.bitwise_and))
                step.settle()
                for i in range(2):
                    step.now(dve.tensor_copy(half_at[i][:, s], half_raw[i][:, s]))
                    wide = [P, n * TOPK, TOPK]
                    m = match[:, s, :]
                    step.now(dve.tensor_tensor(m, half_at[i][:, s].unsqueeze(2).to_broadcast(wide),
                                               iota[:, 0:TOPK].unsqueeze(1).to_broadcast(wide), ALU.is_equal))
                    m4 = m.rearrange("p (h k) j -> p h k j", h=n)
                    step.now(dve.tensor_tensor(m4, m4, key_at_f[:, h, i, :].unsqueeze(2).to_broadcast(shape), ALU.mult))
                    step.now(dve.tensor_reduce(half_key[i][:, s], m, AX.X, ALU.add))
                dve.scalar_tensor_tensor(rows_at[:, b * SLOTS + s.start:b * SLOTS + s.stop], half_key[0][:, s], float(PK), half_key[1][:, s],
                                         ALU.mult, ALU.add).then_inc(index_ready, 1)
                dve.tensor_tensor(gates[:, b, h, :], best[:, h, :], best[:, h, 0:1].to_broadcast([P, n, TOPK]), ALU.subtract).then_inc(margin_ready, 1)

            def normalise(b):
                dve.wait_ge(margin_exp, b + 1)
                g = gates[:, b, :, :]
                step.now(dve.tensor_reduce(gate_sum, g, AX.X, ALU.add))
                step.now(dve.reciprocal(gate_inv, gate_sum))
                step.now(dve.tensor_tensor(g, g, gate_inv.unsqueeze(2).to_broadcast([P, PHEADS, TOPK]), ALU.mult))

            def peer():
                norm("norm2_ms", lambda k: col(C2 + N2_G + k))
                for g in range(4):
                    ready(("keysT", g))
                    take(dve.tensor_copy(keysT[:, 4 * g:4 * g + 4, :], pair(bank_of(("keysT", g)), 4, P)))

                def u_rows(b):
                    ready(("tokens", b, 1))
                    n = (G.took["tokens", b, 0] - 1) % 4
                    assert n % 2 == 0
                    x = psum_all[:, n:n + 2, :].rearrange("p h d -> p (h d)")
                    with dve.Fori(b * ROUNDS, (b + 1) * ROUNDS) as r:
                        for q in range(BATCHES):
                            dve.wait_ge(gathered[q], r * GATHERED + GATHERED * (b * ROUNDS + 1))
                            for j in range(q * BATCH, (q + 1) * BATCH):
                                row = gathered_rows[:, j, :]
                                ins = dve.tensor_tensor_reduce(row, row, x, 1.0, 0.0, ALU.mult, ALU.add, dots[:, j:j + 1])
                            ins.then_inc(dot_done, 1)
                        dve.wait_ge(dot_done, r * BATCHES + BATCHES)
                        dve.tensor_copy(acts[:, bass.ds(r * GATHER, GATHER)], dots).then_inc(dots_kept, 1)
                        dve.wait_ge(dots_kept, r + 1)

                def weights(b):
                    normalise(b)
                    dve.wait_ge(act_ready, b + 1)
                    s = acts[:, b * SLOTS:(b + 1) * SLOTS]
                    dve.tensor_tensor(s, s, gates[:, b, :, :].rearrange("p h k -> p (h k)"), ALU.mult).then_inc(weight_ready, 1)
                    if b:
                        dve.wait_ge(final_out, b)
                    dve.memset(v_sum, 0.0).then_inc(v_zeroed, 1)
                    dve.wait_ge(weight_ready, b + 1)
                    dve.wait_ge(v_zeroed, b + 1)

                def v_rows(b, first, last):
                    def batches(r, free):
                        for q in range(BATCHES):
                            if free:
                                dve.wait_ge(mix_done, (r - 1) * BATCHES + q + 1)
                            shape = [P, BATCH - 1, P]
                            dve.tensor_tensor(diag[:, q, :, :], ident[:, :].unsqueeze(1).to_broadcast(shape),
                                              acts[:, bass.ds(r * GATHER + q * BATCH, BATCH - 1)].unsqueeze(2).to_broadcast(shape), ALU.mult
                                              ).then_inc(diag_ready, 1)
                            dve.wait_ge(gathered[q], r * GATHERED + GATHERED * ((b + 1) * ROUNDS + 1))
                            if free or q:
                                dve.wait_ge(add_done, r * BATCHES + q)
                            dve.scalar_tensor_tensor(v_sum, gathered_rows[:, (q + 1) * BATCH - 1, :],
                                                     acts[:, bass.ds(r * GATHER + (q + 1) * BATCH - 1, 1)], v_sum, ALU.mult, ALU.add
                                                     ).then_inc(add_done, 1)

                    if b == 0 and first == 0:
                        batches(0, False)
                        first = 1
                    if last - first == 1:
                        batches(b * ROUNDS + first, True)
                    elif last > first:
                        with dve.Fori(b * ROUNDS + first, b * ROUNDS + last) as r:
                            batches(r, True)

                def finish(b):
                    ready(("out", b, 1))
                    n = 4 + (G.took["out", b, 0] - 1) % 4
                    dve.wait_ge(add_done, (b + 1) * ROUNDS * BATCHES)
                    dve.tensor_tensor(v_sum, psum_all[:, n:n + 2, :].rearrange("p h d -> p (h d)"), v_sum, ALU.add).then_inc(v_summed, 1)
                    dve.wait_ge(final_std_ready, b + 1)
                    step.now(dve.reciprocal(final_rstd[:, b:b + 1], final_std[:, b:b + 1]))
                    dve.wait_ge(gain_loaded, 16)
                    dve.scalar_tensor_tensor(final_rows[:, b, :], v_sum, final_rstd[:, b:b + 1], final_gain, ALU.mult, ALU.mult
                                             ).then_inc(final_out, 1)

                for half in range(HALVES):
                    choose_keys(0, half)
                    choose_pairs(0, half)
                u_rows(0)
                dve.wait_ge(act_took, G.took["key_scores", 1, 3])
                dve.memset(zero_row, 0.0).then_inc(zero_ready, 1)
                weights(0)
                v_rows(0, 0, 1)
                choose_keys(1, 0)
                v_rows(0, 1, 2)
                choose_pairs(1, 0)
                v_rows(0, 2, 4)
                choose_keys(1, 1)
                v_rows(0, 4, 5)
                choose_pairs(1, 1)
                v_rows(0, 5, ROUNDS)
                finish(0)
                u_rows(1)
                weights(1)
                v_rows(1, 0, ROUNDS)
                finish(1)

            mlstm()
            lru()
            merge()
            peer()


_OUT = ((1, SEQ, D), "float32")


def kernel(**inputs):
    import numpy as _np
    import concourse.bacc as _bacc
    from concourse import mybir as _mybir
    from concourse.bass_utils import run_bass_kernel_spmd as _run

    nc = _bacc.Bacc("TRN2", target_bir_lowering=False, num_devices=1)
    arrays, t = {}, {}
    for name, a in inputs.items():
        a = _np.ascontiguousarray(a)
        arrays[f"in_{name}"] = a
        t[name] = nc.dram_tensor(f"in_{name}", a.shape, _mybir.dt.from_np(a.dtype), kind="ExternalInput").ap()
    out = nc.dram_tensor("out_0", _OUT[0], F32, kind="ExternalOutput").ap()
    two_blocks(nc, t, out)
    r = _run(nc, [arrays], core_ids=[0])
    return r.results[0]["out_0"]
```
